# Optimizing a Trainium2 kernel written in Bass

```python
import math
import jax, jax.numpy as jnp
from jax import lax
import numpy as np

D_MODEL = 1024
BATCH = 1
SEQ = 512
DEPTH = 2

N_MIXERS = 2
N_MLA_LAYERS = (DEPTH + 1) // 2
N_SWA_LAYERS = DEPTH // 2
N_DENSE_LAYERS = (DEPTH + 1) // 2
N_MOE_LAYERS = DEPTH // 2

MLA_HEADS = 8
MLA_Q_RANK = 256
MLA_KV_RANK = 256
MLA_NOPE_DIM = 128
MLA_ROPE_DIM = 64
MLA_V_DIM = 128
MLA_QK_DIM = MLA_NOPE_DIM + MLA_ROPE_DIM
MLA_DOWN_DIM = MLA_Q_RANK + MLA_KV_RANK + MLA_ROPE_DIM
ROPE_THETA = 10000.0

SWA_Q_HEADS = 16
SWA_KV_HEADS = 4
SWA_GROUP = SWA_Q_HEADS // SWA_KV_HEADS
SWA_HEAD_DIM = 64
SWA_WINDOW = 128
SWA_Q_DIM = SWA_Q_HEADS * SWA_HEAD_DIM
SWA_KV_DIM = SWA_KV_HEADS * SWA_HEAD_DIM
SWA_QKV_DIM = SWA_Q_DIM + 2 * SWA_KV_DIM

BLOCK = 128

FFN_DIM = 2816
N_EXPERTS = 8
TOP_K = 2
EXPERT_DIM = 2048

EPS = 1e-6
NEG_INF = -1e30

kernel_name = "hybrid_mla_swa_moe_encoder"

def rmsnorm(x, g):
    xf = x.astype(jnp.float32)
    y = xf * lax.rsqrt(jnp.mean(xf * xf, axis=-1, keepdims=True) + EPS)
    return (y * g.astype(jnp.float32)).astype(x.dtype)

def rope_tables(seq, dim):
    inv = 1.0 / (ROPE_THETA ** (jnp.arange(0, dim, 2, dtype=jnp.float32) / dim))
    ang = jnp.arange(seq, dtype=jnp.float32)[:, None] * inv[None, :]
    return jnp.cos(ang), jnp.sin(ang)

def apply_rope(x, cos, sin):
    xf = x.astype(jnp.float32)
    x1, x2 = jnp.split(xf, 2, axis=-1)
    return jnp.concatenate([x1 * cos - x2 * sin, x2 * cos + x1 * sin], axis=-1).astype(x.dtype)

def alibi_slopes(n):
    return 2.0 ** (-8.0 * jnp.arange(1, n + 1, dtype=jnp.float32) / n)

def mla(h, w_dqkv, q_norm, w_uq, kv_norm, w_uk, w_uv, w_o):
    B, S, _ = h.shape
    nb = S // BLOCK
    cos, sin = rope_tables(S, MLA_ROPE_DIM)
    down = h @ w_dqkv
    c_q = rmsnorm(down[..., :MLA_Q_RANK], q_norm)
    c_kv = rmsnorm(down[..., MLA_Q_RANK:MLA_Q_RANK + MLA_KV_RANK], kv_norm)
    k_rope = apply_rope(down[..., MLA_Q_RANK + MLA_KV_RANK:], cos, sin)
    q = jnp.einsum('bsr,rhd->bshd', c_q, w_uq)
    q_nope = q[..., :MLA_NOPE_DIM]
    q_rope = apply_rope(q[..., MLA_NOPE_DIM:], cos[:, None, :], sin[:, None, :])
    k_nope = jnp.einsum('bsr,rhd->bshd', c_kv, w_uk)
    v = jnp.einsum('bsr,rhd->bshd', c_kv, w_uv)
    scale = MLA_QK_DIM ** -0.5
    qn_b = jnp.moveaxis(q_nope.reshape(B, nb, BLOCK, MLA_HEADS, MLA_NOPE_DIM), 1, 0)
    qr_b = jnp.moveaxis(q_rope.reshape(B, nb, BLOCK, MLA_HEADS, MLA_ROPE_DIM), 1, 0)

    def attend(blk):
        qn, qr = blk
        s = (jnp.einsum('bqhd,bkhd->bhqk', qn, k_nope)
             + jnp.einsum('bqhd,bkd->bhqk', qr, k_rope))
        p = jax.nn.softmax(s.astype(jnp.float32) * scale, axis=-1).astype(v.dtype)
        return jnp.einsum('bhqk,bkhd->bqhd', p, v)

    o = lax.map(attend, (qn_b, qr_b))
    o = jnp.moveaxis(o, 0, 1).reshape(B, S, MLA_HEADS * MLA_V_DIM)
    return o @ w_o

def swa(h, w_qkv, sink, w_o):
    B, S, _ = h.shape
    nb = S // BLOCK
    span = BLOCK + 2 * SWA_WINDOW
    qkv = h @ w_qkv
    q = qkv[..., :SWA_Q_DIM].reshape(B, S, SWA_KV_HEADS, SWA_GROUP, SWA_HEAD_DIM)
    k = qkv[..., SWA_Q_DIM:SWA_Q_DIM + SWA_KV_DIM].reshape(B, S, SWA_KV_HEADS, SWA_HEAD_DIM)
    v = qkv[..., SWA_Q_DIM + SWA_KV_DIM:].reshape(B, S, SWA_KV_HEADS, SWA_HEAD_DIM)
    padw = ((0, 0), (SWA_WINDOW, SWA_WINDOW), (0, 0), (0, 0))
    kp = jnp.pad(k, padw)
    vp = jnp.pad(v, padw)
    slopes = alibi_slopes(SWA_Q_HEADS).reshape(SWA_KV_HEADS, SWA_GROUP)
    sink_l = sink.astype(jnp.float32).reshape(SWA_KV_HEADS, SWA_GROUP)
    scale = SWA_HEAD_DIM ** -0.5

    def block(i):
        start = i * BLOCK
        qb = lax.dynamic_slice_in_dim(q, start, BLOCK, axis=1)
        kb = lax.dynamic_slice_in_dim(kp, start, span, axis=1)
        vb = lax.dynamic_slice_in_dim(vp, start, span, axis=1)
        qpos = start + jnp.arange(BLOCK)
        kpos = start - SWA_WINDOW + jnp.arange(span)
        dist = jnp.abs(qpos[:, None] - kpos[None, :])
        valid = (dist <= SWA_WINDOW) & (kpos >= 0)[None, :] & (kpos < S)[None, :]
        s = jnp.einsum('bqgrd,bkgd->bgrqk', qb, kb).astype(jnp.float32) * scale
        s = s - slopes[:, :, None, None] * dist.astype(jnp.float32)
        s = jnp.where(valid, s, NEG_INF)
        snk = jnp.broadcast_to(sink_l[None, :, :, None, None], s.shape[:-1] + (1,))
        p = jax.nn.softmax(jnp.concatenate([s, snk], axis=-1), axis=-1)[..., :span]
        return jnp.einsum('bgrqk,bkgd->bqgrd', p.astype(vb.dtype), vb)

    o = lax.map(block, jnp.arange(nb))
    o = jnp.moveaxis(o, 0, 1).reshape(B, S, SWA_Q_DIM)
    return o @ w_o

def swiglu(h, w_gate, w_up, w_down):
    return (jax.nn.silu(h @ w_gate) * (h @ w_up)) @ w_down

def moe(h, router, w_gate, w_up, w_down):
    B, S, D = h.shape
    t = h.reshape(-1, D)
    logits = (t @ router).astype(jnp.float32)
    top_val, top_idx = lax.top_k(logits, TOP_K)
    gates = jax.nn.softmax(top_val, axis=-1)
    combine = jnp.sum(jax.nn.one_hot(top_idx, N_EXPERTS, dtype=jnp.float32) * gates[..., None], axis=1)
    combine = combine.astype(t.dtype)
    y = jnp.zeros_like(t)
    for e in range(N_EXPERTS):
        y = y + combine[:, e:e + 1] * swiglu(t, w_gate[e], w_up[e], w_down[e])
    return y.reshape(B, S, D)

def setup_inputs(seed: int = 0) -> dict:
    key = jax.random.key(seed)
    ks = iter(jax.random.split(key, 32))

    def nrm(shape, fan_in):
        return jax.random.normal(next(ks), shape, jnp.float32) * (fan_in ** -0.5)

    def gain(shape):
        return 1.0 + 0.02 * jax.random.normal(next(ks), shape, jnp.float32)

    NA, NS, ND, NM = N_MLA_LAYERS, N_SWA_LAYERS, N_DENSE_LAYERS, N_MOE_LAYERS
    D = D_MODEL
    return {
        "x": jax.random.normal(next(ks), (BATCH, SEQ, D), jnp.float32),
        "mla_norm": gain((NA, D)),
        "mla_w_dqkv": nrm((NA, D, MLA_DOWN_DIM), D),
        "mla_q_norm": gain((NA, MLA_Q_RANK)),
        "mla_w_uq": nrm((NA, MLA_Q_RANK, MLA_HEADS, MLA_QK_DIM), MLA_Q_RANK),
        "mla_kv_norm": gain((NA, MLA_KV_RANK)),
        "mla_w_uk": nrm((NA, MLA_KV_RANK, MLA_HEADS, MLA_NOPE_DIM), MLA_KV_RANK),
        "mla_w_uv": nrm((NA, MLA_KV_RANK, MLA_HEADS, MLA_V_DIM), MLA_KV_RANK),
        "mla_w_o": nrm((NA, MLA_HEADS * MLA_V_DIM, D), MLA_HEADS * MLA_V_DIM),
        "swa_norm": gain((NS, D)),
        "swa_w_qkv": nrm((NS, D, SWA_QKV_DIM), D),
        "swa_sink": 0.5 * jax.random.normal(next(ks), (NS, SWA_Q_HEADS), jnp.float32),
        "swa_w_o": nrm((NS, SWA_Q_DIM, D), SWA_Q_DIM),
        "ffn_norm": gain((ND, D)),
        "ffn_w_gate": nrm((ND, D, FFN_DIM), D),
        "ffn_w_up": nrm((ND, D, FFN_DIM), D),
        "ffn_w_down": nrm((ND, FFN_DIM, D), FFN_DIM),
        "moe_norm": gain((NM, D)),
        "moe_router": nrm((NM, D, N_EXPERTS), D),
        "moe_w_gate": nrm((NM, N_EXPERTS, D, EXPERT_DIM), D),
        "moe_w_up": nrm((NM, N_EXPERTS, D, EXPERT_DIM), D),
        "moe_w_down": nrm((NM, N_EXPERTS, EXPERT_DIM, D), EXPERT_DIM),
        "final_norm": gain((D,)),
    }

def reference(x, mla_norm, mla_w_dqkv, mla_q_norm, mla_w_uq, mla_kv_norm, mla_w_uk, mla_w_uv, mla_w_o,
              swa_norm, swa_w_qkv, swa_sink, swa_w_o,
              ffn_norm, ffn_w_gate, ffn_w_up, ffn_w_down,
              moe_norm, moe_router, moe_w_gate, moe_w_up, moe_w_down,
              final_norm):
    h = x
    for i in range(DEPTH):
        j = i // N_MIXERS
        if i % N_MIXERS == 0:
            h = h + mla(rmsnorm(h, mla_norm[j]), mla_w_dqkv[j], mla_q_norm[j], mla_w_uq[j],
                        mla_kv_norm[j], mla_w_uk[j], mla_w_uv[j], mla_w_o[j])
        else:
            h = h + swa(rmsnorm(h, swa_norm[j]), swa_w_qkv[j], swa_sink[j], swa_w_o[j])
        c = i // 2
        if i % 2 == 0:
            h = h + swiglu(rmsnorm(h, ffn_norm[c]), ffn_w_gate[c], ffn_w_up[c], ffn_w_down[c])
        else:
            h = h + moe(rmsnorm(h, moe_norm[c]), moe_router[c], moe_w_gate[c], moe_w_up[c], moe_w_down[c])
    return rmsnorm(h, final_norm)


_drawn_inputs = setup_inputs


def setup_inputs(seed=0):
    import zlib

    import numpy as np

    out = dict(_drawn_inputs(seed))
    spreads = {}
    factors = {'mla_norm': 4.83,
     'mla_q_norm': 5.288,
     'mla_kv_norm': 5.035,
     'final_norm': 8.0,
     'swa_norm': 8.0,
     'swa_sink': 8.0,
     'ffn_norm': 8.0,
     'moe_norm': 6.196}
    for name, (base, spread) in spreads.items():
        noise = np.random.default_rng([zlib.crc32(name.encode()), seed]).standard_normal(out[name].shape)
        drawn = base * np.exp(spread * noise) if base else spread * noise
        out[name] = __import__('jax').numpy.asarray(drawn.astype(out[name].dtype))
    for name, factor in factors.items():
        out[name] = (out[name] * factor).astype(out[name].dtype)
    return out
```

```python
from contextlib import ExitStack

import numpy as np

import concourse.bass as bass
from concourse import mybir

F32 = mybir.dt.float32
F32R = mybir.dt.float32r
I32 = mybir.dt.int32
ALU = mybir.AluOpType
ACT = mybir.ActivationFunctionType
AXX = mybir.AxisListType.X

P = 128
S = 512
D = 1024
NT = S // P
KD = D // P
EPS = 1e-6

QR = 256
KVR = 256
NOPE = 128
ROPE = 64
HEADS = 8
QK = NOPE + ROPE
DOWN = QR + KVR + ROPE
MLA_SCALE = QK ** -0.5

KVH = 4
GRP = 4
HD = 64
QH = KVH * GRP
SCALE8 = 8.0
SWA_SCALE = HD ** -0.5
WIN = 128
SPAN = 3 * P

FFN = 2816
NE = 8
ED = 2048
FB = 256
FEW = 32
FFN_STEPS = FFN // FB
MOE_STEPS = ED // FB
FFN_TOTAL = 2 * FFN_STEPS
CAP = S

BASE = 16640


def build_trunk(nc, a, out):
    lst_d = nc.dram_tensor("slot_list", [NE * CAP, 1], I32, kind="Internal").ap()
    hn_d = nc.dram_tensor("hn_rows", [S, D], F32, kind="Internal").ap()
    y_d = nc.dram_tensor("expert_rows", [2 * S, D], F32, kind="Internal").ap()

    def at(name, shape, offset, dt=F32):
        return nc.alloc_sbuf_tensor_at(name, shape, dt, offset=offset)

    class Region:

        def __init__(self, start, end):
            self.at, self.end = start, end

        def __call__(self, name, shape, dt=F32):
            size = int(np.prod(shape[1:])) * 4
            x = at(name, shape, self.at, dt)
            self.at += (size + 31) // 32 * 32
            assert self.at <= self.end, (name, self.at, self.end)
            return x

    fixed = Region(BASE, 229344)
    H = fixed("H", [P, NT, D])
    GB = [fixed("gain_a", [P, D]), fixed("gain_b", [P, D])]
    XG = [fixed("rows_a", [P, D]), fixed("rows_b", [P, D])]
    IDN = fixed("identity", [P, P])
    TRI = fixed("earlier", [P, P])
    ONES = fixed("ones", [P, P])
    small = lambda n, w, dt=F32: fixed(n, [P, w], dt)
    SS, SD, RS = small("mean_square", NT), small("std", NT), small("rstd", NT)
    EPSC = small("eps", 1)
    CNT = small("counts", NE + 1, I32)
    LST = small("slot_tokens", NE * NT, I32)
    LSM = small("slot_rows", NE * NT, I32)
    LSG = small("slot_gather", NE * NT, I32)
    G12 = small("gates", 2 * NT)
    AREA = fixed.at

    r = Region(AREA, 229344)
    m_xT = r("mla_xT", [P, KD, S])
    m_wd = r("w_dqkv", [P, KD, DOWN])
    m_wkr = r("w_krope", [P, KD, P])
    m_wo = at("mla_wo", [P, HEADS, D], AREA)
    m_pT = [at("probsT0", [P, NT, S], r.at)]
    m_cn = r("c_norm", [P, NT, QR + KVR])
    m_cT = r("c_T", [P, NT, S])
    m_uq = r("w_uq", [P, 2, HEADS, QK])
    m_uk = r("w_uk", [P, 2, HEADS, NOPE])
    m_pT.append(at("probsT1", [P, NT, S], r.at))
    m_uv = r("w_uv", [P, 2, HEADS * P])
    m_wqr = r("w_qrope", [P, 2, HEADS, P])
    m_v = r("mla_v", [P, NT, HEADS * P])
    m_qn = [r(f"q_nope{i}", [P, S]) for i in range(2)]
    m_kn = [r(f"k_nope{i}", [P, S]) for i in range(2)]
    m_qr = [r(f"q_rope{i}", [ROPE, S]) for i in range(2)]
    m_kr = r("k_rope", [ROPE, S])
    m_t1, m_t2 = r("rope_t1", [ROPE, S]), r("rope_t2", [ROPE, S])
    m_p = [r(f"probs{i}", [P, NT, S]) for i in range(2)]
    m_oT = r("mla_oT", [P, HEADS, S])
    m_tab = r("rope_table", [P, S])
    m_gq = r("gain_qkv", [P, QR + KVR])
    m_sq, m_sd, m_rq = r("c_sq", [P, 2 * NT]), r("c_sd", [P, 2 * NT]), r("c_rstd", [P, 2 * NT])
    m_junk = r("c_junk", [P, 2, QR])
    m_mx, m_nm = r("row_max", [P, HEADS * NT]), r("neg_max", [P, HEADS * NT])
    m_sm, m_rc = r("row_sum", [P, HEADS * NT]), r("row_rcp", [P, HEADS * NT])

    r = Region(AREA, 229344)
    f_xh = r("xT_hi", [P, KD, 2 * P], F32R)
    f_xl = r("xT_lo", [P, KD, 2 * P], F32R)
    f_sg = [r(f"silu{i}", [P, FB]) for i in range(2)]
    f_h = [r(f"hidden{i}", [P, FB]) for i in range(2)]
    f_hh = r("hT_hi", [P, 2, 2, P], F32R)
    f_hl = r("hT_lo", [P, 2, 2, P], F32R)
    f_ld = [r("lo_down1", [P, 2, D], F32R)]
    RAW = r.at
    f_rg = [[r(f"raw_gu{i}{j}", [P, 4, 2 * FB]) for j in range(2)] for i in range(2)]
    f_rd = [r(f"raw_down{i}", [P, 2, D]) for i in range(2)]
    f_hg = [r(f"hi_gu{i}", [P, KD, 2 * FB], F32R) for i in range(2)]
    f_lg = [r(f"lo_gu{i}", [P, KD, 2 * FB], F32R) for i in range(2)]
    f_hd = [r(f"hi_down{i}", [P, 2, D], F32R) for i in range(2)]
    f_ld.insert(0, r("lo_down0", [P, 2, D], F32R))
    f_xb = r("xT_few", [P, KD, FEW])
    f_cb = r("gu_few_half", [P, FB])
    f_gb = r("gu_few", [FEW, 2 * FB])
    f_sb, f_hb = f_sg[1][0:FEW, :], f_h[1][0:FEW, :]
    f_hbT = r("hT_few", [P, 2, FEW])

    r = Region(AREA, 229344)
    s_w = r("w_qkv", [P, KD, QH * HD + 2 * KVH * HD])
    s_o = at("swa_oT", [P, 2, GRP, S], r.at)
    s_xT = r("swa_xT", [P, KD, S])
    s_q = r("swa_qT", [P, 2, GRP, S])
    s_k = r("swa_kT", [P, 2, S])
    s_v = r("swa_v", [P, NT, KVH * HD])
    s_dist = r("distance", [P, SPAN])
    s_s = [r(f"swa_scores{i}", [P, GRP, SPAN]) for i in range(2)]
    s_p = [r(f"swa_probs{i}", [P, GRP, SPAN]) for i in range(2)]
    s_pT = [r(f"swa_probsT{i}", [P, 3, GRP, P]) for i in range(2)]
    s_wo = r("swa_wo", [P, 2, GRP, D])
    s_snk, s_sk8 = r("sink", [P, QH]), r("sink8", [P, QH])
    s_mx, s_nm = r("swa_max", [P, 16 * GRP]), r("swa_neg", [P, 16 * GRP])
    s_es, s_sm = r("swa_esink", [P, 16 * GRP]), r("swa_sum", [P, 16 * GRP])
    s_rc = r("swa_rcp", [P, 16 * GRP])

    r = Region(AREA, RAW)
    g_xT = r("moe_xT", [P, KD, S])
    g_rt = r("router", [P, KD, NE])
    g_c = r("route_consts", [P, 2, NT, NE])
    rt = lambda n, k=NE: r(n, [P, NT, k])
    g_lg, g_eq, g_w1, g_o1, g_l2, g_w2, g_o2 = (rt(n) for n in ("lg", "eq", "w1", "oh1", "l2", "w2", "oh2"))
    g_m, g_rk, g_j, g_j2, g_j3, g_pos0, g_pos = (
        rt(n) for n in ("chosen", "rank", "j1", "j2", "j3", "pos0", "pos"))
    g_m1, g_i1, g_m2, g_i2, g_d, g_e, g_s1 = (r(n, [P, NT]) for n in ("m1", "i1", "m2", "i2", "d21", "e2", "s1"))
    g_pr = [rt(f"pick{c}") for c in range(2)]
    g_sel = r("picked", [P, 2, NT])
    g_posi = r("pos_i", [P, 2, NT], I32)
    g_tok = r("tokens", [P, 2, NT], I32)
    g_zero = r("zero_list", [P, NE * NT], I32)
    g_cf = r("counts_f", [P, NE + 1])

    r = Region(AREA, 229344)
    y_rows = [r(f"y{i}", [P, 2, D]) for i in range(2)]
    y_out = [r(f"out{i}", [P, D]) for i in range(2)]

    ctx = ExitStack()
    with ctx:
        PS = ctx.enter_context(nc.psum_tensor("PS", [P, 8, 512], F32))
        sem = lambda n: ctx.enter_context(nc.semaphore(n))
        ld_h = [sem(f"ld_h{t}") for t in range(NT)]
        ld_id, ld_gain, ld_wd, ld_tab, ld_uq, ld_uk, ld_uv, ld_mwo = (
            sem(n) for n in ("ld_id", "ld_gain", "ld_wd", "ld_tab", "ld_uq", "ld_uk", "ld_uv", "ld_mwo"))
        ld_sw, ld_sc, ld_swo, ld_route = (sem(n) for n in ("ld_sw", "ld_sc", "ld_swo", "ld_route"))
        gain_b = sem("gain_b_loaded")
        chain = sem("dve_chain")
        ss_ready, std_ready, xn_ready, xT_tr, xT_ev = (
            sem(n) for n in ("ss_ready", "std_ready", "xn_ready", "xT_tr", "xT_ev"))
        eps_set, wkr_ready, wqr_ready = sem("eps_set"), sem("wkr_ready"), sem("wqr_ready")
        dq_done, sq_done, cstd, cn_ready, ct_tr, ct_ev, kr_done, kr_ready = (
            sem(n) for n in ("dq_done", "sq_done", "cstd", "cn_ready", "ct_tr", "ct_ev", "kr_done", "kr_ready"))
        v_done, v_ev, pj_done, pj_ev, qr_ready, sc_done, nm_ready, ex_done = (
            sem(n) for n in ("v_done", "v_ev", "pj_done", "pj_ev", "qr_ready", "sc_done", "nm_ready", "ex_done"))
        pn_ready, tr_done, pt_ev, pv_done, o_ev, wo_done, wo_add = (
            sem(n) for n in ("pn_ready", "tr_done", "pt_ev", "pv_done", "o_ev", "wo_done", "wo_add"))
        raw_g = [[sem(f"raw_g{i}{j}") for j in range(2)] for i in range(2)]
        raw_d = [sem(f"raw_d{i}") for i in range(2)]
        hi_g, hi_d, lo_g, lo_d = (sem(n) for n in ("hi_g", "hi_d", "lo_g", "lo_d"))
        xu_tr, xhi_ev, xlo_ev, gu_done, sg_done, h_ready, ht_tr, hth_done, htl_done, down_done, out_free = (
            sem(n) for n in ("xu_tr", "xhi_ev", "xlo_ev", "gu_done", "sg_done", "h_ready", "ht_tr",
                             "hth_done", "htl_done", "down_done", "out_free"))
        q_done, q_ev, sv_done, sv_ev, ss_done, st_ready, sm_ready, se_done, sp_ready, st_tr, spt_ev, spv_done, so_ev = (
            sem(n) for n in ("q_done", "q_ev", "sv_done", "sv_ev", "ss_done", "st_ready", "sm_ready", "se_done",
                             "sp_ready", "st_tr", "spt_ev", "spv_done", "so_ev"))
        snk_ready = sem("snk_ready")
        hn_st = [sem(f"hn_st{i}") for i in range(2)]
        lg_done, d_ready, e_ready, m_ready, rk_done, cnt_ready, pos_ready, zero_set, zero_st, lst_sc, lst_ld = (
            sem(n) for n in ("lg_done", "d_ready", "e_ready", "m_ready", "rk_done", "cnt_ready", "pos_ready",
                             "zero_set", "zero_st", "lst_sc", "lst_ld"))
        xg_ready = [sem(f"xg_ready{i}") for i in range(2)]
        yo_ready, y_free, y_all, lsg_ready = sem("yo_ready"), sem("y_free"), sem("y_all"), sem("lsg_ready")
        y_st = [sem(f"y_st{i}") for i in range(2)]
        y_ld = [sem(f"y_ld{i}") for i in range(2)]
        y_used, fo_ready = sem("y_used"), sem("fo_ready")
        o_st = [sem(f"o_st{i}") for i in range(2)]
        block = ctx.enter_context(nc.Block())

        WIDE = (0, 1, 2, 3)

        U_MOE, S_MOE = 2, FFN_TOTAL

        ONE, TWO, FEWER = (1, False), (2, False), (1, True)

        def shares(kind, k):
            nt, few = kind
            return (k,) if nt == 1 and not few else (k // 2, k // 2)

        def steps(eng, s0, par0, n, step, more):
            assert more or n % 2
            step(s0, par0, 0, True)
            step(s0 + 1, 1 - par0, 1, True)
            with eng.Fori(0, (n - 2) // 2) as j:
                step(s0 + (j * 2 + 2), par0, 2, True)
                step(s0 + (j * 2 + 3), 1 - par0, 2, True)
            if n % 2:
                step(s0 + (n - 1), par0, 2, more)

        def by_count(eng, n, body):
            with eng.If(n > P + FEW):
                body(TWO)
            with eng.Else():
                with eng.If(n > P):
                    body(FEWER)
                with eng.Else():
                    body(ONE)

        @block.sync
        def _(sp):
            def gain(dst, src, s):
                sp.dma_start(dst, src.partition_broadcast(P)).then_inc(s, 16)

            xt = a["x"].rearrange("b (t p) d -> (b t) p d", p=P)
            for t in range(NT):
                sp.dma_start(H[:, t, :], xt[t]).then_inc(ld_h[t], 16)
                if t == 0:
                    sp.dma_start(IDN[:, :], a["identity"]).then_inc(ld_id, 16)
                    gain(GB[0][:, :], a["mla_norm"][0], ld_gain)
            wd = a["mla_w_dqkv"][0].rearrange("(k p) n -> p k n", p=P)
            for k in range(0, KD, 2):
                sp.dma_start(m_wd[:, k:k + 2, :], wd[:, k:k + 2, :]).then_inc(ld_wd, 16)
            sp.dma_start(m_tab[:, :], a["rope_table"]).then_inc(ld_tab, 16)
            gain(m_gq[:, 0:QR], a["mla_q_norm"][0], ld_tab)
            gain(m_gq[:, QR:QR + KVR], a["mla_kv_norm"][0], ld_tab)
            sp.dma_start(m_uv[:, :, :], a["mla_w_uv"][0].rearrange("(c p) h d -> p c (h d)", p=P)).then_inc(ld_uv, 16)
            sp.dma_start(m_uq[:, :, :, :], a["mla_w_uq"][0].rearrange("(c p) h d -> p c h d", p=P)).then_inc(ld_uq, 16)
            sp.dma_start(m_uk[:, :, :, :], a["mla_w_uk"][0].rearrange("(c p) h d -> p c h d", p=P)).then_inc(ld_uk, 16)
            gain(GB[1][:, :], a["ffn_norm"][0], gain_b)
            sp.dma_start(TRI[:, :], a["earlier"]).then_inc(ld_route, 16)
            sp.dma_start(ONES[:, :], a["ones"]).then_inc(ld_route, 16)
            sp.wait_ge(dq_done, NT)
            sp.wait_ge(kr_done, 1)
            sp.wait_ge(wqr_ready, 6)
            sp.dma_start(m_wo[:, :, :], a["mla_w_o"][0].rearrange("(h p) n -> p h n", p=P)).then_inc(ld_mwo, 16)
            sp.wait_ge(xn_ready, NT)
            gain(GB[0][:, :], a["swa_norm"][0], ld_gain)

            def load_g(s, par, rows):
                for i in range(2):
                    sp.wait_ge(lo_g, s * 2 + (i + 1))
                    sp.dma_start(f_rg[par][i][:, :, :], rows(i)).then_inc(raw_g[par][i], 16)

            def load_d(s, par, down):
                sp.wait_ge(lo_d, s + 1)
                sp.dma_start(f_rd[par][:, :, :], down).then_inc(raw_d[par], 16)

            sp.wait_ge(pv_done, HEADS)
            def ffn_g(s):
                load_g(s, s % 2, lambda i: a["ffn_gu"][s % FFN_STEPS, i])

            ffn_g(0)
            for s in range(FFN_TOTAL):
                if s + 1 < FFN_TOTAL:
                    ffn_g(s + 1)
                load_d(s, s % 2, a["ffn_down"][s % FFN_STEPS])

            sp.wait_ge(out_free, 2)
            wq = a["swa_w_qkv"].rearrange("(k p) n -> p k n", p=P)
            for k in range(0, KD, 2):
                sp.dma_start(s_w[:, k:k + 2, :], wq[:, k:k + 2, :]).then_inc(ld_sw, 16)
            sp.dma_start(s_dist[:, :], a["distance"]).then_inc(ld_sc, 16)
            gain(s_snk[:, :], a["swa_sink"][0], ld_sc)
            wo = a["swa_w_o"].rearrange("(c r p) n -> p c r n", c=2, r=GRP)
            for c in range(2):
                sp.dma_start(s_wo[:, c, :, :], wo[:, c]).then_inc(ld_swo, 16)
            sp.wait_ge(xn_ready, 2 * NT)
            gain(GB[1][:, :], a["moe_norm"][0], gain_b)

            sp.wait_ge(sv_done, NT)
            sp.dma_start(g_rt[:, :, :], a["moe_router"][0].rearrange("(k p) n -> p k n", p=P)).then_inc(ld_route, 16)
            sp.dma_start(g_c[:, :, :, :], a["route_consts"]).then_inc(ld_route, 16)
            for t in range(NT):
                sp.wait_ge(xn_ready, 3 * NT + t + 1)
                sp.dma_start(hn_d[t * P:(t + 1) * P, :], XG[t % 2][:, :]).then_inc(hn_st[t % 2], 16)

            sp.wait_ge(wo_add, 4 * NT)
            def expert_gu(e, f):
                return lambda i: a["moe_gu"][bass.ds(e, 1), f, i].rearrange("o p k f -> (o p) k f")

            def expert_loads(e, nxt, sfirst, few):
                for f in range(MOE_STEPS):
                    s = e * MOE_STEPS + (sfirst + f)
                    last = f + 1 == MOE_STEPS
                    if few or f < 1:
                        sp.wait_ge(gu_done, s * 2 + 4)
                    load_g(s + 1, (f + 1) % 2, expert_gu(nxt if last else e, (f + 1) % MOE_STEPS))
                    if few or f < 2:
                        sp.wait_ge(down_done, s + 1)
                    load_d(s, f % 2, a["moe_down"][bass.ds(e, 1), f].rearrange("o p c n -> (o p) c n"))

            def experts(sfirst, turn):
                with sp.Fori(0, NE) as e:
                    nxt = sp.snap((e + 1) % NE, min_val=0, max_val=NE - 1)
                    if turn:
                        expert_loads(e, nxt, sfirst, False)
                    else:
                        n = sp.value_load(CNT[0:1, bass.ds(e, 1)], min_val=0, max_val=CAP)
                        by_count(sp, n, lambda kind: expert_loads(e, nxt, sfirst, kind == FEWER))

            load_g(S_MOE, 0, lambda i: a["moe_gu"][0, 0, i])
            sp.wait_ge(cnt_ready, 1)
            experts(S_MOE, 0)
            most = sp.value_load(CNT[0:1, NE:NE + 1], min_val=0, max_val=CAP)
            with sp.If(most > 2 * P):
                experts(S_MOE + NE * MOE_STEPS, 1)

            sp.wait_ge(y_all, 1)
            yt = y_d.rearrange("(t p c) d -> t p c d", p=P, c=2)
            for t in range(2):
                sp.dma_start(y_rows[t][:, :, :], yt[t]).then_inc(y_ld[t], 16)
            gain(GB[0][:, :], a["final_norm"], ld_gain)
            for t in range(2, NT):
                sp.wait_ge(y_used, t - 1)
                sp.dma_start(y_rows[t % 2][:, :, :], yt[t]).then_inc(y_ld[t % 2], 16)
            ot = out.rearrange("b (t p) d -> (b t) p d", p=P)
            for t in range(NT):
                sp.wait_ge(fo_ready, t + 1)
                sp.dma_start(ot[t], y_out[t % 2][:, :]).then_inc(o_st[t % 2], 16)
            for i in range(2):
                sp.wait_ge(o_st[i], 16 * NT // 2)

        @block.tensor
        def _(pe):
            pe.sem_inc(gu_done, 4)
            pe.sem_inc(down_done, 2)
            pe.wait_ge(ld_id, 16)

            def x_transpose(norm, phase, t, banks):
                pe.wait_ge(xn_ready, NT * norm + t + 1)
                for hf in range(2):
                    i = 2 * t + hf
                    if i >= len(banks):
                        pe.wait_ge(xT_ev, 2 * NT * phase + i - len(banks) + 1)
                    for k in range(4):
                        c = 4 * hf + k
                        last = pe.transpose(PS[:, banks[i % len(banks)], k * P:(k + 1) * P],
                                            XG[t % 2][:, c * P:(c + 1) * P], IDN[:, :])
                    last.then_inc(xT_tr, 1)

            for t in range(NT):
                x_transpose(0, 0, t, WIDE)
            for t in range(NT):
                pe.wait_ge(xT_ev, 2 * t + 2)
                if t == 0:
                    pe.wait_ge(ld_wd, 64)
                if t >= 2:
                    pe.wait_ge(cn_ready, t - 1)
                for k in range(KD):
                    last = pe.matmul(PS[:, 4 + t % 2, :], m_xT[:, k, t * P:(t + 1) * P], m_wd[:, k, 0:QR + KVR],
                                     start=k == 0, stop=k == KD - 1)
                last.then_inc(dq_done, 1)
            pe.wait_ge(wkr_ready, 3)
            for k in range(KD):
                last = pe.matmul(PS[:, 6, :], m_wkr[:, k, :], m_xT[:, k, :], start=k == 0, stop=k == KD - 1)
            last.then_inc(kr_done, 1)
            for t in range(NT):
                pe.wait_ge(cn_ready, t + 1)
                if t:
                    pe.wait_ge(ct_ev, t)
                for c in range(4):
                    last = pe.transpose(PS[:, 7, c * P:(c + 1) * P], m_cn[:, t, c * P:(c + 1) * P], IDN[:, :])
                last.then_inc(ct_tr, 1)
            pe.wait_ge(ct_ev, NT)
            pe.wait_ge(ld_uv, 16)
            for i in range(2 * NT):
                t, n = i // 2, i % 2
                if i >= 4:
                    pe.wait_ge(v_ev, i - 3)
                for c in range(2):
                    last = pe.matmul(PS[:, i % 4, :], m_cT[:, 2 + c, t * P:(t + 1) * P],
                                     m_uv[:, c, n * 512:(n + 1) * 512], start=c == 0, stop=c == 1)
                last.then_inc(v_done, 1)

            def project(h):
                if h == 0:
                    pe.wait_ge(ld_uq, 16)
                    pe.wait_ge(ld_uk, 16)
                    pe.wait_ge(wqr_ready, 6)
                    pe.wait_ge(kr_ready, 1)
                else:
                    pe.wait_ge(pj_ev, 2 * h)
                    pe.wait_ge(qr_ready, h)
                for b, w, c0 in ((4, lambda c: m_uq[:, c, h, 0:NOPE], 0), (5, lambda c: m_uk[:, c, h, :], 2),
                                 (6, lambda c: m_wqr[:, c, h, :], 0)):
                    for c in range(2):
                        last = pe.matmul(PS[:, b, :], w(c), m_cT[:, c0 + c, :], start=c == 0, stop=c == 1)
                    last.then_inc(pj_done, 1)

            project(0)
            for h in range(HEADS):
                b = h % 2
                pe.wait_ge(pj_ev, 2 * h + 2)
                pe.wait_ge(qr_ready, h + 1)
                for qt in range(NT):
                    if h == 0:
                        pe.wait_ge(v_ev, 2 * NT)
                    else:
                        pe.wait_ge(pt_ev, NT * (h - 1) + qt + 1)
                    q = slice(qt * P, (qt + 1) * P)
                    pe.matmul(PS[:, qt, :], m_qn[b][:, q], m_kn[b][:, :], start=True, stop=False)
                    pe.matmul(PS[:, qt, :], m_qr[b][:, q], m_kr[:, :], start=False, stop=True).then_inc(sc_done, 1)
                if h + 1 < HEADS:
                    project(h + 1)
                for qt in range(NT):
                    pe.wait_ge(pn_ready, NT * h + qt + 1)
                    for c in range(NT):
                        last = pe.transpose(PS[:, qt, c * P:(c + 1) * P], m_p[b][:, qt, c * P:(c + 1) * P], IDN[:, :])
                    last.then_inc(tr_done, 1)
                if h:
                    pe.wait_ge(o_ev, h)
                pe.wait_ge(pt_ev, NT * h + NT)
                for c in range(NT):
                    last = pe.matmul(PS[:, 7, :], m_v[:, c, h * P:(h + 1) * P], m_pT[b][:, c, :],
                                     start=c == 0, stop=c == NT - 1)
                last.then_inc(pv_done, 1)

            def out_projection(phase, oT, w, behind):
                for i in range(2 * NT):
                    t, n = i // 2, i % 2
                    if i >= 4:
                        pe.wait_ge(wo_add, 2 * NT * phase + i - 3)
                    for c in range(8):
                        last = pe.matmul(PS[:, i % 4, :], oT(c)[:, t * P:(t + 1) * P],
                                         w(c)[:, n * 512:(n + 1) * 512], start=c == 0, stop=c == 7)
                    last.then_inc(wo_done, 1)
                    if i % 2 and t:
                        behind(t - 1)
                behind(NT - 1)

            pe.wait_ge(o_ev, HEADS)
            pe.wait_ge(ld_mwo, 16)
            out_projection(0, lambda c: m_oT[:, c, :], lambda c: m_wo[:, c, :],
                           lambda t: None)

            def passes(dst, xh, xl, wh, wl, start, stop):
                pe.matmul(dst, xh, wh, start=start, stop=False)
                pe.matmul(dst, xh, wl, start=False, stop=False)
                return pe.matmul(dst, xl, wh, start=False, stop=stop)

            def unit(u, s0, par0, n, kind, source, more, free):
                nt, few = kind
                two = shares(kind, 2)
                four = shares(kind, 4)
                for t in range(nt):
                    source(t)
                    for hf in range(2):
                        if t:
                            pe.wait_ge(xlo_ev, u * 4 + (hf + 1))
                        for k in range(4):
                            c = 4 * hf + k
                            last = pe.transpose(PS[:, 6 + hf, k * P:(k + 1) * P], XG[t][:, c * P:(c + 1) * P],
                                                IDN[:, :])
                        last.then_inc(xu_tr, two[0])
                if few:
                    source(1)
                    pe.wait_ge(xlo_ev, u * 4 + 2)
                    for k in range(KD):
                        last = pe.transpose(PS[:, 6 + k // 4, k % 4 * P:(k % 4 + 1) * P], XG[1][:, k * P:(k + 1) * P],
                                            IDN[:, :])
                    last.then_inc(xu_tr, 2)
                pe.wait_ge(xlo_ev, u * 4 + 4)

                def to_columns(s):
                    for t in range(nt):
                        pe.wait_ge(h_ready, s * 4 + (1 if few else (t + 1) * four[0]))
                        for c in range(2):
                            last = pe.transpose(PS[:, 6 + t, c * P:(c + 1) * P], f_h[t][:, c * P:(c + 1) * P],
                                                IDN[:, :])
                        last.then_inc(ht_tr, two[0])

                def few_to_columns(s):
                    pe.wait_ge(h_ready, s * 4 + 4)
                    for c in range(2):
                        last = pe.transpose(PS[:, 7, c * P:(c + 1) * P], f_h[1][:, c * P:(c + 1) * P], IDN[:, :])
                    last.then_inc(ht_tr, two[0])

                def down(s, par, first, final=False):
                    pe.wait_ge(lo_d, s + 3)
                    if first:
                        free()
                    for t in range(nt):
                        pe.wait_ge(htl_done, s * 2 + (t + 1) * two[0])
                        for n_ in range(2):
                            col = slice(n_ * 512, (n_ + 1) * 512)
                            for c in range(2):
                                last = passes(PS[:, 2 * t + n_, :], f_hh[:, t, c, :], f_hl[:, t, c, :],
                                              f_hd[par][:, c, col], f_ld[par][:, c, col],
                                              first and c == 0, final and c == 1)
                    if few:
                        pe.wait_ge(htl_done, s * 2 + 2)
                        for c in range(2):
                            for j in range(4):
                                last = pe.matmul(PS[FEW * j:FEW * (j + 1), 2, 0:FB], f_hbT[:, c, :],
                                                 f_rd[par][:, c, j * FB:(j + 1) * FB],
                                                 start=first and c == 0, stop=final and c == 1)
                    last.then_inc(down_done, 1)

                def step(s, par, which, nxt):
                    if which:
                        to_columns(s - 1)
                    pe.wait_ge(lo_g, s * 2 + 6)
                    for t in range(nt):
                        tok = slice(t * P, (t + 1) * P)
                        for g in range(2):
                            col = slice(g * FB, (g + 1) * FB)
                            for k in range(KD):
                                last = passes(PS[:, 4 + t, col], f_xh[:, k, tok], f_xl[:, k, tok],
                                              f_hg[par][:, k, col], f_lg[par][:, k, col], k == 0, k == KD - 1)
                        last.then_inc(gu_done, two[0])
                    if few:
                        if which:
                            few_to_columns(s - 1)
                        for k in range(4):
                            for j in range(4):
                                g, hf = j // 2, j % 2
                                last = pe.matmul(PS[FEW * j:FEW * (j + 1), 5, 0:FB], f_xb[:, 4 * hf + k, :],
                                                 f_rg[par][hf][:, k, g * FB:(g + 1) * FB],
                                                 start=k == 0, stop=k == 3)
                        last.then_inc(gu_done, 1)
                    if which:
                        down(s - 1, 1 - par, which == 1)

                steps(pe, s0, par0, n, step, more)
                to_columns(s0 + (n - 1))
                if few:
                    few_to_columns(s0 + (n - 1))
                down(s0 + (n - 1), (par0 + n - 1) % 2, False, True)

            for u in range(2):
                def source(t, u=u):
                    pe.wait_ge(xn_ready, NT + 2 * u + t + 1)

                def free(u=u):
                    if u:
                        pe.wait_ge(out_free, u)

                unit(u, u * FFN_STEPS, u * FFN_STEPS % 2, FFN_STEPS, TWO, source, u == 0, free)

            for t in range(NT):
                x_transpose(2, 1, t, WIDE)
            pe.wait_ge(xT_ev, 4 * NT)
            pe.wait_ge(ld_sw, 64)
            for i in range(10):
                if i >= 4:
                    pe.wait_ge(q_ev, i - 3)
                for k in range(KD):
                    last = pe.matmul(PS[:, i % 4, :], s_w[:, k, i * P:(i + 1) * P], s_xT[:, k, :], start=k == 0, stop=k == KD - 1)
                last.then_inc(q_done, 1)
            for t in range(NT):
                if t >= 2:
                    pe.wait_ge(sv_ev, t - 1)
                for k in range(KD):
                    c0 = QH * HD + KVH * HD
                    last = pe.matmul(PS[:, 4 + t % 2, 0:KVH * HD], s_xT[:, k, t * P:(t + 1) * P],
                                     s_w[:, k, c0:c0 + KVH * HD], start=k == 0, stop=k == KD - 1)
                last.then_inc(sv_done, 1)

            def swa_scores(i):
                g, t = i // NT, i % NT
                half, c = g % 2, g // 2
                rows = slice(half * HD, half * HD + HD)
                lo, hi = max(0, t - 1) * P, min(NT, t + 2) * P
                if i == 0:
                    pe.wait_ge(q_ev, 10)
                else:
                    pe.wait_ge(st_ready, i)
                for r_ in range(GRP):
                    last = pe.matmul(PS[:, r_, 0:hi - lo], s_q[rows, c, r_, t * P:(t + 1) * P],
                                     s_k[rows, c, lo:hi], start=True, stop=True)
                last.then_inc(ss_done, 1)

            def swa_keys(i):
                return [kt for kt in (i % NT - 1, i % NT, i % NT + 1) if 0 <= kt < NT]

            def swa_values(i):
                g = i // NT
                half, keys = g % 2, swa_keys(i)
                pe.wait_ge(spt_ev, i + 1)
                if i:
                    pe.wait_ge(so_ev, i)
                for j, kt in enumerate(keys):
                    last = pe.matmul(PS[half * HD:half * HD + HD, 7, :], s_v[:, kt, g * HD:(g + 1) * HD],
                                     s_pT[i % 2][:, j, :, :].rearrange("p r q -> p (r q)"),
                                     start=j == 0, stop=j == len(keys) - 1)
                last.then_inc(spv_done, 1)

            swa_scores(0)
            swa_scores(1)
            for i in range(16):
                if i + 2 < 16:
                    swa_scores(i + 2)
                pe.wait_ge(sp_ready, i + 1)
                if i == 0:
                    pe.wait_ge(sv_ev, NT)
                else:
                    pe.wait_ge(spt_ev, i)
                for j in range(len(swa_keys(i))):
                    for r_ in range(GRP):
                        last = pe.transpose(PS[:, 4 + j, r_ * P:(r_ + 1) * P],
                                            s_p[i % 2][:, r_, j * P:(j + 1) * P], IDN[:, :])
                last.then_inc(st_tr, 1)
                if i:
                    swa_values(i - 1)
            swa_values(15)
            pe.wait_ge(so_ev, 16)
            pe.wait_ge(ld_swo, 32)
            out_projection(1, lambda c: s_o[:, c // GRP, c % GRP, :], lambda c: s_wo[:, c // GRP, c % GRP, :],
                           lambda t: x_transpose(3, 2, t, (6, 7)))

            pe.wait_ge(xT_ev, 6 * NT)
            pe.wait_ge(ld_route, 64)
            for t in range(NT):
                for k in range(KD):
                    last = pe.matmul(PS[:, 4, t * NE:(t + 1) * NE], g_xT[:, k, t * P:(t + 1) * P], g_rt[:, k, :],
                                     start=k == 0, stop=k == KD - 1)
            last.then_inc(lg_done, 1)
            pe.wait_ge(m_ready, 1)
            for t in range(NT):
                dst = PS[:, 5, t * NE:(t + 1) * NE]
                for t2 in range(t + 1):
                    pe.matmul(dst, (TRI if t2 == t else ONES)[:, :], g_m[:, t2, :], start=t2 == 0, stop=t2 == t)
            for t in range(NT):
                last = pe.matmul(PS[:, 5, NT * NE:NT * NE + NE], ONES[:, :], g_m[:, t, :], start=t == 0, stop=t == NT - 1)
            last.then_inc(rk_done, 1)

            pe.wait_ge(cnt_ready, 1)

            def expert(e, turn, kind):
                def source(t):
                    pe.wait_ge(xg_ready[t], e * 16 + 16 * (NE * turn + 1))

                def free():
                    pe.wait_ge(yo_ready, e * 2 + (2 * NE * turn + 2))

                unit(e + (U_MOE + NE * turn), e * MOE_STEPS + (S_MOE + turn * NE * MOE_STEPS), 0, MOE_STEPS, kind,
                     source, True, free)

            with pe.Fori(0, NE) as e:
                n = pe.value_load(CNT[0:1, bass.ds(e, 1)], min_val=0, max_val=CAP)
                by_count(pe, n, lambda kind: expert(e, 0, kind))
            most = pe.value_load(CNT[0:1, NE:NE + 1], min_val=0, max_val=CAP)
            with pe.If(most > 2 * P):
                with pe.Fori(0, NE) as e:
                    expert(e, 1, TWO)

        @block.scalar
        def _(act):
            def copy(dst, src):
                return act.activation(dst, src, ACT.Copy)

            def std(norm, t):
                act.wait_ge(ss_ready, NT * norm + t + 1)
                act.activation(SD[:, t:t + 1], SS[:, t:t + 1], ACT.Sqrt, bias=EPSC[:, :]).then_inc(std_ready, 1)

            def x_evict(phase, xT, t, banks):
                for hf in range(2):
                    act.wait_ge(xT_tr, 2 * NT * phase + 2 * t + hf + 1)
                    copy(xT[:, 4 * hf:4 * hf + 4, t * P:(t + 1) * P],
                         PS[:, banks[(2 * t + hf) % len(banks)], :].rearrange("p (k q) -> p k q", k=4)).then_inc(xT_ev, 1)

            def stds_and_x(norm, phase, xT, banks):
                for t in range(NT):
                    std(norm, t)
                    if t:
                        x_evict(phase, xT, t - 1, banks)
                x_evict(phase, xT, NT - 1, banks)

            act.wait_ge(eps_set, 1)
            stds_and_x(0, 0, m_xT, WIDE)
            for t in range(NT):
                act.wait_ge(dq_done, t + 1)
                for i in range(2):
                    act.activation(m_junk[:, i, :], PS[:, 4 + t % 2, i * QR:(i + 1) * QR], ACT.Square,
                                   accum_out=m_sq[:, 2 * t + i:2 * t + i + 1]).then_inc(sq_done, 1)
                act.wait_ge(sq_done, 2 * t + 2)
                act.activation(m_sd[:, 2 * t:2 * t + 2], m_sq[:, 2 * t:2 * t + 2], ACT.Sqrt, scale=1.0 / QR,
                               bias=EPSC[:, :]).then_inc(cstd, 1)
            for t in range(NT):
                act.wait_ge(ct_tr, t + 1)
                copy(m_cT[:, :, t * P:(t + 1) * P],
                     PS[:, 7, :].rearrange("p (c q) -> p c q", c=4)).then_inc(ct_ev, 1)
            for i in range(2 * NT):
                act.wait_ge(v_done, i + 1)
                copy(m_v[:, i // 2, (i % 2) * 512:(i % 2 + 1) * 512], PS[:, i % 4, :]).then_inc(v_ev, 1)

            def project_evict(h):
                if h >= 2:
                    act.wait_ge(sc_done, NT * (h - 1))
                act.wait_ge(pj_done, 3 * h + 1)
                copy(m_qn[h % 2][:, :], PS[:, 4, :]).then_inc(pj_ev, 1)
                act.wait_ge(pj_done, 3 * h + 2)
                copy(m_kn[h % 2][:, :], PS[:, 5, :]).then_inc(pj_ev, 1)

            project_evict(0)
            for h in range(HEADS):
                b = h % 2
                for qt in range(NT):
                    i = NT * h + qt
                    act.wait_ge(nm_ready, i + 1)
                    if h >= 2:
                        act.wait_ge(tr_done, i - 2 * NT + 1)
                    act.activation(m_p[b][:, qt, :], PS[:, qt, :], ACT.Exp, bias=m_nm[:, i:i + 1], scale=MLA_SCALE,
                                   accum_out=m_sm[:, i:i + 1]).then_inc(ex_done, 1)
                if h + 1 < HEADS:
                    project_evict(h + 1)
                for qt in range(NT):
                    act.wait_ge(tr_done, NT * h + qt + 1)
                    if h >= 2:
                        act.wait_ge(pv_done, h - 1)
                    copy(m_pT[b][:, :, qt * P:(qt + 1) * P],
                         PS[:, qt, :].rearrange("p (c q) -> p c q", c=NT)).then_inc(pt_ev, 1)
                act.wait_ge(pv_done, h + 1)
                copy(m_oT[:, h, :], PS[:, 7, :]).then_inc(o_ev, 1)

            def hi_gu(s, par):
                for i in range(2):
                    act.wait_ge(raw_g[par][i], s * 8 + (16 - 8 * par))
                    act.wait_ge(gu_done, s * 2 + 2)
                    copy(f_hg[par][:, 4 * i:4 * i + 2, :], f_rg[par][i][:, 0:2, :])
                    copy(f_hg[par][:, 4 * i + 2:4 * i + 4, :], f_rg[par][i][:, 2:4, :]).then_inc(hi_g, 1)

            def unit(u, s0, par0, n, kind, more):
                nt, few = kind
                two, four = shares(kind, 2), shares(kind, 4)
                for q in range(2 * nt):
                    t, hf = q // 2, q % 2
                    act.wait_ge(xu_tr, u * 4 + (q + 1) * two[0])
                    copy(f_xh[:, 4 * hf:4 * hf + 4, t * P:(t + 1) * P],
                         PS[:, 6 + hf, :].rearrange("p (k q) -> p k q", k=4))\
                        .then_inc(xhi_ev, two[0] + (2 if few and q else 0))

                def hidden_T(s):
                    for t in range(nt):
                        act.wait_ge(ht_tr, s * 2 + (t + 1) * two[0])
                        copy(f_hh[:, t, :, :], PS[:, 6 + t, 0:2 * P].rearrange("p (c q) -> p c q", c=2))\
                            .then_inc(hth_done, 2 if few else two[0])

                def step(s, par, which, nxt):
                    if which:
                        hidden_T(s - 1)
                    if nxt:
                        hi_gu(s + 1, 1 - par)
                    for t in range(nt):
                        act.wait_ge(gu_done, s * 2 + (4 + (t + 1) * two[0]))
                        act.activation(f_sg[t][:, :], PS[:, 4 + t, 0:FB], ACT.Silu)\
                            .then_inc(sg_done, 1 if few else four[0])
                    if few:
                        act.wait_ge(gu_done, s * 2 + 6)
                        copy(f_cb[0:FEW, :], PS[FEW:2 * FEW, 5, 0:FB])
                        copy(f_cb[2 * FEW:3 * FEW, :], PS[3 * FEW:P, 5, 0:FB]).then_inc(sg_done, 1)
                    act.wait_ge(raw_d[par], s * 8 + (16 - 8 * par))
                    act.wait_ge(down_done, s + 1)
                    copy(f_hd[par][:, 0, :], f_rd[par][:, 0, :])
                    if few:
                        act.wait_ge(h_ready, s * 4 + 2)
                        act.activation(f_sb, f_gb[:, 0:FB], ACT.Silu).then_inc(sg_done, 2)
                    copy(f_hd[par][:, 1, :], f_rd[par][:, 1, :]).then_inc(hi_d, 1)

                steps(act, s0, par0, n, step, more)
                hidden_T(s0 + (n - 1))

            hi_gu(0, 0)
            for t in range(NT):
                std(1, t)
            for u in range(2):
                unit(u, u * FFN_STEPS, u * FFN_STEPS % 2, FFN_STEPS, TWO, u == 0)

            stds_and_x(2, 1, s_xT, WIDE)
            for i in range(10):
                act.wait_ge(q_done, i + 1)
                dst = s_q[:, i // GRP, i % GRP, :] if i < 8 else s_k[:, i - 8, :]
                copy(dst, PS[:, i % 4, :]).then_inc(q_ev, 1)
            for t in range(NT):
                act.wait_ge(sv_done, t + 1)
                copy(s_v[:, t, :], PS[:, 4 + t % 2, 0:KVH * HD]).then_inc(sv_ev, 1)

            def swa_probs(i):
                t = i % NT
                w = (min(NT, t + 2) - max(0, t - 1)) * P
                act.wait_ge(sm_ready, i + 1)
                if i >= 2:
                    act.wait_ge(st_tr, i - 1)
                for r_ in range(GRP):
                    act.activation(s_p[i % 2][:, r_, 0:w], s_s[i % 2][:, r_, 0:w], ACT.Exp, scale=SWA_SCALE,
                                   bias=s_nm[:, GRP * i + r_:GRP * i + r_ + 1],
                                   accum_out=s_sm[:, GRP * i + r_:GRP * i + r_ + 1])
                c = slice(GRP * i, GRP * i + GRP)
                act.activation(s_es[:, c], s_es[:, c], ACT.Exp, scale=SWA_SCALE).then_inc(se_done, 1)

            def swa_o_evict(i):
                t, half, c = i % NT, (i // NT) % 2, i // NT // 2
                act.wait_ge(spv_done, i + 1)
                rows = slice(half * HD, half * HD + HD)
                copy(s_o[rows, c, :, t * P:(t + 1) * P],
                     PS[rows, 7, :].rearrange("p (r q) -> p r q", r=GRP)).then_inc(so_ev, 1)

            swa_probs(0)
            swa_probs(1)
            for i in range(16):
                t = i % NT
                nk = min(NT, t + 2) - max(0, t - 1)
                act.wait_ge(st_tr, i + 1)
                if i >= 2:
                    act.wait_ge(spv_done, i - 1)
                for j in range(nk):
                    last = copy(s_pT[i % 2][:, j, :, :], PS[:, 4 + j, :].rearrange("p (r q) -> p r q", r=GRP))
                last.then_inc(spt_ev, 1)
                if i + 2 < 16:
                    swa_probs(i + 2)
                if i:
                    swa_o_evict(i - 1)
            swa_o_evict(15)

            stds_and_x(3, 2, g_xT, (6, 7))
            act.wait_ge(d_ready, 1)
            act.activation(g_e[:, :], g_d[:, :], ACT.Exp).then_inc(e_ready, 1)
            hi_gu(S_MOE, 0)
            act.wait_ge(cnt_ready, 1)

            def expert(e, turn, kind):
                u = e + (U_MOE + NE * turn)
                s0 = e * MOE_STEPS + (S_MOE + turn * NE * MOE_STEPS)
                unit(u, s0, 0, MOE_STEPS, kind, True)
                act.wait_ge(down_done, s0 + (MOE_STEPS + 2))
                nt, few = kind
                act.wait_ge(y_free, e + (NE * turn + 1))
                for t in range(nt):
                    for n_ in range(2):
                        last = copy(GB[1 - t][:, n_ * 512:(n_ + 1) * 512], PS[:, 2 * t + n_, :])
                    last.then_inc(yo_ready, shares(kind, 2)[0])
                if few:
                    for j in range(4):
                        last = copy(GB[0][0:FEW, j * FB:(j + 1) * FB], PS[FEW * j:FEW * (j + 1), 2, 0:FB])
                    last.then_inc(yo_ready, 1)

            act.sem_inc(yo_ready, 2)
            with act.Fori(0, NE) as e:
                n = act.value_load(CNT[0:1, bass.ds(e, 1)], min_val=0, max_val=CAP)
                by_count(act, n, lambda kind: expert(e, 0, kind))
            most = act.value_load(CNT[0:1, NE:NE + 1], min_val=0, max_val=CAP)
            with act.If(most > 2 * P):
                with act.Fori(0, NE) as e:
                    expert(e, 1, TWO)
            for t in range(NT):
                std(4, t)

        @block.vector
        def _(dve):
            dve.sem_inc(lo_g, 4)
            dve.sem_inc(lo_d, 2)
            count = [0]

            def link(ins):
                count[0] += 1
                ins.then_inc(chain, 1)
                dve.wait_ge(chain, count[0])

            tt, ts, stt = dve.tensor_tensor, dve.tensor_scalar, dve.scalar_tensor_tensor

            def mean_square(t):
                dve.tensor_tensor_reduce(out=PS[:, 4:6, :].rearrange("p b n -> p (b n)"), in0=H[:, t, :], in1=H[:, t, :],
                                         scale=1.0 / D, scalar=0.0, op0=ALU.mult, op1=ALU.add,
                                         accum_out=SS[:, t:t + 1]).then_inc(ss_ready, 1)

            def rstd(norm, t):
                dve.wait_ge(std_ready, NT * norm + t + 1)
                link(dve.reciprocal(RS[:, t:t + 1], SD[:, t:t + 1]))

            def rows(t, gain_, dst=None):
                return stt((dst or XG[t % 2])[:, :], H[:, t, :], RS[:, t:t + 1], gain_[:, :], ALU.mult, ALU.mult)

            dve.memset(EPSC[:, :], EPS).then_inc(eps_set, 1)
            for t in range(NT):
                dve.wait_ge(ld_h[t], 16)
                if t:
                    dve.wait_ge(ss_ready, t)
                mean_square(t)
            dve.wait_ge(ld_gain, 16)
            for t in range(NT):
                rstd(0, t)
                if t >= 2:
                    dve.wait_ge(xT_tr, 2 * (t - 1))
                rows(t, GB[0]).then_inc(xn_ready, 1)
            dve.wait_ge(ld_tab, 48)
            for t in range(NT):
                dve.wait_ge(cstd, t + 1)
                link(dve.reciprocal(m_rq[:, 2 * t:2 * t + 2], m_sd[:, 2 * t:2 * t + 2]))
                for i in range(2):
                    c = slice(i * QR, (i + 1) * QR)
                    ins = stt(m_cn[:, t, c], PS[:, 4 + t % 2, c], m_rq[:, 2 * t + i:2 * t + i + 1], m_gq[:, c],
                              ALU.mult, ALU.mult)
                ins.then_inc(cn_ready, 1)

            def rope(dst):
                tt(m_t1[:, :], PS[0:ROPE, 6, :], m_tab[0:ROPE, :], ALU.mult)
                link(tt(m_t2[:, :], PS[ROPE:P, 6, :], m_tab[ROPE:P, :], ALU.mult))
                return tt(dst[:, :], m_t1[:, :], m_t2[:, :], ALU.add)

            dve.wait_ge(kr_done, 1)
            rope(m_kr).then_inc(kr_ready, 1)

            def rope_head(h):
                dve.wait_ge(pj_done, 3 * h + 3)
                if h >= 2:
                    dve.wait_ge(sc_done, NT * (h - 1))
                if h:
                    dve.wait_ge(qr_ready, h)
                else:
                    dve.wait_ge(kr_ready, 1)
                rope(m_qr[h % 2]).then_inc(qr_ready, 1)

            def normalise(h, qt):
                i = NT * h + qt
                dve.wait_ge(ex_done, i + 1)
                link(dve.reciprocal(m_rc[:, i:i + 1], m_sm[:, i:i + 1]))
                ts(m_p[h % 2][:, qt, :], m_p[h % 2][:, qt, :], m_rc[:, i:i + 1], None, ALU.mult).then_inc(pn_ready, 1)

            rope_head(0)
            for h in range(HEADS):
                for qt in range(NT):
                    i = NT * h + qt
                    dve.wait_ge(sc_done, i + 1)
                    link(dve.reduce_max(m_mx[:, i:i + 1], PS[:, qt, :], AXX))
                    ts(m_nm[:, i:i + 1], m_mx[:, i:i + 1], -MLA_SCALE, None, ALU.mult).then_inc(nm_ready, 1)
                    if qt:
                        normalise(h, qt - 1)
                normalise(h, NT - 1)
                if h + 1 < HEADS:
                    rope_head(h + 1)

            def add_projection(phase, norm, then):
                for t in range(NT):
                    for n_ in range(2):
                        i, c = 2 * t + n_, slice(n_ * 512, (n_ + 1) * 512)
                        dve.wait_ge(wo_done, 2 * NT * phase + i + 1)
                        tt(H[:, t, c], H[:, t, c], PS[:, i % 4, :], ALU.add).then_inc(wo_add, 1)
                    dve.wait_ge(wo_add, 2 * NT * phase + 2 * t + 2)
                    if t:
                        dve.wait_ge(ss_ready, NT * norm + t)
                    mean_square(t)
                    rstd(norm, t)
                    then(t)

            def lo_part(dst, src, hi):
                return tt(dst, src, hi.bitcast(F32), ALU.subtract)

            def lo_gu(s, par):
                for i in range(2):
                    dve.wait_ge(hi_g, s * 2 + (i + 1))
                    for j in range(2):
                        k = slice(4 * i + 2 * j, 4 * i + 2 * j + 2)
                        last = lo_part(f_lg[par][:, k, :], f_rg[par][i][:, 2 * j:2 * j + 2, :], f_hg[par][:, k, :])
                    last.then_inc(lo_g, 1)

            def unit(u, s0, par0, n, kind, more):
                nt, few = kind
                two, four = shares(kind, 2), shares(kind, 4)
                for q in range(2 * nt):
                    t, hf = q // 2, q % 2
                    dve.wait_ge(xhi_ev, u * 4 + (q + 1) * two[0])
                    k, tok = slice(4 * hf, 4 * hf + 4), slice(t * P, (t + 1) * P)
                    lo_part(f_xl[:, k, tok], PS[:, 6 + hf, :].rearrange("p (k q) -> p k q", k=4),
                            f_xh[:, k, tok]).then_inc(xlo_ev, two[0])
                if few:
                    dve.wait_ge(xu_tr, u * 4 + 4)
                    for hf in range(2):
                        dve.tensor_copy(f_xb[:, 4 * hf:4 * hf + 4, :],
                                        PS[:, 6 + hf, :].rearrange("p (k q) -> p k q", k=4)[:, :, 0:FEW])\
                            .then_inc(xlo_ev, 1)

                def hidden_T(s):
                    for t in range(nt):
                        dve.wait_ge(hth_done, s * 2 + (t + 1) * two[0])
                        lo_part(f_hl[:, t, :, :], PS[:, 6 + t, 0:2 * P].rearrange("p (c q) -> p c q", c=2),
                                f_hh[:, t, :, :]).then_inc(htl_done, two[0])

                def few_hidden_T(s):
                    dve.wait_ge(ht_tr, s * 2 + 2)
                    dve.tensor_copy(f_hbT[:, :, :], PS[:, 7, 0:2 * P].rearrange("p (c q) -> p c q", c=2)[:, :, 0:FEW])\
                        .then_inc(htl_done, 1)

                def step(s, par, which, nxt):
                    if which:
                        hidden_T(s - 1)
                    if nxt:
                        lo_gu(s + 1, 1 - par)
                    if few and which:
                        few_hidden_T(s - 1)
                    for t in range(nt):
                        dve.wait_ge(sg_done, s * 4 + (1 if few else (t + 1) * four[0]))
                        tt(f_h[t][:, :], f_sg[t][:, :], PS[:, 4 + t, FB:2 * FB], ALU.mult)\
                            .then_inc(h_ready, 1 if few else four[0])
                    if few:
                        dve.wait_ge(sg_done, s * 4 + 2)
                        tt(f_gb[:, 0:FB], PS[0:FEW, 5, 0:FB], f_cb[0:FEW, :], ALU.add)
                        tt(f_gb[:, FB:2 * FB], PS[2 * FEW:3 * FEW, 5, 0:FB], f_cb[2 * FEW:3 * FEW, :], ALU.add)\
                            .then_inc(h_ready, 1)
                    dve.wait_ge(hi_d, s + 1)
                    lo_part(f_ld[par][:, 0, :], f_rd[par][:, 0, :], f_hd[par][:, 0, :])
                    if few:
                        dve.wait_ge(sg_done, s * 4 + 4)
                        tt(f_hb, f_sb, f_gb[:, FB:2 * FB], ALU.mult).then_inc(h_ready, 2)
                    lo_part(f_ld[par][:, 1, :], f_rd[par][:, 1, :], f_hd[par][:, 1, :]).then_inc(lo_d, 1)

                steps(dve, s0, par0, n, step, more)
                hidden_T(s0 + (n - 1))
                if few:
                    few_hidden_T(s0 + (n - 1))

            lo_gu(0, 0)
            dve.wait_ge(gain_b, 16)

            def ffn_rows(t):
                rows(t, GB[1]).then_inc(xn_ready, 1)

            add_projection(0, 1, lambda t: ffn_rows(t) if t < 2 else None)
            for u in range(2):
                if u:
                    for t in range(2):
                        dve.wait_ge(xu_tr, 2 * t + 2)
                        ffn_rows(2 + t)
                unit(u, u * FFN_STEPS, u * FFN_STEPS % 2, FFN_STEPS, TWO, u == 0)
                dve.wait_ge(down_done, 2 + (u + 1) * FFN_STEPS)
                for i in range(4):
                    t, c = 2 * u + i // 2, slice((i % 2) * 512, (i % 2 + 1) * 512)
                    ins = tt(H[:, t, c], H[:, t, c], PS[:, i, :], ALU.add)
                ins.then_inc(out_free, 1)
            dve.wait_ge(out_free, 2)

            dve.wait_ge(ld_gain, 32)

            def swa_rows(t):
                rstd(2, t)
                if t >= 2:
                    dve.wait_ge(xT_tr, 2 * NT + 2 * (t - 1))
                rows(t, GB[0]).then_inc(xn_ready, 1)

            for t in range(NT):
                if t:
                    dve.wait_ge(ss_ready, NT * 2 + t)
                mean_square(t)
                if t:
                    swa_rows(t - 1)
            swa_rows(NT - 1)
            dve.wait_ge(ld_sc, 32)
            link(ts(s_sk8[:, :], s_snk[:, :], SCALE8, None, ALU.mult))

            def swa_logits(i):
                g, t = i // NT, i % NT
                w = (min(NT, t + 2) - max(0, t - 1)) * P
                off = P if t == 0 else 0
                b, c = i % 2, slice(GRP * i, GRP * i + GRP)
                dve.wait_ge(ss_done, i + 1)
                if i >= 2:
                    dve.wait_ge(se_done, i - 1)
                for r_ in range(GRP):
                    slope = 2.0 ** (-8.0 * (GRP * g + r_ + 1) / QH)
                    last = stt(s_s[b][:, r_, 0:w], s_dist[:, off:off + w], -SCALE8 * slope, PS[:, r_, 0:w],
                               ALU.mult, ALU.add)
                last.then_inc(st_ready, 1)
                dve.wait_ge(st_ready, i + 1)
                link(dve.reduce_max(s_rc[:, c], s_s[b][:, :, 0:w], AXX))
                link(tt(s_mx[:, c], s_rc[:, c], s_sk8[:, GRP * g:GRP * g + GRP], ALU.max))
                ts(s_nm[:, c], s_mx[:, c], -SWA_SCALE, None, ALU.mult)
                tt(s_es[:, c], s_sk8[:, GRP * g:GRP * g + GRP], s_mx[:, c], ALU.subtract).then_inc(sm_ready, 1)

            def swa_normalise(i):
                t = i % NT
                w = (min(NT, t + 2) - max(0, t - 1)) * P
                c = slice(GRP * i, GRP * i + GRP)
                dve.wait_ge(se_done, i + 1)
                link(tt(s_mx[:, c], s_sm[:, c], s_es[:, c], ALU.add))
                link(dve.reciprocal(s_rc[:, c], s_mx[:, c]))
                for r_ in range(GRP):
                    last = ts(s_p[i % 2][:, r_, 0:w], s_p[i % 2][:, r_, 0:w], s_rc[:, GRP * i + r_:GRP * i + r_ + 1],
                              None, ALU.mult)
                last.then_inc(sp_ready, 1)

            swa_logits(0)
            swa_logits(1)
            for i in range(16):
                swa_normalise(i)
                if i + 2 < 16:
                    swa_logits(i + 2)
            dve.wait_ge(gain_b, 32)

            def moe_rows(t):
                if t >= 2:
                    dve.wait_ge(xT_tr, 4 * NT + 2 * (t - 1))
                    dve.wait_ge(hn_st[t % 2], 16)
                rows(t, GB[1]).then_inc(xn_ready, 1)

            add_projection(1, 3, moe_rows)

            dve.wait_ge(ld_route, 64)
            wide = lambda x: x[:, :].unsqueeze(2).to_broadcast((P, NT, NE))
            rev, at_pos = (g_c[:, i, :, :] for i in range(2))
            dve.wait_ge(lg_done, 1)
            link(dve.tensor_copy(g_lg[:, :, :], PS[:, 4, 0:NT * NE].rearrange("p (t e) -> p t e", t=NT)))

            def pick(lg, m, eq, w, first, oh):
                link(dve.reduce_max(m[:, :], lg[:, :, :], AXX))
                link(tt(eq[:, :, :], lg[:, :, :], wide(m), ALU.is_equal))
                link(tt(w[:, :, :], eq[:, :, :], rev, ALU.mult))
                link(dve.reduce_max(first[:, :], w[:, :, :], AXX))
                link(tt(oh[:, :, :], rev, wide(first), ALU.is_equal))

            pick(g_lg, g_m1, g_eq, g_w1, g_i1, g_o1)
            link(stt(g_l2[:, :, :], g_o1[:, :, :], -3e38, g_lg[:, :, :], ALU.mult, ALU.add))
            pick(g_l2, g_m2, g_eq, g_w2, g_i2, g_o2)
            tt(g_m[:, :, :], g_o1[:, :, :], g_o2[:, :, :], ALU.add).then_inc(m_ready, 1)
            tt(g_d[:, :], g_m2[:, :], g_m1[:, :], ALU.subtract).then_inc(d_ready, 1)
            dve.wait_ge(e_ready, 1)
            link(ts(g_s1[:, :], g_e[:, :], 1.0, None, ALU.add))
            link(dve.reciprocal(G12[:, 0:NT], g_s1[:, :]))
            link(tt(G12[:, NT:2 * NT], g_e[:, :], G12[:, 0:NT], ALU.mult))
            dve.wait_ge(rk_done, 1)
            link(dve.tensor_copy(g_cf[:, 0:NE], PS[:, 5, NT * NE:NT * NE + NE]))
            link(dve.reduce_max(g_cf[:, NE:NE + 1], g_cf[:, 0:NE], AXX))
            dve.tensor_copy(CNT[:, :], g_cf[:, :]).then_inc(cnt_ready, 1)
            link(dve.tensor_copy(g_rk[:, :, :], PS[:, 5, 0:NT * NE].rearrange("p (t e) -> p t e", t=NT)))
            link(ts(g_j[:, :, :], g_rk[:, :, :], float(P), None, ALU.is_ge))
            link(stt(g_j2[:, :, :], g_rk[:, :, :], float(2 * P), g_j[:, :, :], ALU.is_ge, ALU.add))
            link(stt(g_j3[:, :, :], g_rk[:, :, :], float(3 * P), g_j2[:, :, :], ALU.is_ge, ALU.add))
            link(stt(g_pos0[:, :, :], g_rk[:, :, :], float(NE * NT), at_pos, ALU.mult, ALU.add))
            link(stt(g_pos[:, :, :], g_j3[:, :, :], 1.0 - P * NE * NT, g_pos0[:, :, :], ALU.mult, ALU.add))
            for c, oh in enumerate((g_o1, g_o2)):
                link(tt(g_pr[c][:, :, :], oh[:, :, :], g_pos[:, :, :], ALU.mult))
                link(dve.reduce_sum(g_sel[:, c, :], g_pr[c][:, :, :], AXX))
            dve.tensor_copy(g_posi[:, :, :], g_sel[:, :, :]).then_inc(pos_ready, 1)
            dve.wait_ge(lst_ld, 16)
            link(ts(LSM[:, :], LST[:, :], 2 * S - 1, None, ALU.min))
            ts(LSG[:, :], LSM[:, :], 1, None, ALU.arith_shift_right).then_inc(lsg_ready, 1)

            lo_gu(S_MOE, 0)

            def expert(e, turn, kind):
                unit(e + (U_MOE + NE * turn), e * MOE_STEPS + (S_MOE + turn * NE * MOE_STEPS), 0, MOE_STEPS, kind, True)

            with dve.Fori(0, NE) as e:
                n = dve.value_load(CNT[0:1, bass.ds(e, 1)], min_val=0, max_val=CAP)
                by_count(dve, n, lambda kind: expert(e, 0, kind))
            most = dve.value_load(CNT[0:1, NE:NE + 1], min_val=0, max_val=CAP)
            with dve.If(most > 2 * P):
                with dve.Fori(0, NE) as e:
                    expert(e, 1, TWO)

            def final_rows(t):
                rstd(4, t)
                if t == 0:
                    dve.wait_ge(ld_gain, 48)
                if t >= 2:
                    dve.wait_ge(o_st[t % 2], 16)
                rows(t, GB[0], y_out[t % 2]).then_inc(fo_ready, 1)

            for t in range(NT):
                dve.wait_ge(y_ld[t % 2], 16 * (t // 2 + 1))
                for c in range(2):
                    ins = stt(H[:, t, :], y_rows[t % 2][:, c, :], G12[:, c * NT + t:c * NT + t + 1], H[:, t, :],
                              ALU.mult, ALU.add)
                    if c == 0:
                        link(ins)
                ins.then_inc(y_used, 1)
                dve.wait_ge(y_used, t + 1)
                if t:
                    dve.wait_ge(ss_ready, NT * 4 + t)
                mean_square(t)
                if t:
                    final_rows(t - 1)
            final_rows(NT - 1)

        @block.gpsimd
        def _(pool):
            def with_swapped(dst, src, s):
                h_ = ROPE // 2
                pool.tensor_copy(dst[..., 0:ROPE], src).then_inc(s, 1)
                pool.tensor_copy(dst[..., ROPE:ROPE + h_], src[..., h_:ROPE]).then_inc(s, 1)
                pool.tensor_copy(dst[..., ROPE + h_:P], src[..., 0:h_]).then_inc(s, 1)

            pool.wait_ge(ld_wd, 64)
            with_swapped(m_wkr[:, :, :], m_wd[:, :, QR + KVR:DOWN], wkr_ready)
            pool.wait_ge(ld_uq, 16)
            for c in range(2):
                with_swapped(m_wqr[:, c, :, :], m_uq[:, c, :, NOPE:QK], wqr_ready)

            pool.wait_ge(sv_done, NT)
            pool.memset(g_zero[:, :], 2 * S).then_inc(zero_set, 1)
            pool.iota(g_tok[:, :, :], pattern=[[1, 2], [2 * P, NT]], base=0, channel_multiplier=2).then_inc(zero_set, 1)
            pool.wait_ge(zero_set, 2)
            pool.dma_start(lst_d.rearrange("(p j) o -> p (j o)", p=P), g_zero[:, :]).then_inc(zero_st, 16)
            pool.wait_ge(zero_st, 16)
            pool.wait_ge(pos_ready, 1)
            offset = lambda ap: bass.IndirectOffsetOnAxis(ap=ap, axis=0)
            for c in range(2):
                for t in range(NT):
                    pool.indirect_dma_start(out=lst_d, out_offset=offset(g_posi[:, c, t:t + 1]),
                                            in_=g_tok[:, c, t:t + 1], in_offset=None).then_inc(lst_sc, 16)
            pool.wait_ge(lst_sc, 2 * NT * 16)
            pool.dma_start(LST[:, :], lst_d.rearrange("(p j) o -> p (j o)", p=P)).then_inc(lst_ld, 16)
            pool.wait_ge(lst_ld, 16)
            pool.wait_ge(lsg_ready, 1)
            for i in range(2):
                pool.wait_ge(hn_st[i], 16 * NT // 2)

            def gather(k):
                e, turn = k % NE, k // NE
                pool.wait_ge(xu_tr, 4 * (U_MOE + k))
                for t in range(2):
                    if k:
                        pool.wait_ge(xg_ready[t], 16 * k)
                    j = NT * e + 2 * turn + t
                    pool.indirect_dma_start(out=XG[t][:, :], out_offset=None, in_=hn_d,
                                            in_offset=offset(LSG[:, j:j + 1])).then_inc(xg_ready[t], 16)

            def scatter(k):
                e, turn = k % NE, k // NE
                pool.wait_ge(yo_ready, 2 * k + 4)
                for t in range(2):
                    j = NT * e + 2 * turn + t
                    pool.indirect_dma_start(out=y_d, out_offset=offset(LST[:, j:j + 1]), in_=GB[1 - t][:, :],
                                            in_offset=None, bounds_check=2 * S - 1, oob_is_err=False)\
                        .then_inc(y_st[t], 16)
                for t in range(2):
                    pool.wait_ge(y_st[t], 16 * (k + 1))
                pool.sem_inc(y_free, 1)

            def experts(turn):
                gather(NE * turn)
                for e in range(NE):
                    if e + 1 < NE:
                        gather(NE * turn + e + 1)
                    scatter(NE * turn + e)

            pool.wait_ge(xT_tr, 6 * NT)
            pool.sem_inc(y_free, 1)
            experts(0)
            most = pool.value_load(CNT[0:1, NE:NE + 1], min_val=0, max_val=CAP)
            with pool.If(most > 2 * P):
                experts(1)
            pool.sem_inc(y_all, 1)


def constants():
    inv = (1.0 / (np.float32(10000.0) ** (np.arange(0, ROPE, 2, dtype=np.float32) / np.float32(ROPE)))).astype(np.float32)
    ang = (np.arange(S, dtype=np.float32)[:, None] * inv[None, :]).astype(np.float32)
    cos, sin = np.cos(ang).T, np.sin(ang).T
    j = np.arange(SPAN) - WIN
    dist = np.abs(np.arange(P)[:, None] - j[None, :]).astype(np.float32)
    e = np.arange(NE, dtype=np.float32)
    route = np.stack([NE - e, NT * e])[None, :, None, :]
    return {
        "identity": np.eye(P, dtype=np.float32),
        "earlier": np.triu(np.ones((P, P), np.float32), 1),
        "ones": np.ones((P, P), np.float32),
        "rope_table": np.concatenate([cos, cos, -sin, sin]).astype(np.float32),
        "distance": np.where(dist <= WIN, dist, np.float32(1e30)).astype(np.float32),
        "route_consts": np.broadcast_to(route, (P, 2, NT, NE)).astype(np.float32).copy(),
    }


def laid_out(inputs):
    rest = ["x", "mla_norm", "mla_w_dqkv", "mla_q_norm", "mla_w_uq", "mla_kv_norm", "mla_w_uk", "mla_w_uv", "mla_w_o",
            "swa_norm", "swa_sink", "ffn_norm", "moe_norm", "moe_router", "final_norm"]
    got = {n: np.asarray(inputs[n]) for n in rest}

    def gate_up(gate, up, blocks):
        both = np.stack([np.asarray(gate), np.asarray(up)], -2)
        n = both.shape[0]
        x = both.reshape(n, 2, KD // 2, P, 2, blocks, FB)
        return x.transpose(0, 5, 1, 3, 2, 4, 6).reshape(n, blocks, 2, P, KD // 2, 2 * FB)

    def down(w, blocks):
        w = np.asarray(w)
        return w.reshape(w.shape[0], blocks, 2, P, D).transpose(0, 1, 3, 2, 4)

    got["ffn_gu"] = gate_up(inputs["ffn_w_gate"], inputs["ffn_w_up"], FFN_STEPS)[0]
    got["ffn_down"] = down(inputs["ffn_w_down"], FFN_STEPS)[0]
    got["moe_gu"] = gate_up(inputs["moe_w_gate"][0], inputs["moe_w_up"][0], MOE_STEPS)
    got["moe_down"] = down(inputs["moe_w_down"][0], MOE_STEPS)
    w = np.asarray(inputs["swa_w_qkv"])[0]
    q = w[:, :QH * HD].reshape(D, 2, 2, GRP, HD).transpose(0, 1, 3, 2, 4).reshape(D, QH * HD)
    got["swa_w_qkv"] = np.concatenate([q, w[:, QH * HD:]], 1)
    wo = np.asarray(inputs["swa_w_o"])[0]
    got["swa_w_o"] = wo.reshape(2, 2, GRP, HD, D).transpose(0, 2, 1, 3, 4).reshape(QH * HD, D)
    return {n: np.ascontiguousarray(x) for n, x in got.items()}


def kernel(**inputs):
    import concourse.bacc as bacc
    from concourse.bass_utils import run_bass_kernel_spmd

    nc = bacc.Bacc("TRN2", target_bir_lowering=False, num_devices=1)
    arrays, args = {}, {}
    for name, x in {**laid_out(inputs), **constants()}.items():
        arrays[f"in_{name}"] = x
        args[name] = nc.dram_tensor(f"in_{name}", x.shape, mybir.dt.from_np(x.dtype), kind="ExternalInput").ap()
    out = nc.dram_tensor("out", (1, S, D), F32, kind="ExternalOutput").ap()
    build_trunk(nc, args, out)
    r = run_bass_kernel_spmd(nc, [arrays], core_ids=[0])
    return r.results[0]["out"]
```

```python
from contextlib import ExitStack

import numpy as np

import concourse.bass as bass
from concourse import mybir

F32 = mybir.dt.float32
F32R = mybir.dt.float32r
I32 = mybir.dt.int32
ALU = mybir.AluOpType
ACT = mybir.ActivationFunctionType
AXX = mybir.AxisListType.X

P = 128
S = 512
D = 1024
NT = S // P
KD = D // P
EPS = 1e-6

QR = 256
KVR = 256
NOPE = 128
ROPE = 64
HEADS = 8
QK = NOPE + ROPE
DOWN = QR + KVR + ROPE
MLA_SCALE = QK ** -0.5

KVH = 4
GRP = 4
HD = 64
QH = KVH * GRP
SCALE8 = 8.0
SWA_SCALE = HD ** -0.5
WIN = 128
SPAN = 3 * P

FFN = 2816
NE = 8
ED = 2048
FB = 256
FEW = 32
FFN_STEPS = FFN // FB
MOE_STEPS = ED // FB
FFN_TOTAL = 2 * FFN_STEPS
CAP = S

BASE = 16640


def build_trunk(nc, a, out):
    hn_d = nc.dram_tensor("hn_rows", [S, D], F32, kind="Internal").ap()
    y_d = nc.dram_tensor("expert_rows", [2 * S, D], F32, kind="Internal").ap()

    def at(name, shape, offset, dt=F32):
        return nc.alloc_sbuf_tensor_at(name, shape, dt, offset=offset)

    class Region:

        def __init__(self, start, end):
            self.at, self.end = start, end

        def __call__(self, name, shape, dt=F32):
            size = int(np.prod(shape[1:])) * 4
            x = at(name, shape, self.at, dt)
            self.at += (size + 31) // 32 * 32
            assert self.at <= self.end, (name, self.at, self.end)
            return x

    fixed = Region(BASE, 229344)
    H = fixed("H", [P, NT, D])
    GB = [fixed("gain_a", [P, D]), fixed("gain_b", [P, D])]
    XG = [fixed("rows_a", [P, D]), fixed("rows_b", [P, D])]
    IDN = fixed("identity", [P, P])
    TRI = fixed("earlier", [P, P])
    ONES = fixed("ones", [P, P])
    small = lambda n, w, dt=F32: fixed(n, [P, w], dt)
    SS, SD, RS = small("mean_square", NT), small("std", NT), small("rstd", NT)
    EPSC = small("eps", 1)
    CNT = small("counts", NE + 1, I32)
    LST = small("slot_tokens", NE * NT, I32)
    LSM = small("slot_rows", NE * NT, I32)
    LSG = small("slot_gather", NE * NT, I32)
    G12 = small("gates", 2 * NT)
    AREA = fixed.at

    r = Region(AREA, 229344)
    m_xT = r("mla_xT", [P, KD, S])
    m_wd = r("w_dqkv", [P, KD, DOWN])
    m_wkr = r("w_krope", [P, KD, P])
    m_wo = at("mla_wo", [P, HEADS, D], AREA)
    m_pT = [at("probsT0", [P, NT, S], r.at)]
    m_cn = r("c_norm", [P, NT, QR + KVR])
    m_cT = r("c_T", [P, NT, S])
    m_uq = r("w_uq", [P, 2, HEADS, QK])
    m_uk = r("w_uk", [P, 2, HEADS, NOPE])
    m_pT.append(at("probsT1", [P, NT, S], r.at))
    m_uv = r("w_uv", [P, 2, HEADS * P])
    m_wqr = r("w_qrope", [P, 2, HEADS, P])
    m_v = r("mla_v", [P, NT, HEADS * P])
    m_qn = [r(f"q_nope{i}", [P, S], F32R) for i in range(2)]
    m_kn = [r(f"k_nope{i}", [P, S], F32R) for i in range(2)]
    m_qr = [r(f"q_rope{i}", [2 * ROPE, S], F32R) for i in range(2)]
    m_kr = r("k_rope", [2 * ROPE, S], F32R)
    m_t1, m_t2 = r("rope_t1", [ROPE, S]), r("rope_t2", [ROPE, S])
    m_p = [r(f"probs{i}", [P, NT, S]) for i in range(2)]
    m_oT = r("mla_oT", [P, HEADS, S])
    m_tab = r("rope_table", [P, S])
    m_gq = r("gain_qkv", [P, QR + KVR])
    m_sq, m_sd, m_rq = r("c_sq", [P, 2 * NT]), r("c_sd", [P, 2 * NT]), r("c_rstd", [P, 2 * NT])
    m_junk = r("c_junk", [P, 2, QR])
    m_mx, m_nm = r("row_max", [P, HEADS * NT]), r("neg_max", [P, HEADS * NT])
    m_sm, m_rc = r("row_sum", [P, HEADS * NT]), r("row_rcp", [P, HEADS * NT])

    m_qnl = [r(f"q_nope_lo{i}", [P, S], F32R) for i in range(2)]
    m_knl = [r(f"k_nope_lo{i}", [P, S], F32R) for i in range(2)]
    m_krl = r("k_rope_lo", [ROPE, S], F32R)

    r = Region(AREA, 229344)
    f_xh = r("xT_hi", [P, KD, 2 * P], F32R)
    f_xl = r("xT_lo", [P, KD, 2 * P], F32R)
    f_sg = [r(f"silu{i}", [P, FB]) for i in range(2)]
    f_h = [r(f"hidden{i}", [P, FB]) for i in range(2)]
    f_hh = r("hT_hi", [P, 2, 2, P], F32R)
    f_hl = r("hT_lo", [P, 2, 2, P], F32R)
    f_ld = [r("lo_down1", [P, 2, D], F32R)]
    RAW = r.at
    ROUTED = AREA + 4 * KD * S + 2048
    f_rg = [[r(f"raw_gu{i}{j}", [P, 4, 2 * FB]) for j in range(2)] for i in range(2)]
    f_rd = [r(f"raw_down{i}", [P, 2, D]) for i in range(2)]
    f_hg = [r(f"hi_gu{i}", [P, KD, 2 * FB], F32R) for i in range(2)]
    f_lg = [r(f"lo_gu{i}", [P, KD, 2 * FB], F32R) for i in range(2)]
    f_hd = [r(f"hi_down{i}", [P, 2, D], F32R) for i in range(2)]
    f_ld.insert(0, r("lo_down0", [P, 2, D], F32R))
    f_xb = r("xT_few", [P, KD, FEW])
    f_cb = r("gu_few_half", [P, FB])
    f_gb = r("gu_few", [FEW, 2 * FB])
    f_sb, f_hb = f_sg[1][0:FEW, :], f_h[1][0:FEW, :]
    f_hbT = r("hT_few", [P, 2, FEW])

    s_xT = at("swa_xT", [P, KD, S], AREA)
    PARTS = (RAW, RAW + 6 * 8192, RAW + 10 * 8192)
    assert 4 * KD * 512 == 2 * 8192
    s_w = [at(f"w_qkv{i}", [P, KD, 512], o) for i, o in enumerate(PARTS)]
    s_wo = [at(f"swa_wo{c}", [P, GRP, D], PARTS[c]) for c in range(2)]
    r = Region(ROUTED, RAW)
    s_s = [r(f"swa_scores{i}", [P, GRP, SPAN]) for i in range(2)]
    r = Region(RAW + 2 * 8192, PARTS[1])
    s_q = r("swa_qT", [P, 2, GRP, S])
    s_o = r("swa_oT", [P, 2, GRP, S])
    r = Region(PARTS[1] + 2 * 8192, PARTS[2])
    s_p = [r(f"swa_probs{i}", [P, GRP, SPAN]) for i in range(2)]
    s_k = r("swa_kT", [P, 2, S])
    r = Region(PARTS[2] + 2 * 8192, 229344)
    s_pT = [r(f"swa_probsT{i}", [P, 3, GRP, P]) for i in range(2)]
    s_v = r("swa_v", [P, NT, KVH * HD])
    s_dist = r("distance", [P, SPAN])
    s_snk, s_sk8 = r("sink", [P, QH]), r("sink8", [P, QH])
    s_mx, s_nm = r("swa_max", [P, 16 * GRP]), r("swa_neg", [P, 16 * GRP])
    s_es, s_sm = r("swa_esink", [P, 16 * GRP]), r("swa_sum", [P, 16 * GRP])
    s_rc = r("swa_rcp", [P, 16 * GRP])

    r = Region(AREA, RAW)
    g_xT = r("moe_xT", [P, KD, S])
    g_rt = r("router", [P, KD, NE])
    g_c = r("route_consts", [P, 2, NT, NE])
    rt = lambda n, k=NE: r(n, [P, NT, k])
    g_sc = r("slot_consts", [P, P + NE * NT + 2 * NT])
    assert r.at <= ROUTED
    g_lg, g_eq, g_w1, g_l2, g_w2 = (rt(n) for n in ("lg", "eq", "w1", "l2", "w2"))
    g_oh = r("choices", [P, 2, NT, NE])
    g_o1, g_o2 = g_oh[:, 0, :, :], g_oh[:, 1, :, :]
    g_m = r("chosen", [P, (NT + 1) * NE])
    g_rk, g_j, g_j2 = (rt(n) for n in ("rank", "j1", "j2"))
    g_tile, g_part, g_list = (rt(n) for n in ("slot_tile", "slot_partition", "list_column"))
    g_m1, g_i1, g_m2, g_i2, g_d, g_e, g_s1 = (r(n, [P, NT]) for n in ("m1", "i1", "m2", "i2", "d21", "e2", "s1"))
    g_pr = [r(f"pick{c}", [P, 2 * NT, NE]) for c in range(2)]
    g_sel = [r(f"picked{c}", [P, 2 * NT]) for c in range(2)]
    g_at = r("slot_rows_hot", [P, 2 * NT, P])
    g_val = r("slot_values", [P, 2 * NT, NE * NT])
    g_lf = r("list_f", [P, NE * NT])
    g_cf = r("counts_f", [P, NE + 1])

    r = Region(RAW + 14 * 8192, 229344)
    y_rows = [r(f"y{i}", [P, 2, D]) for i in range(2)]
    y_out = [r(f"out{i}", [P, D]) for i in range(2)]

    ctx = ExitStack()
    with ctx:
        PS = ctx.enter_context(nc.psum_tensor("PS", [P, 8, 512], F32))
        sem = lambda n: ctx.enter_context(nc.semaphore(n))
        ld_h = [sem(f"ld_h{t}") for t in range(NT)]
        ld_id, ld_gain, ld_wd, ld_tab, ld_uq, ld_uk, ld_uv, ld_mwo = (
            sem(n) for n in ("ld_id", "ld_gain", "ld_wd", "ld_tab", "ld_uq", "ld_uk", "ld_uv", "ld_mwo"))
        ld_sw = [sem(f"ld_sw{c}") for c in range(3)]
        ld_sc, ld_swo, ld_route = (sem(n) for n in ("ld_sc", "ld_swo", "ld_route"))
        gain_b = sem("gain_b_loaded")
        chain = sem("dve_chain")
        ss_ready, std_ready, xn_ready, xT_tr, xT_ev = (
            sem(n) for n in ("ss_ready", "std_ready", "xn_ready", "xT_tr", "xT_ev"))
        eps_set, wkr_ready, wqr_ready = sem("eps_set"), sem("wkr_ready"), sem("wqr_ready")
        dq_done, sq_done, cstd, cn_ready, ct_tr, ct_ev, kr_done, kr_ready = (
            sem(n) for n in ("dq_done", "sq_done", "cstd", "cn_ready", "ct_tr", "ct_ev", "kr_done", "kr_ready"))
        pj_lo, qs_ready, qh_ready, ks_ready, kh_ready = (
            sem(n) for n in ("pj_lo", "qs_ready", "qh_ready", "ks_ready", "kh_ready"))
        v_done, v_ev, pj_done, pj_ev, qr_ready, sc_done, nm_ready, ex_done = (
            sem(n) for n in ("v_done", "v_ev", "pj_done", "pj_ev", "qr_ready", "sc_done", "nm_ready", "ex_done"))
        pn_ready, tr_done, pt_ev, pv_done, o_ev, wo_done, wo_add = (
            sem(n) for n in ("pn_ready", "tr_done", "pt_ev", "pv_done", "o_ev", "wo_done", "wo_add"))
        raw_g = [[sem(f"raw_g{i}{j}") for j in range(2)] for i in range(2)]
        raw_d = [sem(f"raw_d{i}") for i in range(2)]
        hi_g, hi_d, lo_g, lo_d = (sem(n) for n in ("hi_g", "hi_d", "lo_g", "lo_d"))
        xu_tr, xhi_ev, xlo_ev = ([sem(f"{n}{t}") for t in range(2)] for n in ("xu_tr", "xhi_ev", "xlo_ev"))
        gu_done, sg_done, h_ready, ht_tr, hth_done, htl_done, down_done, out_free = (
            sem(n) for n in ("gu_done", "sg_done", "h_ready", "ht_tr",
                             "hth_done", "htl_done", "down_done", "out_free"))
        q_done, q_ev, sv_done, sv_ev, ss_done, st_ready, sm_ready, se_done, sp_ready, st_tr, spt_ev, spv_done, so_ev = (
            sem(n) for n in ("q_done", "q_ev", "sv_done", "sv_ev", "ss_done", "st_ready", "sm_ready", "se_done",
                             "sp_ready", "st_tr", "spt_ev", "spv_done", "so_ev"))
        snk_ready = sem("snk_ready")
        hn_st = [sem(f"hn_st{i}") for i in range(2)]
        lg_done, d_ready, e_ready, m_ready, rk_done, cnt_ready, hot_ready, list_done = (
            sem(n) for n in ("lg_done", "d_ready", "e_ready", "m_ready", "rk_done", "cnt_ready", "hot_ready",
                             "list_done"))
        xg_ready = [sem(f"xg_ready{i}") for i in range(2)]
        yo_ready, y_free, y_all, lsg_ready = sem("yo_ready"), sem("y_free"), sem("y_all"), sem("lsg_ready")
        y_st = [sem(f"y_st{i}") for i in range(2)]
        y_ld = [sem(f"y_ld{i}") for i in range(2)]
        y_used, fo_ready = sem("y_used"), sem("fo_ready")
        o_st = [sem(f"o_st{i}") for i in range(2)]
        block = ctx.enter_context(nc.Block())

        WIDE = (0, 1, 2, 3)
        X_BANKS = ((4, 5), (6, 7))

        U_MOE, S_MOE = 2, FFN_TOTAL

        ONE, TWO, FEWER = (1, False), (2, False), (1, True)

        def shares(kind, k):
            nt, few = kind
            return (k,) if nt == 1 and not few else (k // 2, k // 2)

        def steps(eng, s0, par0, n, step, more):
            assert more or n % 2
            step(s0, par0, 0, True)
            step(s0 + 1, 1 - par0, 1, True)
            with eng.Fori(0, (n - 2) // 2) as j:
                step(s0 + (j * 2 + 2), par0, 2, True)
                step(s0 + (j * 2 + 3), 1 - par0, 2, True)
            if n % 2:
                step(s0 + (n - 1), par0, 2, more)

        def by_count(eng, n, body):
            with eng.If(n > P + FEW):
                body(TWO)
            with eng.Else():
                with eng.If(n > P):
                    body(FEWER)
                with eng.Else():
                    body(ONE)

        @block.sync
        def _(sp):
            def gain(dst, src, s):
                sp.dma_start(dst, src.partition_broadcast(P)).then_inc(s, 16)

            xt = a["x"].rearrange("b (t p) d -> (b t) p d", p=P)
            wd = a["mla_w_dqkv"][0].rearrange("(k p) n -> p k n", p=P)
            for t in range(NT):
                sp.dma_start(H[:, t, :], xt[t]).then_inc(ld_h[t], 16)
                if t == 0:
                    sp.dma_start(IDN[:, :], a["identity"]).then_inc(ld_id, 16)
                    gain(GB[0][:, :], a["mla_norm"][0], ld_gain)
                if t == 1:
                    for k in range(0, KD, 2):
                        sp.dma_start(m_wd[:, k:k + 2, :], wd[:, k:k + 2, :]).then_inc(ld_wd, 16)
            sp.dma_start(m_tab[:, :], a["rope_table"]).then_inc(ld_tab, 16)
            gain(m_gq[:, 0:QR], a["mla_q_norm"][0], ld_tab)
            gain(m_gq[:, QR:QR + KVR], a["mla_kv_norm"][0], ld_tab)
            sp.dma_start(m_uv[:, :, :], a["mla_w_uv"][0].rearrange("(c p) h d -> p c (h d)", p=P)).then_inc(ld_uv, 16)
            sp.dma_start(m_uq[:, :, :, :], a["mla_w_uq"][0].rearrange("(c p) h d -> p c h d", p=P)).then_inc(ld_uq, 16)
            sp.dma_start(m_uk[:, :, :, :], a["mla_w_uk"][0].rearrange("(c p) h d -> p c h d", p=P)).then_inc(ld_uk, 16)
            gain(GB[1][:, :], a["ffn_norm"][0], gain_b)
            sp.dma_start(TRI[:, :], a["earlier"]).then_inc(ld_route, 16)
            sp.dma_start(ONES[:, :], a["ones"]).then_inc(ld_route, 16)
            sp.wait_ge(dq_done, NT)
            sp.wait_ge(kr_done, 1)
            sp.wait_ge(wqr_ready, 6)
            sp.dma_start(m_wo[:, :, :], a["mla_w_o"][0].rearrange("(h p) n -> p h n", p=P)).then_inc(ld_mwo, 16)
            sp.wait_ge(xn_ready, NT)
            gain(GB[0][:, :], a["swa_norm"][0], ld_gain)

            def load_g(s, par, rows):
                for i in range(2):
                    sp.wait_ge(lo_g, s * 2 + (i + 1))
                    sp.dma_start(f_rg[par][i][:, :, :], rows(i)).then_inc(raw_g[par][i], 16)

            def load_d(s, par, down):
                sp.wait_ge(lo_d, s + 1)
                sp.dma_start(f_rd[par][:, :, :], down).then_inc(raw_d[par], 16)

            sp.wait_ge(pv_done, HEADS)
            def ffn_g(s):
                load_g(s, s % 2, lambda i: a["ffn_gu"][s % FFN_STEPS, i])

            ffn_g(0)
            for s in range(FFN_TOTAL):
                if s + 1 < FFN_TOTAL:
                    ffn_g(s + 1)
                load_d(s, s % 2, a["ffn_down"][s % FFN_STEPS])

            wq = a["swa_w_qkv"].rearrange("(k p) n -> p k n", p=P)
            for c in (0, 2, 1):
                if c == 0:
                    sp.wait_ge(lo_g, 2 * FFN_TOTAL + 2)
                else:
                    sp.wait_ge(gu_done, 2 * FFN_TOTAL + 2)
                for k in range(0, KD, 4):
                    sp.dma_start(s_w[c][:, k:k + 4, :], wq[:, k:k + 4, c * 512:(c + 1) * 512]).then_inc(ld_sw[c], 16)
            sp.wait_ge(out_free, 2)
            sp.dma_start(s_dist[:, :], a["distance"]).then_inc(ld_sc, 16)
            gain(s_snk[:, :], a["swa_sink"][0], ld_sc)
            wo = a["swa_w_o"].rearrange("(c r p) n -> p c r n", c=2, r=GRP)
            sp.wait_ge(xn_ready, 3 * NT)
            gain(GB[1][:, :], a["moe_norm"][0], gain_b)
            for c in range(2):
                sp.wait_ge(q_done, 4 * c + 4)
                sp.dma_start(s_wo[c][:, :, :], wo[:, c]).then_inc(ld_swo, 16)

            sp.wait_ge(q_done, 10)
            sp.dma_start(g_rt[:, :, :], a["moe_router"][0].rearrange("(k p) n -> p k n", p=P)).then_inc(ld_route, 16)
            sp.dma_start(g_c[:, :, :, :], a["route_consts"]).then_inc(ld_route, 16)
            sp.dma_start(g_sc[:, :], a["slot_consts"]).then_inc(ld_route, 16)
            for t in range(NT):
                sp.wait_ge(xn_ready, 3 * NT + t + 1)
                sp.dma_start(hn_d[t * P:(t + 1) * P, :], XG[t % 2][:, :]).then_inc(hn_st[t % 2], 16)

            sp.wait_ge(wo_add, 4 * NT)
            def expert_gu(e, f):
                return lambda i: a["moe_gu"][bass.ds(e, 1), f, i].rearrange("o p k f -> (o p) k f")

            def expert_down(e, f):
                return a["moe_down"][bass.ds(e, 1), f].rearrange("o p c n -> (o p) c n")

            def expert_loads(e, nxt, sfirst, few):
                for f in range(MOE_STEPS):
                    s = e * MOE_STEPS + (sfirst + f)

                    def loads():
                        if few:
                            sp.wait_ge(gu_done, s * 2 + 6)
                        over = f + 2 >= MOE_STEPS
                        load_g(s + 2, f % 2, expert_gu(nxt if over else e, (f + 2) % MOE_STEPS))

                    def loads_down():
                        if few or f == 0:
                            sp.wait_ge(down_done, s + 2)
                        over = f + 1 == MOE_STEPS
                        load_d(s + 1, (f + 1) % 2, expert_down(nxt if over else e, (f + 1) % MOE_STEPS))

                    if f + 1 < MOE_STEPS:
                        loads()
                        loads_down()
                    else:
                        with sp.If(e < NE - 1):
                            loads()
                            loads_down()

            def second_loads(s):
                sp.wait_ge(gu_done, s * 2 + 4)
                load_g(s + 1, 1, lambda i: a["moe_gu"][0, 1, i])
                sp.wait_ge(down_done, s + 1)
                load_d(s, 0, a["moe_down"][0, 0])

            def experts(sfirst, turn):
                second_loads(sfirst)
                if turn == 0:
                    sp.wait_ge(cnt_ready, 1)
                with sp.Fori(0, NE) as e:
                    nxt = sp.snap((e + 1) % NE, min_val=0, max_val=NE - 1)
                    if turn:
                        expert_loads(e, nxt, sfirst, False)
                    else:
                        n = sp.value_load(CNT[0:1, bass.ds(e, 1)], min_val=0, max_val=CAP)
                        by_count(sp, n, lambda kind: expert_loads(e, nxt, sfirst, kind == FEWER))

            load_g(S_MOE, 0, lambda i: a["moe_gu"][0, 0, i])
            experts(S_MOE, 0)
            most = sp.value_load(CNT[0:1, NE:NE + 1], min_val=0, max_val=CAP)
            with sp.If(most > 2 * P):
                experts(S_MOE + NE * MOE_STEPS, 1)

            sp.wait_ge(y_all, 1)
            yt = y_d.rearrange("(t p c) d -> t p c d", p=P, c=2)
            for t in range(2):
                sp.dma_start(y_rows[t][:, :, :], yt[t]).then_inc(y_ld[t], 16)
            gain(GB[0][:, :], a["final_norm"], ld_gain)
            for t in range(2, NT):
                sp.wait_ge(y_used, t - 1)
                sp.dma_start(y_rows[t % 2][:, :, :], yt[t]).then_inc(y_ld[t % 2], 16)
            ot = out.rearrange("b (t p) d -> (b t) p d", p=P)
            for t in range(NT):
                sp.wait_ge(fo_ready, t + 1)
                sp.dma_start(ot[t], y_out[t % 2][:, :]).then_inc(o_st[t % 2], 16)
            for i in range(2):
                sp.wait_ge(o_st[i], 16 * NT // 2)

        @block.tensor
        def _(pe):
            pe.sem_inc(gu_done, 4)
            pe.sem_inc(down_done, 2)
            pe.wait_ge(ld_id, 16)

            def x_transpose(norm, phase, t, banks):
                pe.wait_ge(xn_ready, NT * norm + t + 1)
                for hf in range(2):
                    i = 2 * t + hf
                    if i >= len(banks):
                        pe.wait_ge(xT_ev, 2 * NT * phase + i - len(banks) + 1)
                    for k in range(4):
                        c = 4 * hf + k
                        last = pe.transpose(PS[:, banks[i % len(banks)], k * P:(k + 1) * P],
                                            XG[t % 2][:, c * P:(c + 1) * P], IDN[:, :])
                    last.then_inc(xT_tr, 1)

            def passes(dst, xh, xl, wh, wl, start, stop):
                pe.matmul(dst, xh, wh, start=start, stop=False)
                pe.matmul(dst, xh, wl, start=False, stop=False)
                return pe.matmul(dst, xl, wh, start=False, stop=stop)

            x_transpose(0, 0, 0, WIDE)
            for t in range(NT):
                if t + 1 < NT:
                    x_transpose(0, 0, t + 1, WIDE)
                pe.wait_ge(xT_ev, 2 * t + 2)
                if t == 0:
                    pe.wait_ge(ld_wd, 64)
                if t >= 2:
                    pe.wait_ge(cn_ready, t - 1)
                for k in range(KD):
                    last = pe.matmul(PS[:, 4 + t % 2, :], m_xT[:, k, t * P:(t + 1) * P], m_wd[:, k, 0:QR + KVR],
                                     start=k == 0, stop=k == KD - 1)
                last.then_inc(dq_done, 1)
            pe.wait_ge(wkr_ready, 3)
            for k in range(KD):
                last = pe.matmul(PS[:, 6, :], m_wkr[:, k, :], m_xT[:, k, :], start=k == 0, stop=k == KD - 1)
            last.then_inc(kr_done, 1)
            for t in range(NT):
                pe.wait_ge(cn_ready, t + 1)
                if t:
                    pe.wait_ge(ct_ev, t)
                for c in range(4):
                    last = pe.transpose(PS[:, 7, c * P:(c + 1) * P], m_cn[:, t, c * P:(c + 1) * P], IDN[:, :])
                last.then_inc(ct_tr, 1)
            pe.wait_ge(ct_ev, NT)
            pe.wait_ge(ld_uv, 16)
            for i in range(2 * NT):
                t, n = i // 2, i % 2
                if i >= 4:
                    pe.wait_ge(v_ev, i - 3)
                for c in range(2):
                    last = pe.matmul(PS[:, i % 4, :], m_cT[:, 2 + c, t * P:(t + 1) * P],
                                     m_uv[:, c, n * 512:(n + 1) * 512], start=c == 0, stop=c == 1)
                last.then_inc(v_done, 1)

            def project(h):
                if h == 0:
                    pe.wait_ge(ld_uq, 16)
                    pe.wait_ge(ld_uk, 16)
                    pe.wait_ge(wqr_ready, 6)
                    pe.wait_ge(kr_ready, 1)
                else:
                    pe.wait_ge(pj_lo, 2 * h)
                    pe.wait_ge(qr_ready, h)
                for b, w, c0 in ((6, lambda c: m_wqr[:, c, h, :], 0), (4, lambda c: m_uq[:, c, h, 0:NOPE], 0),
                                 (5, lambda c: m_uk[:, c, h, :], 2)):
                    for c in range(2):
                        last = pe.matmul(PS[:, b, :], w(c), m_cT[:, c0 + c, :], start=c == 0, stop=c == 1)
                    last.then_inc(pj_done, 1)

            def scores(h):
                b = h % 2
                pe.wait_ge(pj_lo, 2 * h + 2)
                pe.wait_ge(qr_ready, h + 1)
                for qt in range(NT):
                    if h == 0:
                        pe.wait_ge(v_ev, 2 * NT)
                    else:
                        pe.wait_ge(pt_ev, NT * (h - 1) + qt + 1)
                    q = slice(qt * P, (qt + 1) * P)
                    passes(PS[:, qt, :], m_qn[b][:, q], m_qnl[b][:, q], m_kn[b][:, :], m_knl[b][:, :], True, False)
                    pe.matmul(PS[:, qt, :], m_qr[b][:, q], m_kr[:, :], start=False, stop=False)
                    pe.matmul(PS[:, qt, :], m_qr[b][0:ROPE, q], m_krl[:, :], start=False, stop=True)\
                        .then_inc(sc_done, 1)

            project(0)
            scores(0)
            for h in range(HEADS):
                b = h % 2
                if h + 1 < HEADS:
                    project(h + 1)
                for qt in range(NT):
                    pe.wait_ge(pn_ready, NT * h + qt + 1)
                    for c in range(NT):
                        last = pe.transpose(PS[:, qt, c * P:(c + 1) * P], m_p[b][:, qt, c * P:(c + 1) * P], IDN[:, :])
                    last.then_inc(tr_done, 1)
                if h + 1 < HEADS:
                    scores(h + 1)
                if h:
                    pe.wait_ge(o_ev, h)
                pe.wait_ge(pt_ev, NT * h + NT)
                for c in range(NT):
                    last = pe.matmul(PS[:, 7, :], m_v[:, c, h * P:(h + 1) * P], m_pT[b][:, c, :],
                                     start=c == 0, stop=c == NT - 1)
                last.then_inc(pv_done, 1)

            def out_projection(phase, oT, w, behind):
                for i in range(2 * NT):
                    t, n = i // 2, i % 2
                    if i >= 4:
                        pe.wait_ge(wo_add, 2 * NT * phase + i - 3)
                    for c in range(8):
                        last = pe.matmul(PS[:, i % 4, :], oT(c)[:, t * P:(t + 1) * P],
                                         w(c)[:, n * 512:(n + 1) * 512], start=c == 0, stop=c == 7)
                    last.then_inc(wo_done, 1)
                    if i % 2 and t:
                        behind(t - 1)
                behind(NT - 1)

            pe.wait_ge(o_ev, HEADS)
            pe.wait_ge(ld_mwo, 16)
            out_projection(0, lambda c: m_oT[:, c, :], lambda c: m_wo[:, c, :],
                           lambda t: None)

            def unit_x(t, banks=None):
                for hf in range(2):
                    for k in range(4):
                        c = 4 * hf + k
                        last = pe.transpose(PS[:, (banks or X_BANKS[t])[hf], k * P:(k + 1) * P],
                                            XG[t][:, c * P:(c + 1) * P], IDN[:, :])
                    last.then_inc(xu_tr[t], 1)

            def unit(u, s0, par0, n, kind, source, more, free, before_last, b_behind_a=False):
                nt, few = kind
                two = shares(kind, 2)
                four = shares(kind, 4)
                if nt == 2 or few:
                    source(1)
                    if b_behind_a:
                        pe.wait_ge(xlo_ev[0], u * 2 + 2)
                    unit_x(1)
                else:
                    pe.sem_inc(xu_tr[1], 2)

                def to_columns(s):
                    for t in range(nt):
                        pe.wait_ge(h_ready, s * 4 + (1 if few else (t + 1) * four[0]))
                        for c in range(2):
                            last = pe.transpose(PS[:, 6 + t, c * P:(c + 1) * P], f_h[t][:, c * P:(c + 1) * P],
                                                IDN[:, :])
                        last.then_inc(ht_tr, two[0])

                def few_to_columns(s):
                    pe.wait_ge(h_ready, s * 4 + 4)
                    for c in range(2):
                        last = pe.transpose(PS[:, 7, c * P:(c + 1) * P], f_h[1][:, c * P:(c + 1) * P], IDN[:, :])
                    last.then_inc(ht_tr, two[0])

                def down(s, par, first, final=False):
                    pe.wait_ge(lo_d, s + 3)
                    if first:
                        free()
                    for t in range(nt):
                        pe.wait_ge(htl_done, s * 2 + (t + 1) * two[0])
                        for n_ in range(2):
                            col = slice(n_ * 512, (n_ + 1) * 512)
                            for c in range(2):
                                last = passes(PS[:, 2 * t + n_, :], f_hh[:, t, c, :], f_hl[:, t, c, :],
                                              f_hd[par][:, c, col], f_ld[par][:, c, col],
                                              first and c == 0, final and c == 1)
                    if few:
                        pe.wait_ge(htl_done, s * 2 + 2)
                        for c in range(2):
                            for j in range(4):
                                last = pe.matmul(PS[FEW * j:FEW * (j + 1), 2, 0:FB], f_hbT[:, c, :],
                                                 f_rd[par][:, c, j * FB:(j + 1) * FB],
                                                 start=first and c == 0, stop=final and c == 1)
                    last.then_inc(down_done, 1)

                def step(s, par, which, nxt):
                    if which:
                        to_columns(s - 1)
                    pe.wait_ge(lo_g, s * 2 + 6)
                    for t in range(nt):
                        if which == 0:
                            pe.wait_ge(xlo_ev[t], u * 2 + 2)
                        tok = slice(t * P, (t + 1) * P)
                        for g in range(2):
                            col = slice(g * FB, (g + 1) * FB)
                            for k in range(KD):
                                last = passes(PS[:, 4 + t, col], f_xh[:, k, tok], f_xl[:, k, tok],
                                              f_hg[par][:, k, col], f_lg[par][:, k, col], k == 0, k == KD - 1)
                        last.then_inc(gu_done, two[0])
                    if few:
                        if which:
                            few_to_columns(s - 1)
                        else:
                            pe.wait_ge(xlo_ev[1], u * 2 + 2)
                        for k in range(4):
                            for j in range(4):
                                g, hf = j // 2, j % 2
                                last = pe.matmul(PS[FEW * j:FEW * (j + 1), 5, 0:FB], f_xb[:, 4 * hf + k, :],
                                                 f_rg[par][hf][:, k, g * FB:(g + 1) * FB],
                                                 start=k == 0, stop=k == 3)
                        last.then_inc(gu_done, 1)
                    if which:
                        down(s - 1, 1 - par, which == 1)

                steps(pe, s0, par0, n, step, more)
                to_columns(s0 + (n - 1))
                if few:
                    few_to_columns(s0 + (n - 1))
                before_last()
                down(s0 + (n - 1), (par0 + n - 1) % 2, False, True)

            def ffn_x():
                pe.wait_ge(xn_ready, NT + 3)
                unit_x(0)

            pe.wait_ge(xn_ready, NT + 1)
            unit_x(0, (6, 7))
            for u in range(2):
                def source(t, u=u):
                    pe.wait_ge(xn_ready, NT + 2 * u + t + 1)

                def free(u=u):
                    if u:
                        pe.wait_ge(out_free, u)

                unit(u, u * FFN_STEPS, u * FFN_STEPS % 2, FFN_STEPS, TWO, source, u == 0, free,
                     (lambda: x_transpose(2, 1, 0, (4, 5, 6, 7))) if u else ffn_x, u == 0)

            def swa_v(t):
                pe.wait_ge(xT_ev, 2 * NT + 2 * max(t, 1) + 2)
                if t >= 2:
                    pe.wait_ge(sv_ev, t - 1)
                for k in range(KD):
                    last = pe.matmul(PS[:, 6 + t % 2, 0:KVH * HD], s_xT[:, k, t * P:(t + 1) * P],
                                     s_w[2][:, k, KVH * HD:2 * KVH * HD], start=k == 0, stop=k == KD - 1)
                last.then_inc(sv_done, 1)

            x_transpose(2, 1, 1, (4, 5, 6, 7))
            pe.wait_ge(ld_sw[2], 32)
            for t in range(2):
                swa_v(t)
            for t in range(2, NT):
                x_transpose(2, 1, t, (4, 5))
            for t in range(2, NT):
                swa_v(t)
            for i in range(10):
                if i % 4 == 0 and i < 8:
                    pe.wait_ge(ld_sw[i // 4], 32)
                if i >= 4:
                    pe.wait_ge(q_ev, i - 3)
                for k in range(KD):
                    last = pe.matmul(PS[:, i % 4, :], s_w[i // 4][:, k, i % 4 * P:(i % 4 + 1) * P], s_xT[:, k, :],
                                     start=k == 0, stop=k == KD - 1)
                last.then_inc(q_done, 1)

            def swa_scores(i):
                g, t = i // NT, i % NT
                half, c = g % 2, g // 2
                rows = slice(half * HD, half * HD + HD)
                lo, hi = max(0, t - 1) * P, min(NT, t + 2) * P
                if i == 0:
                    pe.wait_ge(q_ev, 10)
                else:
                    pe.wait_ge(st_ready, i)
                for r_ in range(GRP):
                    last = pe.matmul(PS[:, r_, 0:hi - lo], s_q[rows, c, r_, t * P:(t + 1) * P],
                                     s_k[rows, c, lo:hi], start=True, stop=True)
                last.then_inc(ss_done, 1)

            def swa_keys(i):
                return [kt for kt in (i % NT - 1, i % NT, i % NT + 1) if 0 <= kt < NT]

            def swa_values(i):
                g = i // NT
                half, keys = g % 2, swa_keys(i)
                pe.wait_ge(spt_ev, i + 1)
                if i:
                    pe.wait_ge(so_ev, i)
                for j, kt in enumerate(keys):
                    last = pe.matmul(PS[half * HD:half * HD + HD, 7, :], s_v[:, kt, g * HD:(g + 1) * HD],
                                     s_pT[i % 2][:, j, :, :].rearrange("p r q -> p (r q)"),
                                     start=j == 0, stop=j == len(keys) - 1)
                last.then_inc(spv_done, 1)

            swa_scores(0)
            swa_scores(1)
            for i in range(16):
                if i + 2 < 16:
                    swa_scores(i + 2)
                pe.wait_ge(sp_ready, i + 1)
                if i == 0:
                    pe.wait_ge(sv_ev, NT)
                else:
                    pe.wait_ge(spt_ev, i)
                for j in range(len(swa_keys(i))):
                    for r_ in range(GRP):
                        last = pe.transpose(PS[:, 4 + j, r_ * P:(r_ + 1) * P],
                                            s_p[i % 2][:, r_, j * P:(j + 1) * P], IDN[:, :])
                last.then_inc(st_tr, 1)
                if i:
                    swa_values(i - 1)
            swa_values(15)
            pe.wait_ge(so_ev, 16)
            pe.wait_ge(ld_swo, 32)

            def logits(t):
                pe.wait_ge(xT_ev, 4 * NT + 2 * t + 2)
                for k in range(KD):
                    last = pe.matmul(PS[:, 0, t * NE:(t + 1) * NE], g_xT[:, k, t * P:(t + 1) * P], g_rt[:, k, :],
                                     start=k == 0, stop=k == KD - 1)
                return last

            def moe_x(t):
                if t == NT - 1:
                    pe.wait_ge(ld_route, 80)
                    pe.wait_ge(wo_add, 2 * NT + 6)
                    for t2 in range(t):
                        logits(t2)
                x_transpose(3, 2, t, (6, 7))

            out_projection(1, lambda c: s_o[:, c // GRP, c % GRP, :], lambda c: s_wo[c // GRP][:, c % GRP, :],
                           moe_x)

            logits(NT - 1).then_inc(lg_done, 1)
            pe.wait_ge(m_ready, 1)
            pe.matmul(PS[:, 5, 0:(NT + 1) * NE], TRI[:, :], g_m[:, :], start=True, stop=False)
            for back in range(1, NT + 1):
                last = pe.matmul(PS[:, 5, back * NE:(NT + 1) * NE], ONES[:, :], g_m[:, 0:(NT + 1 - back) * NE],
                                 start=False, stop=back == NT)
            last.then_inc(rk_done, 1)
            for i in range(2 * NT):
                pe.wait_ge(hot_ready, i + 1)
                last = pe.matmul(PS[:, 4, 0:NE * NT], g_at[:, i, :], g_val[:, i, :], start=i == 0,
                                 stop=i == 2 * NT - 1)
            last.then_inc(list_done, 1)

            pe.wait_ge(cnt_ready, 1)

            def expert(e, turn, kind):
                def source(t):
                    pe.wait_ge(xg_ready[t], e * 16 + 16 * (NE * turn + 1))

                def free():
                    pe.wait_ge(yo_ready, e * 2 + (2 * NE * turn + 2))

                def next_x():
                    pe.wait_ge(xg_ready[0], e * 16 + 16 * (NE * turn + 2))
                    unit_x(0)

                unit(e + (U_MOE + NE * turn), e * MOE_STEPS + (S_MOE + turn * NE * MOE_STEPS), 0, MOE_STEPS, kind,
                     source, True, free, next_x)

            pe.wait_ge(xg_ready[0], 16)
            unit_x(0)
            with pe.Fori(0, NE) as e:
                n = pe.value_load(CNT[0:1, bass.ds(e, 1)], min_val=0, max_val=CAP)
                by_count(pe, n, lambda kind: expert(e, 0, kind))
            most = pe.value_load(CNT[0:1, NE:NE + 1], min_val=0, max_val=CAP)
            with pe.If(most > 2 * P):
                with pe.Fori(0, NE) as e:
                    expert(e, 1, TWO)

        @block.scalar
        def _(act):
            def copy(dst, src):
                return act.activation(dst, src, ACT.Copy)

            def std(norm, t):
                act.wait_ge(ss_ready, NT * norm + t + 1)
                act.activation(SD[:, t:t + 1], SS[:, t:t + 1], ACT.Sqrt, bias=EPSC[:, :]).then_inc(std_ready, 1)

            def x_evict(phase, xT, t, banks):
                for hf in range(2):
                    act.wait_ge(xT_tr, 2 * NT * phase + 2 * t + hf + 1)
                    copy(xT[:, 4 * hf:4 * hf + 4, t * P:(t + 1) * P],
                         PS[:, banks[(2 * t + hf) % len(banks)], :].rearrange("p (k q) -> p k q", k=4)).then_inc(xT_ev, 1)

            def stds_and_x(norm, phase, xT, banks):
                for t in range(NT):
                    std(norm, t)
                    if t:
                        x_evict(phase, xT, t - 1, banks)
                x_evict(phase, xT, NT - 1, banks)

            act.wait_ge(eps_set, 1)

            def c_std(t):
                act.wait_ge(dq_done, t + 1)
                for i in range(2):
                    act.activation(m_junk[:, i, :], PS[:, 4 + t % 2, i * QR:(i + 1) * QR], ACT.Square,
                                   accum_out=m_sq[:, 2 * t + i:2 * t + i + 1]).then_inc(sq_done, 1)
                act.wait_ge(sq_done, 2 * t + 2)
                act.activation(m_sd[:, 2 * t:2 * t + 2], m_sq[:, 2 * t:2 * t + 2], ACT.Sqrt, scale=1.0 / QR,
                               bias=EPSC[:, :]).then_inc(cstd, 1)

            for t in range(NT):
                std(0, t)
                x_evict(0, m_xT, t, WIDE)
                if t >= 2:
                    c_std(t - 2)
            for t in range(NT - 2, NT):
                c_std(t)
            for t in range(NT):
                act.wait_ge(ct_tr, t + 1)
                copy(m_cT[:, :, t * P:(t + 1) * P],
                     PS[:, 7, :].rearrange("p (c q) -> p c q", c=4)).then_inc(ct_ev, 1)
            act.wait_ge(ks_ready, 1)
            for half in range(2):
                copy(m_kr[half * ROPE:(half + 1) * ROPE, :], m_t1[:, :]).then_inc(kh_ready, 1)
            for i in range(2 * NT):
                act.wait_ge(v_done, i + 1)
                copy(m_v[:, i // 2, (i % 2) * 512:(i % 2 + 1) * 512], PS[:, i % 4, :]).then_inc(v_ev, 1)

            def project_evict(h):
                if h >= 2:
                    act.wait_ge(sc_done, NT * (h - 1))
                act.wait_ge(pj_done, 3 * h + 2)
                copy(m_qn[h % 2][:, :], PS[:, 4, :]).then_inc(pj_ev, 1)
                act.wait_ge(pj_done, 3 * h + 3)
                copy(m_kn[h % 2][:, :], PS[:, 5, :]).then_inc(pj_ev, 1)
                act.wait_ge(qs_ready, h + 1)
                copy(m_qr[h % 2][0:ROPE, :], m_t1[:, :]).then_inc(qh_ready, 1)

            def o_evict(h):
                act.wait_ge(pv_done, h + 1)
                copy(m_oT[:, h, :], PS[:, 7, :]).then_inc(o_ev, 1)

            project_evict(0)
            for h in range(HEADS):
                b = h % 2
                for qt in range(NT):
                    i = NT * h + qt
                    act.wait_ge(nm_ready, i + 1)
                    if h >= 2:
                        act.wait_ge(tr_done, i - 2 * NT + 1)
                    act.activation(m_p[b][:, qt, :], PS[:, qt, :], ACT.Exp, bias=m_nm[:, i:i + 1], scale=MLA_SCALE,
                                   accum_out=m_sm[:, i:i + 1]).then_inc(ex_done, 1)
                if h:
                    o_evict(h - 1)
                if h + 1 < HEADS:
                    project_evict(h + 1)
                for qt in range(NT):
                    act.wait_ge(tr_done, NT * h + qt + 1)
                    if h >= 2:
                        act.wait_ge(pv_done, h - 1)
                    copy(m_pT[b][:, :, qt * P:(qt + 1) * P],
                         PS[:, qt, :].rearrange("p (c q) -> p c q", c=NT)).then_inc(pt_ev, 1)
            o_evict(HEADS - 1)

            def hi_gu(s, par):
                for i in range(2):
                    act.wait_ge(raw_g[par][i], s * 8 + (16 - 8 * par))
                    act.wait_ge(gu_done, s * 2 + 2)
                    copy(f_hg[par][:, 4 * i:4 * i + 2, :], f_rg[par][i][:, 0:2, :])
                    copy(f_hg[par][:, 4 * i + 2:4 * i + 4, :], f_rg[par][i][:, 2:4, :]).then_inc(hi_g, 1)

            def unit_x_high(u, t, banks=None):
                for hf in range(2):
                    act.wait_ge(xu_tr[t], u * 2 + (hf + 1))
                    copy(f_xh[:, 4 * hf:4 * hf + 4, t * P:(t + 1) * P],
                         PS[:, (banks or X_BANKS[t])[hf], :].rearrange("p (k q) -> p k q", k=4))\
                        .then_inc(xhi_ev[t], 1)

            def unit(u, s0, par0, n, kind, more, before_last, behind_x=None):
                nt, few = kind
                two, four = shares(kind, 2), shares(kind, 4)
                if nt == 2:
                    unit_x_high(u, 1)
                else:
                    act.sem_inc(xhi_ev[1], 2)
                if behind_x:
                    behind_x()

                def hidden_T(s):
                    for t in range(nt):
                        act.wait_ge(ht_tr, s * 2 + (t + 1) * two[0])
                        copy(f_hh[:, t, :, :], PS[:, 6 + t, 0:2 * P].rearrange("p (c q) -> p c q", c=2))\
                            .then_inc(hth_done, 2 if few else two[0])

                def step(s, par, which, nxt):
                    if which:
                        hidden_T(s - 1)
                    if nxt:
                        hi_gu(s + 1, 1 - par)
                    for t in range(nt):
                        act.wait_ge(gu_done, s * 2 + (4 + (t + 1) * two[0]))
                        act.activation(f_sg[t][:, :], PS[:, 4 + t, 0:FB], ACT.Silu)\
                            .then_inc(sg_done, 1 if few else four[0])
                    if few:
                        act.wait_ge(gu_done, s * 2 + 6)
                        copy(f_cb[0:FEW, :], PS[FEW:2 * FEW, 5, 0:FB])
                        copy(f_cb[2 * FEW:3 * FEW, :], PS[3 * FEW:P, 5, 0:FB]).then_inc(sg_done, 1)
                    act.wait_ge(raw_d[par], s * 8 + (16 - 8 * par))
                    act.wait_ge(down_done, s + 1)
                    copy(f_hd[par][:, 0, :], f_rd[par][:, 0, :])
                    if few:
                        act.wait_ge(h_ready, s * 4 + 2)
                        act.activation(f_sb, f_gb[:, 0:FB], ACT.Silu).then_inc(sg_done, 2)
                    copy(f_hd[par][:, 1, :], f_rd[par][:, 1, :]).then_inc(hi_d, 1)

                steps(act, s0, par0, n, step, more)
                hidden_T(s0 + (n - 1))
                before_last()

            hi_gu(0, 0)
            for t in range(NT):
                std(1, t)
            unit_x_high(0, 0, (6, 7))
            for u in range(2):
                unit(u, u * FFN_STEPS, u * FFN_STEPS % 2, FFN_STEPS, TWO, u == 0,
                     (lambda: x_evict(1, s_xT, 0, (4, 5, 6, 7))) if u else lambda: unit_x_high(1, 0),
                     (lambda: [std(2, t) for t in range(2)]) if u else None)

            def swa_v_evict(t):
                act.wait_ge(sv_done, t + 1)
                copy(s_v[:, t, :], PS[:, 6 + t % 2, 0:KVH * HD]).then_inc(sv_ev, 1)

            x_evict(1, s_xT, 1, (4, 5, 6, 7))
            for t in range(2, NT):
                std(2, t)
            for t in range(2):
                swa_v_evict(t)
            for t in range(2, NT):
                x_evict(1, s_xT, t, (4, 5))
            for t in range(2, NT):
                swa_v_evict(t)
            for i in range(10):
                act.wait_ge(q_done, i + 1)
                dst = s_q[:, i // GRP, i % GRP, :] if i < 8 else s_k[:, i - 8, :]
                copy(dst, PS[:, i % 4, :]).then_inc(q_ev, 1)

            def swa_probs(i):
                t = i % NT
                w = (min(NT, t + 2) - max(0, t - 1)) * P
                act.wait_ge(sm_ready, i + 1)
                if i >= 2:
                    act.wait_ge(st_tr, i - 1)
                for r_ in range(GRP):
                    act.activation(s_p[i % 2][:, r_, 0:w], s_s[i % 2][:, r_, 0:w], ACT.Exp, scale=SWA_SCALE,
                                   bias=s_nm[:, GRP * i + r_:GRP * i + r_ + 1],
                                   accum_out=s_sm[:, GRP * i + r_:GRP * i + r_ + 1])
                c = slice(GRP * i, GRP * i + GRP)
                act.activation(s_es[:, c], s_es[:, c], ACT.Exp, scale=SWA_SCALE).then_inc(se_done, 1)

            def swa_o_evict(i):
                t, half, c = i % NT, (i // NT) % 2, i // NT // 2
                act.wait_ge(spv_done, i + 1)
                rows = slice(half * HD, half * HD + HD)
                copy(s_o[rows, c, :, t * P:(t + 1) * P],
                     PS[rows, 7, :].rearrange("p (r q) -> p r q", r=GRP)).then_inc(so_ev, 1)

            swa_probs(0)
            swa_probs(1)
            for i in range(16):
                t = i % NT
                nk = min(NT, t + 2) - max(0, t - 1)
                act.wait_ge(st_tr, i + 1)
                if i >= 2:
                    act.wait_ge(spv_done, i - 1)
                for j in range(nk):
                    last = copy(s_pT[i % 2][:, j, :, :], PS[:, 4 + j, :].rearrange("p (r q) -> p r q", r=GRP))
                last.then_inc(spt_ev, 1)
                if i + 2 < 16:
                    swa_probs(i + 2)
                if i:
                    swa_o_evict(i - 1)
            swa_o_evict(15)

            stds_and_x(3, 2, g_xT, (6, 7))
            act.wait_ge(d_ready, 1)
            act.activation(g_e[:, :], g_d[:, :], ACT.Exp).then_inc(e_ready, 1)
            hi_gu(S_MOE, 0)
            act.wait_ge(cnt_ready, 1)

            def expert(e, turn, kind):
                u = e + (U_MOE + NE * turn)
                s0 = e * MOE_STEPS + (S_MOE + turn * NE * MOE_STEPS)
                unit(u, s0, 0, MOE_STEPS, kind, True, lambda: unit_x_high(u + 1, 0))
                act.wait_ge(down_done, s0 + (MOE_STEPS + 2))
                nt, few = kind
                act.wait_ge(y_free, e + (NE * turn + 1))
                for t in range(nt):
                    for n_ in range(2):
                        last = copy(GB[1 - t][:, n_ * 512:(n_ + 1) * 512], PS[:, 2 * t + n_, :])
                    last.then_inc(yo_ready, shares(kind, 2)[0])
                if few:
                    for j in range(4):
                        last = copy(GB[0][0:FEW, j * FB:(j + 1) * FB], PS[FEW * j:FEW * (j + 1), 2, 0:FB])
                    last.then_inc(yo_ready, 1)

            act.sem_inc(yo_ready, 2)
            unit_x_high(U_MOE, 0)
            with act.Fori(0, NE) as e:
                n = act.value_load(CNT[0:1, bass.ds(e, 1)], min_val=0, max_val=CAP)
                by_count(act, n, lambda kind: expert(e, 0, kind))
            most = act.value_load(CNT[0:1, NE:NE + 1], min_val=0, max_val=CAP)
            with act.If(most > 2 * P):
                with act.Fori(0, NE) as e:
                    expert(e, 1, TWO)
            for t in range(NT):
                std(4, t)

        @block.vector
        def _(dve):
            dve.sem_inc(lo_g, 4)
            dve.sem_inc(lo_d, 2)
            count = [0]

            def link(ins):
                count[0] += 1
                ins.then_inc(chain, 1)
                dve.wait_ge(chain, count[0])

            tt, ts, stt = dve.tensor_tensor, dve.tensor_scalar, dve.scalar_tensor_tensor

            def mean_square(t, squares=None):
                if squares is None:
                    squares = PS[:, 4:6, :].rearrange("p b n -> p (b n)")
                dve.tensor_tensor_reduce(out=squares, in0=H[:, t, :], in1=H[:, t, :],
                                         scale=1.0 / D, scalar=0.0, op0=ALU.mult, op1=ALU.add,
                                         accum_out=SS[:, t:t + 1]).then_inc(ss_ready, 1)

            def rstd(norm, t):
                dve.wait_ge(std_ready, NT * norm + t + 1)
                link(dve.reciprocal(RS[:, t:t + 1], SD[:, t:t + 1]))

            def rows(t, gain_, dst=None):
                return stt((dst or XG[t % 2])[:, :], H[:, t, :], RS[:, t:t + 1], gain_[:, :], ALU.mult, ALU.mult)

            def lo_part(dst, src, hi):
                return tt(dst, src, hi.bitcast(F32), ALU.subtract)

            dve.memset(EPSC[:, :], EPS).then_inc(eps_set, 1)
            for t in range(NT):
                dve.wait_ge(ld_h[t], 16)
                if t:
                    dve.wait_ge(ss_ready, t)
                mean_square(t, PS[:, 6:8, :].rearrange("p b n -> p (b n)"))
                if t == 0:
                    dve.wait_ge(ld_gain, 16)
                rstd(0, t)
                if t >= 2:
                    dve.wait_ge(xT_tr, 2 * (t - 1))
                rows(t, GB[0]).then_inc(xn_ready, 1)
            dve.wait_ge(ld_tab, 48)
            for t in range(NT):
                dve.wait_ge(cstd, t + 1)
                link(dve.reciprocal(m_rq[:, 2 * t:2 * t + 2], m_sd[:, 2 * t:2 * t + 2]))
                for i in range(2):
                    c = slice(i * QR, (i + 1) * QR)
                    ins = stt(m_cn[:, t, c], PS[:, 4 + t % 2, c], m_rq[:, 2 * t + i:2 * t + i + 1], m_gq[:, c],
                              ALU.mult, ALU.mult)
                ins.then_inc(cn_ready, 1)

            def rope():
                tt(m_t1[:, :], PS[0:ROPE, 6, :], m_tab[0:ROPE, :], ALU.mult)
                link(tt(m_t2[:, :], PS[ROPE:P, 6, :], m_tab[ROPE:P, :], ALU.mult))
                return tt(m_t1[:, :], m_t1[:, :], m_t2[:, :], ALU.add)

            dve.wait_ge(kr_done, 1)
            rope().then_inc(ks_ready, 1)
            dve.wait_ge(kh_ready, 2)
            lo_part(m_krl[:, :], m_t1[:, :], m_kr[0:ROPE, :]).then_inc(kr_ready, 1)

            def rope_head(h):
                dve.wait_ge(pj_done, 3 * h + 1)
                if h >= 2:
                    dve.wait_ge(sc_done, NT * (h - 1))
                if h:
                    dve.wait_ge(qr_ready, h)
                else:
                    dve.wait_ge(kr_ready, 1)
                rope().then_inc(qs_ready, 1)
                for i, (hi, lo) in enumerate(((m_qn, m_qnl), (m_kn, m_knl))):
                    dve.wait_ge(pj_ev, 2 * h + i + 1)
                    lo_part(lo[h % 2][:, :], PS[:, 4 + i, :], hi[h % 2][:, :]).then_inc(pj_lo, 1)
                dve.wait_ge(qh_ready, h + 1)
                lo_part(m_qr[h % 2][ROPE:P, :], m_t1[:, :], m_qr[h % 2][0:ROPE, :]).then_inc(qr_ready, 1)

            def normalise(h, qt):
                i = NT * h + qt
                dve.wait_ge(ex_done, i + 1)
                link(dve.reciprocal(m_rc[:, i:i + 1], m_sm[:, i:i + 1]))
                ts(m_p[h % 2][:, qt, :], m_p[h % 2][:, qt, :], m_rc[:, i:i + 1], None, ALU.mult).then_inc(pn_ready, 1)

            rope_head(0)
            for h in range(HEADS):
                for qt in range(NT):
                    i = NT * h + qt
                    dve.wait_ge(sc_done, i + 1)
                    link(dve.reduce_max(m_mx[:, i:i + 1], PS[:, qt, :], AXX))
                    ts(m_nm[:, i:i + 1], m_mx[:, i:i + 1], -MLA_SCALE, None, ALU.mult).then_inc(nm_ready, 1)
                    if qt:
                        normalise(h, qt - 1)
                normalise(h, NT - 1)
                if h + 1 < HEADS:
                    rope_head(h + 1)

            def add_projection(phase, norm, then):
                for t in range(NT):
                    for n_ in range(2):
                        i, c = 2 * t + n_, slice(n_ * 512, (n_ + 1) * 512)
                        dve.wait_ge(wo_done, 2 * NT * phase + i + 1)
                        tt(H[:, t, c], H[:, t, c], PS[:, i % 4, :], ALU.add).then_inc(wo_add, 1)
                    dve.wait_ge(wo_add, 2 * NT * phase + 2 * t + 2)
                    if t:
                        dve.wait_ge(ss_ready, NT * norm + t)
                    mean_square(t)
                    rstd(norm, t)
                    then(t)

            def lo_gu(s, par):
                for i in range(2):
                    dve.wait_ge(hi_g, s * 2 + (i + 1))
                    for j in range(2):
                        k = slice(4 * i + 2 * j, 4 * i + 2 * j + 2)
                        last = lo_part(f_lg[par][:, k, :], f_rg[par][i][:, 2 * j:2 * j + 2, :], f_hg[par][:, k, :])
                    last.then_inc(lo_g, 1)

            def unit_x_low(u, t, banks=None):
                for hf in range(2):
                    dve.wait_ge(xhi_ev[t], u * 2 + (hf + 1))
                    k, tok = slice(4 * hf, 4 * hf + 4), slice(t * P, (t + 1) * P)
                    lo_part(f_xl[:, k, tok], PS[:, (banks or X_BANKS[t])[hf], :].rearrange("p (k q) -> p k q", k=4),
                            f_xh[:, k, tok]).then_inc(xlo_ev[t], 1)

            def unit(u, s0, par0, n, kind, more, before_last, behind_x=None):
                nt, few = kind
                two, four = shares(kind, 2), shares(kind, 4)
                if nt == 2:
                    unit_x_low(u, 1)
                elif few:
                    dve.wait_ge(xu_tr[1], u * 2 + 2)
                    for hf in range(2):
                        dve.tensor_copy(f_xb[:, 4 * hf:4 * hf + 4, :],
                                        PS[:, 6 + hf, :].rearrange("p (k q) -> p k q", k=4)[:, :, 0:FEW])\
                            .then_inc(xlo_ev[1], 1)
                else:
                    dve.sem_inc(xlo_ev[1], 2)
                if behind_x:
                    behind_x()

                def hidden_T(s):
                    for t in range(nt):
                        dve.wait_ge(hth_done, s * 2 + (t + 1) * two[0])
                        lo_part(f_hl[:, t, :, :], PS[:, 6 + t, 0:2 * P].rearrange("p (c q) -> p c q", c=2),
                                f_hh[:, t, :, :]).then_inc(htl_done, two[0])

                def few_hidden_T(s):
                    dve.wait_ge(ht_tr, s * 2 + 2)
                    dve.tensor_copy(f_hbT[:, :, :], PS[:, 7, 0:2 * P].rearrange("p (c q) -> p c q", c=2)[:, :, 0:FEW])\
                        .then_inc(htl_done, 1)

                def step(s, par, which, nxt):
                    if which:
                        hidden_T(s - 1)
                    if nxt:
                        lo_gu(s + 1, 1 - par)
                    if few and which:
                        few_hidden_T(s - 1)
                    for t in range(nt):
                        dve.wait_ge(sg_done, s * 4 + (1 if few else (t + 1) * four[0]))
                        tt(f_h[t][:, :], f_sg[t][:, :], PS[:, 4 + t, FB:2 * FB], ALU.mult)\
                            .then_inc(h_ready, 1 if few else four[0])
                    if few:
                        dve.wait_ge(sg_done, s * 4 + 2)
                        tt(f_gb[:, 0:FB], PS[0:FEW, 5, 0:FB], f_cb[0:FEW, :], ALU.add)
                        tt(f_gb[:, FB:2 * FB], PS[2 * FEW:3 * FEW, 5, 0:FB], f_cb[2 * FEW:3 * FEW, :], ALU.add)\
                            .then_inc(h_ready, 1)
                    dve.wait_ge(hi_d, s + 1)
                    lo_part(f_ld[par][:, 0, :], f_rd[par][:, 0, :], f_hd[par][:, 0, :])
                    if few:
                        dve.wait_ge(sg_done, s * 4 + 4)
                        tt(f_hb, f_sb, f_gb[:, FB:2 * FB], ALU.mult).then_inc(h_ready, 2)
                    lo_part(f_ld[par][:, 1, :], f_rd[par][:, 1, :], f_hd[par][:, 1, :]).then_inc(lo_d, 1)

                steps(dve, s0, par0, n, step, more)
                hidden_T(s0 + (n - 1))
                if few:
                    few_hidden_T(s0 + (n - 1))
                before_last()

            lo_gu(0, 0)
            dve.wait_ge(gain_b, 16)

            def ffn_rows(t):
                rows(t, GB[1]).then_inc(xn_ready, 1)

            def swa_rows(t):
                rstd(2, t)
                if t >= 2:
                    dve.wait_ge(xT_tr, 2 * NT + 2 * (t - 1))
                rows(t, GB[0]).then_inc(xn_ready, 1)

            def swa_square(t):
                if t:
                    dve.wait_ge(ss_ready, NT * 2 + t)
                mean_square(t, GB[1][:, :])

            def swa_rows_early():
                dve.wait_ge(out_free, 1)
                dve.wait_ge(xu_tr[1], 4)
                dve.wait_ge(ld_gain, 32)
                for t in range(2):
                    swa_square(t)
                for t in range(2):
                    swa_rows(t)

            add_projection(0, 1, lambda t: ffn_rows(t) if t < 2 else None)

            def ffn_rows_late():
                for t in range(2):
                    dve.wait_ge(xu_tr[t], 2)
                    ffn_rows(2 + t)

            unit_x_low(0, 0, (6, 7))
            for u in range(2):
                unit(u, u * FFN_STEPS, u * FFN_STEPS % 2, FFN_STEPS, TWO, u == 0,
                     (lambda: None) if u else lambda: unit_x_low(1, 0), swa_rows_early if u else ffn_rows_late)
                dve.wait_ge(down_done, 2 + (u + 1) * FFN_STEPS)
                for t in range(2 * u, 2 * u + 2):
                    for n_ in range(2):
                        c = slice(n_ * 512, (n_ + 1) * 512)
                        ins = tt(H[:, t, c], H[:, t, c], PS[:, 2 * (t - 2 * u) + n_, :], ALU.add)
                    if t % 2:
                        ins.then_inc(out_free, 1)
                    elif u:
                        link(ins)
                        swa_square(t)

            dve.wait_ge(out_free, 2)
            swa_square(NT - 1)
            for t in range(2, NT):
                swa_rows(t)
            dve.wait_ge(ld_sc, 32)
            link(ts(s_sk8[:, :], s_snk[:, :], SCALE8, None, ALU.mult))

            def swa_logits(i):
                g, t = i // NT, i % NT
                w = (min(NT, t + 2) - max(0, t - 1)) * P
                off = P if t == 0 else 0
                b, c = i % 2, slice(GRP * i, GRP * i + GRP)
                dve.wait_ge(ss_done, i + 1)
                if i >= 2:
                    dve.wait_ge(se_done, i - 1)
                for r_ in range(GRP):
                    slope = 2.0 ** (-8.0 * (GRP * g + r_ + 1) / QH)
                    last = stt(s_s[b][:, r_, 0:w], s_dist[:, off:off + w], -SCALE8 * slope, PS[:, r_, 0:w],
                               ALU.mult, ALU.add)
                last.then_inc(st_ready, 1)
                dve.wait_ge(st_ready, i + 1)
                link(dve.reduce_max(s_rc[:, c], s_s[b][:, :, 0:w], AXX))
                link(tt(s_mx[:, c], s_rc[:, c], s_sk8[:, GRP * g:GRP * g + GRP], ALU.max))
                ts(s_nm[:, c], s_mx[:, c], -SWA_SCALE, None, ALU.mult)
                tt(s_es[:, c], s_sk8[:, GRP * g:GRP * g + GRP], s_mx[:, c], ALU.subtract).then_inc(sm_ready, 1)

            def swa_normalise(i):
                t = i % NT
                w = (min(NT, t + 2) - max(0, t - 1)) * P
                c = slice(GRP * i, GRP * i + GRP)
                dve.wait_ge(se_done, i + 1)
                link(tt(s_mx[:, c], s_sm[:, c], s_es[:, c], ALU.add))
                link(dve.reciprocal(s_rc[:, c], s_mx[:, c]))
                for r_ in range(GRP):
                    last = ts(s_p[i % 2][:, r_, 0:w], s_p[i % 2][:, r_, 0:w], s_rc[:, GRP * i + r_:GRP * i + r_ + 1],
                              None, ALU.mult)
                last.then_inc(sp_ready, 1)

            swa_logits(0)
            swa_logits(1)
            for i in range(16):
                swa_normalise(i)
                if i + 2 < 16:
                    swa_logits(i + 2)
            dve.wait_ge(gain_b, 32)

            def moe_rows(t):
                if t >= 2:
                    dve.wait_ge(xT_tr, 4 * NT + 2 * (t - 1))
                    dve.wait_ge(hn_st[t % 2], 16)
                rows(t, GB[1]).then_inc(xn_ready, 1)

            add_projection(1, 3, moe_rows)

            dve.wait_ge(ld_route, 80)
            dve.memset(g_m[:, NT * NE:], 0.0)
            wide = lambda x: x[:, :].unsqueeze(2).to_broadcast((P, NT, NE))
            rev, at_list = (g_c[:, i, :, :] for i in range(2))
            slot_row, list_column, choice_value = g_sc[:, 0:P], g_sc[:, P:P + NE * NT], g_sc[:, P + NE * NT:]
            dve.wait_ge(lg_done, 1)
            link(dve.tensor_copy(g_lg[:, :, :], PS[:, 0, 0:NT * NE].rearrange("p (t e) -> p t e", t=NT)))

            def pick(lg, m, eq, w, first, oh):
                link(dve.reduce_max(m[:, :], lg[:, :, :], AXX))
                link(tt(eq[:, :, :], lg[:, :, :], wide(m), ALU.is_equal))
                link(tt(w[:, :, :], eq[:, :, :], rev, ALU.mult))
                link(dve.reduce_max(first[:, :], w[:, :, :], AXX))
                link(tt(oh[:, :, :], rev, wide(first), ALU.is_equal))

            pick(g_lg, g_m1, g_eq, g_w1, g_i1, g_o1)
            link(stt(g_l2[:, :, :], g_o1[:, :, :], -3e38, g_lg[:, :, :], ALU.mult, ALU.add))
            pick(g_l2, g_m2, g_eq, g_w2, g_i2, g_o2)
            tt(g_m[:, 0:NT * NE].rearrange("p (t e) -> p t e", t=NT), g_o1[:, :, :], g_o2[:, :, :], ALU.add).then_inc(m_ready, 1)
            tt(g_d[:, :], g_m2[:, :], g_m1[:, :], ALU.subtract).then_inc(d_ready, 1)
            dve.wait_ge(e_ready, 1)
            link(ts(g_s1[:, :], g_e[:, :], 1.0, None, ALU.add))
            link(dve.reciprocal(G12[:, 0:NT], g_s1[:, :]))
            link(tt(G12[:, NT:2 * NT], g_e[:, :], G12[:, 0:NT], ALU.mult))
            dve.wait_ge(rk_done, 1)
            link(dve.tensor_copy(g_cf[:, 0:NE], PS[:, 5, NT * NE:NT * NE + NE]))
            link(dve.reduce_max(g_cf[:, NE:NE + 1], g_cf[:, 0:NE], AXX))
            dve.tensor_copy(CNT[:, :], g_cf[:, :]).then_inc(cnt_ready, 1)
            link(dve.tensor_copy(g_rk[:, :, :], PS[:, 5, 0:NT * NE].rearrange("p (t e) -> p t e", t=NT)))
            link(ts(g_j[:, :, :], g_rk[:, :, :], float(P), None, ALU.is_ge))
            link(stt(g_j2[:, :, :], g_rk[:, :, :], float(2 * P), g_j[:, :, :], ALU.is_ge, ALU.add))
            link(stt(g_tile[:, :, :], g_rk[:, :, :], float(3 * P), g_j2[:, :, :], ALU.is_ge, ALU.add))
            tt(g_list[:, :, :], g_tile[:, :, :], at_list, ALU.add)
            link(stt(g_part[:, :, :], g_tile[:, :, :], float(-P), g_rk[:, :, :], ALU.mult, ALU.add))
            for i, x in enumerate((g_part, g_list)):
                for c in range(2):
                    ins = tt(g_pr[i][:, c * NT:(c + 1) * NT, :], g_oh[:, c, :, :], x[:, :, :], ALU.mult)
            link(ins)
            for i in range(2):
                ins = dve.reduce_sum(g_sel[i][:, :], g_pr[i][:, :, :], AXX)
            link(ins)
            for i in range(2 * NT):
                ts(g_at[:, i, :], slot_row, g_sel[0][:, i:i + 1], None, ALU.is_equal)
                ts(g_val[:, i, :], list_column, g_sel[1][:, i:i + 1], choice_value[:, i:i + 1], ALU.is_equal, ALU.mult)\
                    .then_inc(hot_ready, 1)
            dve.wait_ge(list_done, 1)
            link(ts(g_lf[:, :], PS[:, 4, 0:NE * NT], float(2 * S), None, ALU.add))
            link(dve.tensor_copy(LST[:, :], g_lf[:, :]))
            link(ts(LSM[:, :], LST[:, :], 2 * S - 1, None, ALU.min))
            ts(LSG[:, :], LSM[:, :], 1, None, ALU.arith_shift_right).then_inc(lsg_ready, 1)

            unit_x_low(U_MOE, 0)
            lo_gu(S_MOE, 0)

            def expert(e, turn, kind):
                u = e + (U_MOE + NE * turn)
                unit(u, e * MOE_STEPS + (S_MOE + turn * NE * MOE_STEPS), 0, MOE_STEPS, kind, True,
                     lambda: unit_x_low(u + 1, 0))

            with dve.Fori(0, NE) as e:
                n = dve.value_load(CNT[0:1, bass.ds(e, 1)], min_val=0, max_val=CAP)
                by_count(dve, n, lambda kind: expert(e, 0, kind))
            most = dve.value_load(CNT[0:1, NE:NE + 1], min_val=0, max_val=CAP)
            with dve.If(most > 2 * P):
                with dve.Fori(0, NE) as e:
                    expert(e, 1, TWO)

            def final_rows(t):
                rstd(4, t)
                if t == 0:
                    dve.wait_ge(ld_gain, 48)
                if t >= 2:
                    dve.wait_ge(o_st[t % 2], 16)
                rows(t, GB[0], y_out[t % 2]).then_inc(fo_ready, 1)

            for t in range(NT):
                dve.wait_ge(y_ld[t % 2], 16 * (t // 2 + 1))
                for c in range(2):
                    ins = stt(H[:, t, :], y_rows[t % 2][:, c, :], G12[:, c * NT + t:c * NT + t + 1], H[:, t, :],
                              ALU.mult, ALU.add)
                    if c == 0:
                        link(ins)
                ins.then_inc(y_used, 1)
                dve.wait_ge(y_used, t + 1)
                if t:
                    dve.wait_ge(ss_ready, NT * 4 + t)
                mean_square(t)
                if t:
                    final_rows(t - 1)
            final_rows(NT - 1)

        @block.gpsimd
        def _(pool):
            def with_swapped(dst, src, s):
                h_ = ROPE // 2
                pool.tensor_copy(dst[..., 0:ROPE], src).then_inc(s, 1)
                pool.tensor_copy(dst[..., ROPE:ROPE + h_], src[..., h_:ROPE]).then_inc(s, 1)
                pool.tensor_copy(dst[..., ROPE + h_:P], src[..., 0:h_]).then_inc(s, 1)

            pool.wait_ge(ld_wd, 64)
            with_swapped(m_wkr[:, :, :], m_wd[:, :, QR + KVR:DOWN], wkr_ready)
            pool.wait_ge(ld_uq, 16)
            for c in range(2):
                with_swapped(m_wqr[:, c, :, :], m_uq[:, c, :, NOPE:QK], wqr_ready)

            offset = lambda ap: bass.IndirectOffsetOnAxis(ap=ap, axis=0)
            pool.wait_ge(lsg_ready, 1)
            for i in range(2):
                pool.wait_ge(hn_st[i], 16 * NT // 2)

            def gather(k, t):
                e, turn = k % NE, min(k // NE, 1)
                pool.wait_ge(xu_tr[t], 2 * (U_MOE + k))
                if k:
                    pool.wait_ge(xg_ready[t], 16 * k)
                j = NT * e + 2 * turn + t
                pool.indirect_dma_start(out=XG[t][:, :], out_offset=None, in_=hn_d,
                                        in_offset=offset(LSG[:, j:j + 1])).then_inc(xg_ready[t], 16)

            def scatter(k):
                e, turn = k % NE, k // NE
                pool.wait_ge(yo_ready, 2 * k + 4)
                for t in range(2):
                    j = NT * e + 2 * turn + t
                    pool.indirect_dma_start(out=y_d, out_offset=offset(LST[:, j:j + 1]), in_=GB[1 - t][:, :],
                                            in_offset=None, bounds_check=2 * S - 1, oob_is_err=False)\
                        .then_inc(y_st[t], 16)
                for t in range(2):
                    pool.wait_ge(y_st[t], 16 * (k + 1))
                pool.sem_inc(y_free, 1)

            def experts(turn):
                if turn == 0:
                    gather(0, 0)
                gather(NE * turn, 1)
                for k in range(NE * turn, NE * turn + NE):
                    gather(k + 1, 0)
                    if (k + 1) % NE:
                        gather(k + 1, 1)
                    scatter(k)

            pool.sem_inc(y_free, 1)
            experts(0)
            most = pool.value_load(CNT[0:1, NE:NE + 1], min_val=0, max_val=CAP)
            with pool.If(most > 2 * P):
                experts(1)
            pool.sem_inc(y_all, 1)


def constants():
    inv = (1.0 / (np.float32(10000.0) ** (np.arange(0, ROPE, 2, dtype=np.float32) / np.float32(ROPE)))).astype(np.float32)
    ang = (np.arange(S, dtype=np.float32)[:, None] * inv[None, :]).astype(np.float32)
    cos, sin = np.cos(ang).T, np.sin(ang).T
    j = np.arange(SPAN) - WIN
    dist = np.abs(np.arange(P)[:, None] - j[None, :]).astype(np.float32)
    e = np.arange(NE, dtype=np.float32)
    route = np.stack([NE - e, NT * e])[None, :, None, :]
    choice = (np.arange(P)[:, None, None] + P * np.arange(NT)) * 2 + np.arange(2)[:, None] - 2 * S
    numbers = np.broadcast_to(np.concatenate([np.arange(P), np.arange(NE * NT)]), (P, P + NE * NT))
    return {
        "slot_consts": np.concatenate([numbers, choice.reshape(P, 2 * NT)], 1).astype(np.float32),
        "identity": np.eye(P, dtype=np.float32),
        "earlier": np.triu(np.ones((P, P), np.float32), 1),
        "ones": np.ones((P, P), np.float32),
        "rope_table": np.concatenate([cos, cos, -sin, sin]).astype(np.float32),
        "distance": np.where(dist <= WIN, dist, np.float32(1e30)).astype(np.float32),
        "route_consts": np.broadcast_to(route, (P, 2, NT, NE)).astype(np.float32).copy(),
    }


def laid_out(inputs):
    rest = ["x", "mla_norm", "mla_w_dqkv", "mla_q_norm", "mla_w_uq", "mla_kv_norm", "mla_w_uk", "mla_w_uv", "mla_w_o",
            "swa_norm", "swa_sink", "ffn_norm", "moe_norm", "moe_router", "final_norm"]
    got = {n: np.asarray(inputs[n]) for n in rest}

    def gate_up(gate, up, blocks):
        both = np.stack([np.asarray(gate), np.asarray(up)], -2)
        n = both.shape[0]
        x = both.reshape(n, 2, KD // 2, P, 2, blocks, FB)
        return x.transpose(0, 5, 1, 3, 2, 4, 6).reshape(n, blocks, 2, P, KD // 2, 2 * FB)

    def down(w, blocks):
        w = np.asarray(w)
        return w.reshape(w.shape[0], blocks, 2, P, D).transpose(0, 1, 3, 2, 4)

    got["ffn_gu"] = gate_up(inputs["ffn_w_gate"], inputs["ffn_w_up"], FFN_STEPS)[0]
    got["ffn_down"] = down(inputs["ffn_w_down"], FFN_STEPS)[0]
    got["moe_gu"] = gate_up(inputs["moe_w_gate"][0], inputs["moe_w_up"][0], MOE_STEPS)
    got["moe_down"] = down(inputs["moe_w_down"][0], MOE_STEPS)
    w = np.asarray(inputs["swa_w_qkv"])[0]
    q = w[:, :QH * HD].reshape(D, 2, 2, GRP, HD).transpose(0, 1, 3, 2, 4).reshape(D, QH * HD)
    got["swa_w_qkv"] = np.concatenate([q, w[:, QH * HD:]], 1)
    wo = np.asarray(inputs["swa_w_o"])[0]
    got["swa_w_o"] = wo.reshape(2, 2, GRP, HD, D).transpose(0, 2, 1, 3, 4).reshape(QH * HD, D)
    return {n: np.ascontiguousarray(x) for n, x in got.items()}


def kernel(**inputs):
    import concourse.bacc as bacc
    from concourse.bass_utils import run_bass_kernel_spmd

    nc = bacc.Bacc("TRN2", target_bir_lowering=False, num_devices=1)
    arrays, args = {}, {}
    for name, x in {**laid_out(inputs), **constants()}.items():
        arrays[f"in_{name}"] = x
        args[name] = nc.dram_tensor(f"in_{name}", x.shape, mybir.dt.from_np(x.dtype), kind="ExternalInput").ap()
    out = nc.dram_tensor("out", (1, S, D), F32, kind="ExternalOutput").ap()
    build_trunk(nc, args, out)
    r = run_bass_kernel_spmd(nc, [arrays], core_ids=[0])
    return r.results[0]["out"]
```

```python
from contextlib import ExitStack

import numpy as np

import concourse.bass as bass
from concourse import mybir

F32 = mybir.dt.float32
F32R = mybir.dt.float32r
I32 = mybir.dt.int32
ALU = mybir.AluOpType
ACT = mybir.ActivationFunctionType
AXX = mybir.AxisListType.X

P = 128
S = 512
D = 1024
NT = S // P
KD = D // P
EPS = 1e-6

QR = 256
KVR = 256
NOPE = 128
ROPE = 64
HEADS = 8
QK = NOPE + ROPE
DOWN = QR + KVR + ROPE
MLA_SCALE = QK ** -0.5

KVH = 4
GRP = 4
HD = 64
QH = KVH * GRP
SCALE8 = 8.0
SWA_SCALE = HD ** -0.5
WIN = 128
SPAN = 3 * P

FFN = 2816
NE = 8
ED = 2048
FB = 256
FEW = 32
FFN_STEPS = FFN // FB
MOE_STEPS = ED // FB
FFN_TOTAL = 2 * FFN_STEPS
CAP = S

BASE = 16640


def build_trunk(nc, a, out):
    hn_d = nc.dram_tensor("hn_rows", [S, D], F32, kind="Internal").ap()
    y_d = nc.dram_tensor("expert_rows", [2 * S, D], F32, kind="Internal").ap()

    def at(name, shape, offset, dt=F32):
        return nc.alloc_sbuf_tensor_at(name, shape, dt, offset=offset)

    class Region:

        def __init__(self, start, end):
            self.at, self.end = start, end

        def __call__(self, name, shape, dt=F32):
            size = int(np.prod(shape[1:])) * 4
            x = at(name, shape, self.at, dt)
            self.at += (size + 31) // 32 * 32
            assert self.at <= self.end, (name, self.at, self.end)
            return x

    fixed = Region(BASE, 229344)
    H = fixed("H", [P, NT, D])
    GB = [fixed("gain_a", [P, D]), fixed("gain_b", [P, D])]
    XG = [fixed("rows_a", [P, D]), fixed("rows_b", [P, D])]
    IDN = fixed("identity", [P, P])
    TRI = fixed("earlier", [P, P])
    ONES = fixed("ones", [P, P])
    small = lambda n, w, dt=F32: fixed(n, [P, w], dt)
    SS, SD, RS = small("mean_square", NT), small("std", NT), small("rstd", NT)
    EPSC = small("eps", 1)
    f_one = small("table_load", 1)
    CNT = small("counts", NE + 1, I32)
    LST = small("slot_tokens", NE * NT, I32)
    LSM = small("slot_rows", NE * NT, I32)
    LSG = small("slot_gather", NE * NT, I32)
    G12 = small("gates", 2 * NT)
    AREA = fixed.at

    r = Region(AREA, 229344)
    m_xT = r("mla_xT", [P, KD, S])
    m_wd = r("w_dqkv", [P, KD, DOWN])
    m_wkr = r("w_krope", [P, KD, P])
    m_wo = at("mla_wo", [P, HEADS, D], AREA)
    m_pT = [at("probsT0", [P, NT, S], r.at)]
    m_cn = r("c_norm", [P, NT, QR + KVR])
    m_cT = r("c_T", [P, NT, S])
    m_uq = r("w_uq", [P, 2, HEADS, QK])
    m_uk = r("w_uk", [P, 2, HEADS, NOPE])
    m_pT.append(at("probsT1", [P, NT, S], r.at))
    m_uv = r("w_uv", [P, 2, HEADS * P])
    m_wqr = r("w_qrope", [P, 2, HEADS, P])
    m_v = r("mla_v", [P, NT, HEADS * P])
    m_qn = [r(f"q_nope{i}", [P, S], F32R) for i in range(2)]
    m_kn = [r(f"k_nope{i}", [P, S], F32R) for i in range(2)]
    m_qr = [r(f"q_rope{i}", [2 * ROPE, S], F32R) for i in range(2)]
    m_kr = r("k_rope", [2 * ROPE, S], F32R)
    m_t1, m_t2 = r("rope_t1", [ROPE, S]), r("rope_t2", [ROPE, S])
    m_p = [r(f"probs{i}", [P, NT, S]) for i in range(2)]
    m_oT = r("mla_oT", [P, HEADS, S])
    m_tab = r("rope_table", [P, S])
    m_gq = r("gain_qkv", [P, QR + KVR])
    m_sq, m_sd, m_rq = r("c_sq", [P, 2 * NT]), r("c_sd", [P, 2 * NT]), r("c_rstd", [P, 2 * NT])
    m_junk = r("c_junk", [P, 2, QR])
    m_mx, m_nm = r("row_max", [P, HEADS * NT]), r("neg_max", [P, HEADS * NT])
    m_sm, m_rc = r("row_sum", [P, HEADS * NT]), r("row_rcp", [P, HEADS * NT])

    m_qnl = [r(f"q_nope_lo{i}", [P, S], F32R) for i in range(2)]
    m_knl = [r(f"k_nope_lo{i}", [P, S], F32R) for i in range(2)]
    m_krl = r("k_rope_lo", [ROPE, S], F32R)

    r = Region(AREA, 229344)
    f_xh = r("xT_hi", [P, KD, 2 * P], F32R)
    f_xl = r("xT_lo", [P, KD, 2 * P], F32R)
    f_sg = [r(f"silu{i}", [P, FB]) for i in range(2)]
    f_h = [r(f"hidden{i}", [P, FB]) for i in range(2)]
    f_hh = r("hT_hi", [P, 2, 2, P], F32R)
    f_hl = r("hT_lo", [P, 2, 2, P], F32R)
    f_ld = [r("lo_down1", [P, 2, D], F32R)]
    RAW = r.at
    ROUTED = AREA + 4 * KD * S + 2048
    f_rg = [[r(f"raw_gu{i}{j}", [P, 4, 2 * FB]) for j in range(2)] for i in range(2)]
    f_rd = [r(f"raw_down{i}", [P, 2, D]) for i in range(2)]
    f_hg = [r(f"hi_gu{i}", [P, KD, 2 * FB], F32R) for i in range(2)]
    f_lg = [r(f"lo_gu{i}", [P, KD, 2 * FB], F32R) for i in range(2)]
    f_hd = [r(f"hi_down{i}", [P, 2, D], F32R) for i in range(2)]
    f_ld.insert(0, r("lo_down0", [P, 2, D], F32R))
    f_xb = r("xT_few", [P, KD, FEW])
    f_cb = r("gu_few_half", [P, FB])
    f_gb = r("gu_few", [FEW, 2 * FB])
    f_sb, f_hb = f_sg[1][0:FEW, :], f_h[1][0:FEW, :]
    f_hbT = r("hT_few", [P, 2, FEW])

    PLACE = 8192
    s_xT = at("swa_xT_hi", [P, KD, S], AREA, F32R)
    s_xl = at("swa_xT_lo", [P, KD, S], RAW + 4 * PLACE, F32R)
    PARTS = (RAW, RAW + 6 * PLACE, RAW + 10 * PLACE)
    assert 4 * KD * 512 == 2 * PLACE
    s_w = [at(f"w_qkv{i}", [P, KD, 512], o) for i, o in enumerate(PARTS)]
    s_wl = [at(f"w_qkv_lo{i}", [P, KD, 512], o, F32R) for i, o in enumerate(PARTS)]
    s_wh = [at(f"w_qkv_hi{i}", [P, KD, 512], RAW + o * PLACE, F32R) for i, o in enumerate((12, 8, 2))]
    s_wo = [at(f"swa_wo{c}", [P, GRP, D], PARTS[c]) for c in range(2)]
    s_wol = [at(f"swa_wo_lo{c}", [P, GRP, D], PARTS[c], F32R) for c in range(2)]
    s_woh = [at(f"swa_wo_hi{c}", [P, GRP, D], o, F32R) for c, o in
             enumerate((RAW + 8 * PLACE + 5 * 4 * GRP * SPAN, RAW + 14 * PLACE))]
    s_q = [at(f"swa_qT{c}", [P, 2, GRP, S], RAW + o * PLACE, F32R) for c, o in enumerate((14, 2))]
    r = Region(ROUTED, RAW)
    s_s = [r("swa_scores0", [P, GRP, SPAN])]
    s_kh = r("swa_kT_hi", [P, KVH, S], F32R)
    s_squares = at("squares", [P, D], RAW + 2 * PLACE)
    s_o = at("swa_oT_hi", [P, 2, GRP, S], RAW + 4 * PLACE, F32R)
    s_or = at("swa_oT", [P, 2, GRP, S], AREA)
    s_ol = at("swa_oT_lo", [P, 2, GRP, S], AREA, F32R)
    r = Region(RAW + 8 * PLACE, RAW + 14 * PLACE)
    s_p = [r(f"swa_probs{i}", [P, GRP, SPAN]) for i in range(2)]
    s_pT = [r(f"swa_probsT{i}", [P, 3, GRP, P]) for i in range(2)]
    s_s.append(r("swa_scores1", [P, GRP, SPAN]))
    r = Region(RAW + 16 * PLACE, 229344)
    s_kl = r("swa_kT_lo", [P, 2, S], F32R)
    s_v = r("swa_v", [P, NT, KVH * HD])
    s_dist = r("distance", [P, SPAN])
    s_snk, s_sk8 = r("sink", [P, QH]), r("sink8", [P, QH])
    s_mx, s_nm = r("swa_max", [P, 16 * GRP]), r("swa_neg", [P, 16 * GRP])
    s_es, s_sm = r("swa_esink", [P, 16 * GRP]), r("swa_sum", [P, 16 * GRP])
    s_rc = r("swa_rcp", [P, 16 * GRP])

    g_xT = at("moe_xT", [P, KD, S], RAW + 8 * PLACE)
    r = Region(AREA + 4 * KD * S, RAW)
    g_rt = r("router", [P, KD, NE])
    g_c = r("route_consts", [P, 2, NT, NE])
    rt = lambda n, k=NE: r(n, [P, NT, k])
    g_sc = r("slot_consts", [P, P + NE * NT + 2 * NT])
    assert r.at <= ROUTED
    g_lg, g_eq, g_w1, g_l2, g_w2 = (rt(n) for n in ("lg", "eq", "w1", "l2", "w2"))
    g_oh = r("choices", [P, 2, NT, NE])
    g_o1, g_o2 = g_oh[:, 0, :, :], g_oh[:, 1, :, :]
    g_m = r("chosen", [P, (NT + 1) * NE])
    g_rk, g_j, g_j2 = (rt(n) for n in ("rank", "j1", "j2"))
    g_tile, g_part, g_list = (rt(n) for n in ("slot_tile", "slot_partition", "list_column"))
    g_m1, g_i1, g_m2, g_i2, g_d, g_e, g_s1 = (r(n, [P, NT]) for n in ("m1", "i1", "m2", "i2", "d21", "e2", "s1"))
    g_pr = [r(f"pick{c}", [P, 2 * NT, NE]) for c in range(2)]
    g_sel = [r(f"picked{c}", [P, 2 * NT]) for c in range(2)]
    g_at = r("slot_rows_hot", [P, 2 * NT, P])
    g_val = r("slot_values", [P, 2 * NT, NE * NT])
    g_lf = r("list_f", [P, NE * NT])
    g_cf = r("counts_f", [P, NE + 1])

    r = Region(RAW + 14 * 8192, 229344)
    y_rows = [r(f"y{i}", [P, 2, D]) for i in range(NT - 1)]
    y_rows.append(at(f"y{NT - 1}", [P, 2, D], RAW - 4 * 2 * D))

    ctx = ExitStack()
    with ctx:
        PS = ctx.enter_context(nc.psum_tensor("PS", [P, 8, 512], F32))
        sem = lambda n: ctx.enter_context(nc.semaphore(n))
        ld_h = [sem(f"ld_h{t}") for t in range(NT)]
        ld_wd = [sem(f"ld_wd{i}") for i in range(KD // 2)]
        ld_id, ld_gain, ld_tab, ld_uq, ld_uk, ld_uv, ld_mwo = (
            sem(n) for n in ("ld_id", "ld_gain", "ld_tab", "ld_uq", "ld_uk", "ld_uv", "ld_mwo"))
        ld_sw = [sem(f"ld_sw{c}") for c in range(3)]
        ld_swo = [sem(f"ld_swo{c}") for c in range(2)]
        ld_sc, ld_route = (sem(n) for n in ("ld_sc", "ld_route"))
        swo_hi, swo_lo, so_lo = sem("swo_hi"), sem("swo_lo"), sem("so_lo")
        gain_b = sem("gain_b_loaded")
        chain = sem("dve_chain")
        ss_ready, std_ready, xn_ready, xT_tr, xT_ev = (
            sem(n) for n in ("ss_ready", "std_ready", "xn_ready", "xT_tr", "xT_ev"))
        eps_set, wkr_ready, wqr_ready = sem("eps_set"), sem("wkr_ready"), sem("wqr_ready")
        dq_done, sq_done, cstd, cn_ready, ct_tr, ct_ev, kr_done, kr_ready = (
            sem(n) for n in ("dq_done", "sq_done", "cstd", "cn_ready", "ct_tr", "ct_ev", "kr_done", "kr_ready"))
        pj_lo, qs_ready, qh_ready, ks_ready, kh_ready = (
            sem(n) for n in ("pj_lo", "qs_ready", "qh_ready", "ks_ready", "kh_ready"))
        v_done, v_ev, pj_done, pj_ev, qr_ready, sc_done, nm_ready, ex_done = (
            sem(n) for n in ("v_done", "v_ev", "pj_done", "pj_ev", "qr_ready", "sc_done", "nm_ready", "ex_done"))
        pn_ready, tr_done, pt_ev, pv_done, o_ev, wo_done, wo_add = (
            sem(n) for n in ("pn_ready", "tr_done", "pt_ev", "pv_done", "o_ev", "wo_done", "wo_add"))
        raw_g = [[sem(f"raw_g{i}{j}") for j in range(2)] for i in range(2)]
        raw_d = [sem(f"raw_d{i}") for i in range(2)]
        hi_g, hi_d, lo_g, lo_d = (sem(n) for n in ("hi_g", "hi_d", "lo_g", "lo_d"))
        xu_tr, xhi_ev, xlo_ev = ([sem(f"{n}{t}") for t in range(2)] for n in ("xu_tr", "xhi_ev", "xlo_ev"))
        gu_done, sg_done, h_ready, ht_tr, hth_done, htl_done, down_done, out_free = (
            sem(n) for n in ("gu_done", "sg_done", "h_ready", "ht_tr",
                             "hth_done", "htl_done", "down_done", "out_free"))
        q_done, q_ev, sv_done, sv_ev, ss_done, st_ready, sm_ready, se_done, sp_ready, st_tr, spt_ev, spv_done, so_ev = (
            sem(n) for n in ("q_done", "q_ev", "sv_done", "sv_ev", "ss_done", "st_ready", "sm_ready", "se_done",
                             "sp_ready", "st_tr", "spt_ev", "spv_done", "so_ev"))
        sx_lo, sw_hi, sw_lo, q_lo = sem("sx_lo"), sem("sw_hi"), sem("sw_lo"), sem("q_lo")
        hn_st = [sem(f"hn_st{i}") for i in range(2)]
        lg_done, d_ready, e_ready, m_ready, rk_done, cnt_ready, hot_ready, list_done = (
            sem(n) for n in ("lg_done", "d_ready", "e_ready", "m_ready", "rk_done", "cnt_ready", "hot_ready",
                             "list_done"))
        xg_ready = [sem(f"xg_ready{i}") for i in range(2)]
        yo_ready, y_free, y_all, lsg_ready = sem("yo_ready"), sem("y_free"), sem("y_all"), sem("lsg_ready")
        y_st = [sem(f"y_st{i}") for i in range(2)]
        y_ld = [sem(f"y_ld{t}") for t in range(NT)]
        y_used, fo_ready = sem("y_used"), sem("fo_ready")
        o_st = sem("o_st")
        block = ctx.enter_context(nc.Block())

        WIDE = (0, 1, 2, 3)
        X_BANKS = ((4, 5), (6, 7))
        WO_FROM = 4
        HALVES = (slice(0, HD), slice(HD, P))
        QK_CHUNKS = (8, 9, 0, 1, 2, 3, 4, 5, 6, 7)

        U_MOE, S_MOE = 2, FFN_TOTAL

        ONE, TWO, FEWER = (1, False), (2, False), (1, True)

        def shares(kind, k):
            nt, few = kind
            return (k,) if nt == 1 and not few else (k // 2, k // 2)

        def steps(eng, s0, par0, n, step, more):
            assert more or n % 2
            step(s0, par0, 0, True)
            step(s0 + 1, 1 - par0, 1, True)
            with eng.Fori(0, (n - 2) // 2) as j:
                step(s0 + (j * 2 + 2), par0, 2, True)
                step(s0 + (j * 2 + 3), 1 - par0, 2, True)
            if n % 2:
                step(s0 + (n - 1), par0, 2, more)

        def rows_out(eng, copy, e, turn, kind, half):
            nt, few = kind
            eng.wait_ge(down_done, e * MOE_STEPS + (S_MOE + turn * NE * MOE_STEPS + MOE_STEPS + 2))
            eng.wait_ge(y_free, e + (NE * turn + 1))
            for t in range(nt):
                last = copy(GB[1 - t][:, half * 512:(half + 1) * 512], PS[:, 2 * t + half, :])
            if few:
                for j in (2 * half, 2 * half + 1):
                    last = copy(GB[0][0:FEW, j * FB:(j + 1) * FB], PS[FEW * j:FEW * (j + 1), 2, 0:FB])
            last.then_inc(yo_ready, 1)

        def by_count(eng, n, body):
            with eng.If(n > P + FEW):
                body(TWO)
            with eng.Else():
                with eng.If(n > P):
                    body(FEWER)
                with eng.Else():
                    body(ONE)

        @block.sync
        def _(sp):
            def gain(dst, src, s):
                sp.dma_start(dst, src.partition_broadcast(P)).then_inc(s, 16)

            xt = a["x"].rearrange("b (t p) d -> (b t) p d", p=P)
            wd = a["mla_w_dqkv"][0].rearrange("(k p) n -> p k n", p=P)
            for t in range(NT):
                sp.dma_start(H[:, t, :], xt[t]).then_inc(ld_h[t], 16)
                if t == 0:
                    sp.dma_start(IDN[:, :], a["identity"]).then_inc(ld_id, 16)
                    gain(GB[0][:, :], a["mla_norm"][0], ld_gain)
                if t == 1:
                    for k in range(0, KD, 2):
                        sp.dma_start(m_wd[:, k:k + 2, :], wd[:, k:k + 2, :]).then_inc(ld_wd[k // 2], 16)
            sp.dma_start(m_tab[:, :], a["rope_table"]).then_inc(ld_tab, 16)
            gain(m_gq[:, 0:QR], a["mla_q_norm"][0], ld_tab)
            gain(m_gq[:, QR:QR + KVR], a["mla_kv_norm"][0], ld_tab)
            sp.dma_start(m_uv[:, :, :], a["mla_w_uv"][0].rearrange("(c p) h d -> p c (h d)", p=P)).then_inc(ld_uv, 16)
            sp.dma_start(m_uq[:, :, :, :], a["mla_w_uq"][0].rearrange("(c p) h d -> p c h d", p=P)).then_inc(ld_uq, 16)
            sp.dma_start(m_uk[:, :, :, :], a["mla_w_uk"][0].rearrange("(c p) h d -> p c h d", p=P)).then_inc(ld_uk, 16)
            gain(GB[1][:, :], a["ffn_norm"][0], gain_b)
            sp.dma_start(TRI[:, :], a["earlier"]).then_inc(ld_route, 16)
            sp.dma_start(ONES[:, :], a["ones"]).then_inc(ld_route, 16)
            sp.wait_ge(dq_done, NT)
            sp.wait_ge(kr_done, 1)
            sp.wait_ge(wqr_ready, 6)
            sp.dma_start(m_wo[:, :, :], a["mla_w_o"][0].rearrange("(h p) n -> p h n", p=P)).then_inc(ld_mwo, 16)
            sp.wait_ge(xn_ready, NT)
            gain(GB[0][:, :], a["swa_norm"][0], ld_gain)

            def load_g(s, par, rows):
                for i in range(2):
                    sp.wait_ge(lo_g, s * 2 + (i + 1))
                    sp.dma_start(f_rg[par][i][:, :, :], rows(i)).then_inc(raw_g[par][i], 16)

            def load_d(s, par, down):
                sp.wait_ge(lo_d, s + 1)
                sp.dma_start(f_rd[par][:, :, :], down).then_inc(raw_d[par], 16)

            sp.wait_ge(pv_done, HEADS)
            def ffn_g(s):
                load_g(s, s % 2, lambda i: a["ffn_gu"][s % FFN_STEPS, i])

            ffn_g(0)
            for s in range(FFN_TOTAL):
                if s + 1 < FFN_TOTAL:
                    ffn_g(s + 1)
                load_d(s, s % 2, a["ffn_down"][s % FFN_STEPS])

            wq = a["swa_w_qkv"].rearrange("(k p) n -> p k n", p=P)
            for c in (0, 2, 1):
                if c == 0:
                    sp.wait_ge(lo_g, 2 * FFN_TOTAL + 2)
                else:
                    sp.wait_ge(gu_done, 2 * FFN_TOTAL + 2)
                for k in range(0, KD, 4):
                    sp.dma_start(s_w[c][:, k:k + 4, :], wq[:, k:k + 4, c * 512:(c + 1) * 512]).then_inc(ld_sw[c], 16)
            sp.wait_ge(out_free, 2)
            sp.dma_start(s_dist[:, :], a["distance"]).then_inc(ld_sc, 16)
            gain(s_snk[:, :], a["swa_sink"][0], ld_sc)
            wo = a["swa_w_o"].rearrange("(c r p) n -> p c r n", c=2, r=GRP)
            sp.wait_ge(xn_ready, 3 * NT)
            gain(GB[1][:, :], a["moe_norm"][0], gain_b)
            for c in range(2):
                sp.wait_ge(q_done, 4 * c + 6)
                sp.dma_start(s_wo[c][:, :, :], wo[:, c]).then_inc(ld_swo[c], 16)

            sp.wait_ge(q_done, 10)
            sp.dma_start(g_rt[:, :, :], a["moe_router"][0].rearrange("(k p) n -> p k n", p=P)).then_inc(ld_route, 16)
            sp.dma_start(g_c[:, :, :, :], a["route_consts"]).then_inc(ld_route, 16)
            sp.dma_start(g_sc[:, :], a["slot_consts"]).then_inc(ld_route, 16)
            for t in range(NT):
                sp.wait_ge(xn_ready, 3 * NT + t + 1)
                sp.dma_start(hn_d[t * P:(t + 1) * P, :], XG[t % 2][:, :]).then_inc(hn_st[t % 2], 16)

            sp.wait_ge(wo_add, 4 * NT)
            def expert_gu(e, f):
                return lambda i: a["moe_gu"][bass.ds(e, 1), f, i].rearrange("o p k f -> (o p) k f")

            def expert_down(e, f):
                return a["moe_down"][bass.ds(e, 1), f].rearrange("o p c n -> (o p) c n")

            def expert_loads(e, nxt, sfirst, few):
                for f in range(MOE_STEPS):
                    s = e * MOE_STEPS + (sfirst + f)

                    def loads():
                        if few:
                            sp.wait_ge(gu_done, s * 2 + 6)
                        over = f + 2 >= MOE_STEPS
                        load_g(s + 2, f % 2, expert_gu(nxt if over else e, (f + 2) % MOE_STEPS))

                    def loads_down():
                        if few or f == 0:
                            sp.wait_ge(down_done, s + 2)
                        over = f + 1 == MOE_STEPS
                        load_d(s + 1, (f + 1) % 2, expert_down(nxt if over else e, (f + 1) % MOE_STEPS))

                    if f + 1 < MOE_STEPS:
                        loads()
                        loads_down()
                    else:
                        with sp.If(e < NE - 1):
                            loads()
                            loads_down()

            def second_loads(s):
                sp.wait_ge(gu_done, s * 2 + 4)
                load_g(s + 1, 1, lambda i: a["moe_gu"][0, 1, i])
                sp.wait_ge(down_done, s + 1)
                load_d(s, 0, a["moe_down"][0, 0])

            def experts(sfirst, turn):
                second_loads(sfirst)
                if turn == 0:
                    sp.wait_ge(cnt_ready, 1)
                with sp.Fori(0, NE) as e:
                    nxt = sp.snap((e + 1) % NE, min_val=0, max_val=NE - 1)
                    if turn:
                        expert_loads(e, nxt, sfirst, False)
                    else:
                        n = sp.value_load(CNT[0:1, bass.ds(e, 1)], min_val=0, max_val=CAP)
                        by_count(sp, n, lambda kind: expert_loads(e, nxt, sfirst, kind == FEWER))

            load_g(S_MOE, 0, lambda i: a["moe_gu"][0, 0, i])
            sp.wait_ge(ss_ready, 4 * NT)
            experts(S_MOE, 0)
            most = sp.value_load(CNT[0:1, NE:NE + 1], min_val=0, max_val=CAP)
            with sp.If(most > 2 * P):
                experts(S_MOE + NE * MOE_STEPS, 1)

            sp.wait_ge(y_all, 1)
            yt = y_d.rearrange("(t p c) d -> t p c d", p=P, c=2)
            for t in range(NT):
                sp.dma_start(y_rows[t][:, :, :], yt[t]).then_inc(y_ld[t], 16)
                if t == 0:
                    gain(GB[0][:, :], a["final_norm"], ld_gain)
            ot = out.rearrange("b (t p) d -> (b t) p d", p=P)
            for t in range(NT):
                sp.wait_ge(fo_ready, t + 1)
                sp.dma_start(ot[t], y_rows[t][:, 0, :]).then_inc(o_st, 16)
            sp.wait_ge(o_st, 16 * NT)

        @block.tensor
        def _(pe):
            pe.sem_inc(gu_done, 4)
            pe.sem_inc(down_done, 2)
            pe.wait_ge(ld_id, 16)

            def x_transpose(norm, phase, t, banks, emptied=None):
                pe.wait_ge(xn_ready, NT * norm + t + 1)
                for hf in range(2):
                    i = 2 * t + hf
                    if i >= len(banks):
                        if emptied is None:
                            pe.wait_ge(xT_ev, 2 * NT * phase + i - len(banks) + 1)
                        else:
                            pe.wait_ge(emptied, i - len(banks) + 1)
                    for k in range(4):
                        c = 4 * hf + k
                        last = pe.transpose(PS[:, banks[i % len(banks)], k * P:(k + 1) * P],
                                            XG[t % 2][:, c * P:(c + 1) * P], IDN[:, :])
                    last.then_inc(xT_tr, 1)

            def passes(dst, xh, xl, wh, wl, start, stop):
                pe.matmul(dst, xh, wh, start=start, stop=False)
                pe.matmul(dst, xh, wl, start=False, stop=False)
                return pe.matmul(dst, xl, wh, start=False, stop=stop)

            x_transpose(0, 0, 0, WIDE)
            for t in range(NT):
                if t + 1 < NT:
                    x_transpose(0, 0, t + 1, WIDE)
                pe.wait_ge(xT_ev, 2 * t + 2)
                if t >= 2:
                    pe.wait_ge(cn_ready, t - 1)
                for k in range(KD):
                    if t == 0 and k % 2 == 0:
                        pe.wait_ge(ld_wd[k // 2], 16)
                    last = pe.matmul(PS[:, 4 + t % 2, :], m_xT[:, k, t * P:(t + 1) * P], m_wd[:, k, 0:QR + KVR],
                                     start=k == 0, stop=k == KD - 1)
                last.then_inc(dq_done, 1)
            pe.wait_ge(wkr_ready, 3)
            for k in range(KD):
                last = pe.matmul(PS[:, 6, :], m_wkr[:, k, :], m_xT[:, k, :], start=k == 0, stop=k == KD - 1)
            last.then_inc(kr_done, 1)
            for t in range(NT):
                pe.wait_ge(cn_ready, t + 1)
                for c in range(4):
                    last = pe.transpose(PS[:, t, c * P:(c + 1) * P], m_cn[:, t, c * P:(c + 1) * P], IDN[:, :])
                last.then_inc(ct_tr, 1)
            pe.wait_ge(ct_ev, NT)
            pe.wait_ge(ld_uv, 16)
            for i in range(2 * NT):
                t, n = i // 2, i % 2
                if i >= 4:
                    pe.wait_ge(v_ev, i - 3)
                for c in range(2):
                    last = pe.matmul(PS[:, i % 4, :], m_cT[:, 2 + c, t * P:(t + 1) * P],
                                     m_uv[:, c, n * 512:(n + 1) * 512], start=c == 0, stop=c == 1)
                last.then_inc(v_done, 1)

            def project(h):
                if h == 0:
                    pe.wait_ge(ld_uq, 16)
                    pe.wait_ge(ld_uk, 16)
                    pe.wait_ge(wqr_ready, 6)
                    pe.wait_ge(kr_ready, 1)
                else:
                    pe.wait_ge(pj_lo, 2 * h)
                    pe.wait_ge(qr_ready, h)
                for b, w, c0 in ((6, lambda c: m_wqr[:, c, h, :], 0), (4, lambda c: m_uq[:, c, h, 0:NOPE], 0),
                                 (5, lambda c: m_uk[:, c, h, :], 2)):
                    for c in range(2):
                        last = pe.matmul(PS[:, b, :], w(c), m_cT[:, c0 + c, :], start=c == 0, stop=c == 1)
                    last.then_inc(pj_done, 1)

            def scores(h):
                b = h % 2
                pe.wait_ge(pj_lo, 2 * h + 2)
                pe.wait_ge(qr_ready, h + 1)
                for qt in range(NT):
                    if h == 0:
                        pe.wait_ge(v_ev, 2 * NT)
                    else:
                        pe.wait_ge(pt_ev, NT * (h - 1) + qt + 1)
                    q = slice(qt * P, (qt + 1) * P)
                    passes(PS[:, qt, :], m_qn[b][:, q], m_qnl[b][:, q], m_kn[b][:, :], m_knl[b][:, :], True, False)
                    pe.matmul(PS[:, qt, :], m_qr[b][:, q], m_kr[:, :], start=False, stop=False)
                    pe.matmul(PS[:, qt, :], m_qr[b][0:ROPE, q], m_krl[:, :], start=False, stop=True)\
                        .then_inc(sc_done, 1)

            project(0)
            scores(0)
            for h in range(HEADS):
                b = h % 2
                if h + 1 < HEADS:
                    project(h + 1)
                for qt in range(NT):
                    pe.wait_ge(pn_ready, NT * h + qt + 1)
                    for c in range(NT):
                        last = pe.transpose(PS[:, qt, c * P:(c + 1) * P], m_p[b][:, qt, c * P:(c + 1) * P], IDN[:, :])
                    last.then_inc(tr_done, 1)
                if h + 1 < HEADS:
                    scores(h + 1)
                if h:
                    pe.wait_ge(o_ev, h)
                pe.wait_ge(pt_ev, NT * h + NT)
                for c in range(NT):
                    last = pe.matmul(PS[:, 7, :], m_v[:, c, h * P:(h + 1) * P], m_pT[b][:, c, :],
                                     start=c == 0, stop=c == NT - 1)
                last.then_inc(pv_done, 1)

            def out_projection(phase, t, product):
                for n in range(2):
                    i = 2 * t + n
                    if i >= 4:
                        pe.wait_ge(wo_add, 2 * NT * phase + i - 3)
                    for c in range(8):
                        last = product(PS[:, i % 4, :], c, slice(t * P, (t + 1) * P), slice(n * 512, (n + 1) * 512))
                    last.then_inc(wo_done, 1)

            pe.wait_ge(o_ev, HEADS)
            pe.wait_ge(ld_mwo, 16)
            for t in range(NT):
                out_projection(0, t, lambda dst, c, tok, col: pe.matmul(
                    dst, m_oT[:, c, tok], m_wo[:, c, col], start=c == 0, stop=c == HEADS - 1))

            def unit_x(t, banks=None):
                for hf in range(2):
                    for k in range(4):
                        c = 4 * hf + k
                        last = pe.transpose(PS[:, (banks or X_BANKS[t])[hf], k * P:(k + 1) * P],
                                            XG[t][:, c * P:(c + 1) * P], IDN[:, :])
                    last.then_inc(xu_tr[t], 1)

            def unit(u, s0, par0, n, kind, source, more, free, before_last, b_behind_a=False):
                nt, few = kind
                two = shares(kind, 2)
                four = shares(kind, 4)
                if nt == 2 or few:
                    source(1)
                    if b_behind_a:
                        pe.wait_ge(xlo_ev[0], u * 2 + 2)
                    unit_x(1)
                else:
                    pe.sem_inc(xu_tr[1], 2)

                def to_columns(s):
                    for t in range(nt):
                        pe.wait_ge(h_ready, s * 4 + (1 if few else (t + 1) * four[0]))
                        for c in range(2):
                            last = pe.transpose(PS[:, 6 + t, c * P:(c + 1) * P], f_h[t][:, c * P:(c + 1) * P],
                                                IDN[:, :])
                        last.then_inc(ht_tr, two[0])

                def few_to_columns(s):
                    pe.wait_ge(h_ready, s * 4 + 4)
                    for c in range(2):
                        last = pe.transpose(PS[:, 7, c * P:(c + 1) * P], f_h[1][:, c * P:(c + 1) * P], IDN[:, :])
                    last.then_inc(ht_tr, two[0])

                def down(s, par, first, final=False):
                    pe.wait_ge(lo_d, s + 3)
                    if first:
                        free()
                    for t in range(nt):
                        pe.wait_ge(htl_done, s * 2 + (t + 1) * two[0])
                        for n_ in range(2):
                            col = slice(n_ * 512, (n_ + 1) * 512)
                            for c in range(2):
                                last = passes(PS[:, 2 * t + n_, :], f_hh[:, t, c, :], f_hl[:, t, c, :],
                                              f_hd[par][:, c, col], f_ld[par][:, c, col],
                                              first and c == 0, final and c == 1)
                    if few:
                        pe.wait_ge(htl_done, s * 2 + 2)
                        for c in range(2):
                            for j in range(4):
                                last = pe.matmul(PS[FEW * j:FEW * (j + 1), 2, 0:FB], f_hbT[:, c, :],
                                                 f_rd[par][:, c, j * FB:(j + 1) * FB],
                                                 start=first and c == 0, stop=final and c == 1)
                    last.then_inc(down_done, 1)

                def step(s, par, which, nxt):
                    if which:
                        to_columns(s - 1)
                    pe.wait_ge(lo_g, s * 2 + 6)
                    for t in range(nt):
                        if which == 0:
                            pe.wait_ge(xlo_ev[t], u * 2 + 2)
                        tok = slice(t * P, (t + 1) * P)
                        for g in range(2):
                            col = slice(g * FB, (g + 1) * FB)
                            for k in range(KD):
                                last = passes(PS[:, 4 + t, col], f_xh[:, k, tok], f_xl[:, k, tok],
                                              f_hg[par][:, k, col], f_lg[par][:, k, col], k == 0, k == KD - 1)
                        last.then_inc(gu_done, two[0])
                    if few:
                        if which:
                            few_to_columns(s - 1)
                        else:
                            pe.wait_ge(xlo_ev[1], u * 2 + 2)
                        for k in range(4):
                            for j in range(4):
                                g, hf = j // 2, j % 2
                                last = pe.matmul(PS[FEW * j:FEW * (j + 1), 5, 0:FB], f_xb[:, 4 * hf + k, :],
                                                 f_rg[par][hf][:, k, g * FB:(g + 1) * FB],
                                                 start=k == 0, stop=k == 3)
                        last.then_inc(gu_done, 1)
                    if which:
                        down(s - 1, 1 - par, which == 1)

                steps(pe, s0, par0, n, step, more)
                to_columns(s0 + (n - 1))
                if few:
                    few_to_columns(s0 + (n - 1))
                before_last()
                down(s0 + (n - 1), (par0 + n - 1) % 2, False, True)

            def ffn_x():
                pe.wait_ge(xn_ready, NT + 3)
                unit_x(0)

            pe.wait_ge(xn_ready, NT + 1)
            unit_x(0, (6, 7))
            for u in range(2):
                def source(t, u=u):
                    pe.wait_ge(xn_ready, NT + 2 * u + t + 1)

                def free(u=u):
                    if u:
                        pe.wait_ge(out_free, u)

                unit(u, u * FFN_STEPS, u * FFN_STEPS % 2, FFN_STEPS, TWO, source, u == 0, free,
                     (lambda: x_transpose(2, 1, 0, (4, 5, 6, 7))) if u else ffn_x, u == 0)

            def swa_v(t):
                pe.wait_ge(sx_lo, 2 * t + 2)
                if t >= 2:
                    pe.wait_ge(sv_ev, t - 1)
                tok, col = slice(t * P, (t + 1) * P), slice(KVH * HD, 2 * KVH * HD)
                for k in range(KD):
                    last = passes(PS[:, 4 + t % 2, 0:KVH * HD], s_xT[:, k, tok], s_xl[:, k, tok],
                                  s_wh[2][:, k, col], s_wl[2][:, k, col], k == 0, k == KD - 1)
                last.then_inc(sv_done, 1)

            x_transpose(2, 1, 1, (4, 5, 6, 7), sx_lo)
            pe.wait_ge(sw_lo, 2)
            for t in range(2):
                swa_v(t)
            for t in range(2, NT):
                x_transpose(2, 1, t, (6, 7), sx_lo)
            for t in range(2, NT):
                swa_v(t)
            for i, chunk in enumerate(QK_CHUNKS):
                part, col = chunk // 4, slice(chunk % 4 * P, (chunk % 4 + 1) * P)
                if chunk in (0, 4):
                    pe.wait_ge(sw_lo, 4 + 2 * part)
                if i >= 4:
                    pe.wait_ge(q_lo, i - 3)
                for k in range(KD):
                    last = passes(PS[:, i % 4, :], s_wh[part][:, k, col], s_wl[part][:, k, col],
                                  s_xT[:, k, :], s_xl[:, k, :], k == 0, k == KD - 1)
                last.then_inc(q_done, 1)

            def swa_scores(i):
                g, t = i // NT, i % NT
                half, c = g % 2, g // 2
                rows = slice(half * HD, half * HD + HD)
                lo, hi = max(0, t - 1) * P, min(NT, t + 2) * P
                if i == 0:
                    pe.wait_ge(q_lo, 10)
                else:
                    pe.wait_ge(st_ready, i)
                for r_ in range(GRP):
                    tok = slice(t * P, (t + 1) * P)
                    pe.matmul(PS[:, r_, 0:hi - lo], s_q[c][:, half, r_, tok], s_kh[:, g, lo:hi], start=True, stop=False)
                    last = pe.matmul(PS[:, r_, 0:hi - lo], s_q[c][rows, half, r_, tok], s_kl[rows, c, lo:hi],
                                     start=False, stop=True)
                last.then_inc(ss_done, 1)

            def swa_keys(i):
                return [kt for kt in (i % NT - 1, i % NT, i % NT + 1) if 0 <= kt < NT]

            def swa_values(i):
                g = i // NT
                half, keys = g % 2, swa_keys(i)
                pe.wait_ge(spt_ev, i + 1)
                if i:
                    pe.wait_ge(so_ev, i)
                for j, kt in enumerate(keys):
                    last = pe.matmul(PS[half * HD:half * HD + HD, 7, :], s_v[:, kt, g * HD:(g + 1) * HD],
                                     s_pT[i % 2][:, j, :, :].rearrange("p r q -> p (r q)"),
                                     start=j == 0, stop=j == len(keys) - 1)
                last.then_inc(spv_done, 1)

            def swa_out(t):
                pe.wait_ge(so_lo, 13 + t)
                out_projection(1, t, lambda dst, c, tok, col: passes(
                    dst, s_o[:, c // GRP, c % GRP, tok], s_ol[:, c // GRP, c % GRP, tok],
                    s_woh[c // GRP][:, c % GRP, col], s_wol[c // GRP][:, c % GRP, col], c == 0, c == 7))

            swa_scores(0)
            swa_scores(1)
            for i in range(16):
                if i + 2 < 16:
                    swa_scores(i + 2)
                if i == 15:
                    pe.wait_ge(st_ready, 16)
                    pe.wait_ge(swo_lo, 2 * GRP)
                    swa_out(0)
                pe.wait_ge(sp_ready, i + 1)
                if i == 0:
                    pe.wait_ge(sv_ev, NT)
                else:
                    pe.wait_ge(spt_ev, i)
                for j in range(len(swa_keys(i))):
                    for r_ in range(GRP):
                        last = pe.transpose(PS[:, 4 + j, r_ * P:(r_ + 1) * P],
                                            s_p[i % 2][:, r_, j * P:(j + 1) * P], IDN[:, :])
                last.then_inc(st_tr, 1)
                if i:
                    swa_values(i - 1)
            swa_values(15)

            def logits(t):
                pe.wait_ge(xT_ev, 4 * NT + 2 * t + 2)
                for k in range(KD):
                    last = pe.matmul(PS[:, 0, t * NE:(t + 1) * NE], g_xT[:, k, t * P:(t + 1) * P], g_rt[:, k, :],
                                     start=k == 0, stop=k == KD - 1)
                return last

            def moe_x(t):
                if t == NT - 1:
                    pe.wait_ge(ld_route, 80)
                    pe.wait_ge(wo_add, 2 * NT + 6)
                    for t2 in range(t):
                        logits(t2)
                x_transpose(3, 2, t, (6, 7))

            for t in range(1, NT):
                swa_out(t)
                if t == 1:
                    pe.wait_ge(so_ev, 16)
                moe_x(t - 1)
            moe_x(NT - 1)

            logits(NT - 1).then_inc(lg_done, 1)
            pe.wait_ge(m_ready, 1)
            pe.matmul(PS[:, 5, 0:(NT + 1) * NE], TRI[:, :], g_m[:, :], start=True, stop=False)
            for back in range(1, NT + 1):
                last = pe.matmul(PS[:, 5, back * NE:(NT + 1) * NE], ONES[:, :], g_m[:, 0:(NT + 1 - back) * NE],
                                 start=False, stop=back == NT)
            last.then_inc(rk_done, 1)
            for i in range(2 * NT):
                pe.wait_ge(hot_ready, i + 1)
                last = pe.matmul(PS[:, 4, 0:NE * NT], g_at[:, i, :], g_val[:, i, :], start=i == 0,
                                 stop=i == 2 * NT - 1)
            last.then_inc(list_done, 1)

            pe.wait_ge(cnt_ready, 1)

            def expert(e, turn, kind):
                def source(t):
                    pe.wait_ge(xg_ready[t], e * 16 + 16 * (NE * turn + 1))

                def free():
                    pe.wait_ge(yo_ready, e * 2 + (2 * NE * turn + 2))

                def next_x():
                    pe.wait_ge(xg_ready[0], e * 16 + 16 * (NE * turn + 2))
                    unit_x(0)

                unit(e + (U_MOE + NE * turn), e * MOE_STEPS + (S_MOE + turn * NE * MOE_STEPS), 0, MOE_STEPS, kind,
                     source, True, free, next_x)

            pe.wait_ge(xg_ready[0], 16)
            unit_x(0)
            with pe.Fori(0, NE) as e:
                n = pe.value_load(CNT[0:1, bass.ds(e, 1)], min_val=0, max_val=CAP)
                by_count(pe, n, lambda kind: expert(e, 0, kind))
            most = pe.value_load(CNT[0:1, NE:NE + 1], min_val=0, max_val=CAP)
            with pe.If(most > 2 * P):
                with pe.Fori(0, NE) as e:
                    expert(e, 1, TWO)

        @block.scalar
        def _(act):
            def copy(dst, src):
                return act.activation(dst, src, ACT.Copy)

            def std(norm, t):
                act.wait_ge(ss_ready, NT * norm + t + 1)
                act.activation(SD[:, t:t + 1], SS[:, t:t + 1], ACT.Sqrt, bias=EPSC[:, :]).then_inc(std_ready, 1)

            def x_evict(phase, xT, t, banks):
                for hf in range(2):
                    act.wait_ge(xT_tr, 2 * NT * phase + 2 * t + hf + 1)
                    copy(xT[:, 4 * hf:4 * hf + 4, t * P:(t + 1) * P],
                         PS[:, banks[(2 * t + hf) % len(banks)], :].rearrange("p (k q) -> p k q", k=4)).then_inc(xT_ev, 1)

            def stds_and_x(norm, phase, xT, banks):
                for t in range(NT):
                    std(norm, t)
                    if t:
                        x_evict(phase, xT, t - 1, banks)
                x_evict(phase, xT, NT - 1, banks)

            act.wait_ge(eps_set, 1)

            def c_std(t):
                act.wait_ge(dq_done, t + 1)
                for i in range(2):
                    act.activation(m_junk[:, i, :], PS[:, 4 + t % 2, i * QR:(i + 1) * QR], ACT.Square,
                                   accum_out=m_sq[:, 2 * t + i:2 * t + i + 1]).then_inc(sq_done, 1)
                act.wait_ge(sq_done, 2 * t + 2)
                act.activation(m_sd[:, 2 * t:2 * t + 2], m_sq[:, 2 * t:2 * t + 2], ACT.Sqrt, scale=1.0 / QR,
                               bias=EPSC[:, :]).then_inc(cstd, 1)

            for t in range(NT):
                std(0, t)
                x_evict(0, m_xT, t, WIDE)
                if t >= 2:
                    c_std(t - 2)
            for t in range(NT - 2, NT):
                c_std(t)
            for t in range(NT):
                act.wait_ge(ct_tr, t + 1)
                copy(m_cT[:, :, t * P:(t + 1) * P],
                     PS[:, t, :].rearrange("p (c q) -> p c q", c=4)).then_inc(ct_ev, 1)
            act.wait_ge(ks_ready, 1)
            for half in range(2):
                copy(m_kr[half * ROPE:(half + 1) * ROPE, :], m_t1[:, :]).then_inc(kh_ready, 1)
            for i in range(2 * NT):
                act.wait_ge(v_done, i + 1)
                copy(m_v[:, i // 2, (i % 2) * 512:(i % 2 + 1) * 512], PS[:, i % 4, :]).then_inc(v_ev, 1)

            def project_evict(h):
                if h >= 2:
                    act.wait_ge(sc_done, NT * (h - 1))
                act.wait_ge(pj_done, 3 * h + 2)
                copy(m_qn[h % 2][:, :], PS[:, 4, :]).then_inc(pj_ev, 1)
                act.wait_ge(pj_done, 3 * h + 3)
                copy(m_kn[h % 2][:, :], PS[:, 5, :]).then_inc(pj_ev, 1)
                act.wait_ge(qs_ready, h + 1)
                copy(m_qr[h % 2][0:ROPE, :], m_t1[:, :]).then_inc(qh_ready, 1)

            def o_evict(h):
                act.wait_ge(pv_done, h + 1)
                copy(m_oT[:, h, :], PS[:, 7, :]).then_inc(o_ev, 1)

            project_evict(0)
            for h in range(HEADS):
                b = h % 2
                for qt in range(NT):
                    i = NT * h + qt
                    act.wait_ge(nm_ready, i + 1)
                    if h >= 2:
                        act.wait_ge(tr_done, i - 2 * NT + 1)
                    act.activation(m_p[b][:, qt, :], PS[:, qt, :], ACT.Exp, bias=m_nm[:, i:i + 1], scale=MLA_SCALE,
                                   accum_out=m_sm[:, i:i + 1]).then_inc(ex_done, 1)
                if h:
                    o_evict(h - 1)
                if h + 1 < HEADS:
                    project_evict(h + 1)
                for qt in range(NT):
                    act.wait_ge(tr_done, NT * h + qt + 1)
                    if h >= 2:
                        act.wait_ge(pv_done, h - 1)
                    copy(m_pT[b][:, :, qt * P:(qt + 1) * P],
                         PS[:, qt, :].rearrange("p (c q) -> p c q", c=NT)).then_inc(pt_ev, 1)
            o_evict(HEADS - 1)

            def qkv_high(c):
                act.wait_ge(ld_sw[c], 32)
                for k in range(0, KD, 4):
                    copy(s_wh[c][:, k:k + 4, :], s_w[c][:, k:k + 4, :]).then_inc(sw_hi, 1)

            def hi_gu(s, par):
                for i in range(2):
                    act.wait_ge(raw_g[par][i], s * 8 + (16 - 8 * par))
                    act.wait_ge(gu_done, s * 2 + 2)
                    copy(f_hg[par][:, 4 * i:4 * i + 2, :], f_rg[par][i][:, 0:2, :])
                    copy(f_hg[par][:, 4 * i + 2:4 * i + 4, :], f_rg[par][i][:, 2:4, :]).then_inc(hi_g, 1)

            def unit_x_high(u, t, banks=None):
                for hf in range(2):
                    act.wait_ge(xu_tr[t], u * 2 + (hf + 1))
                    copy(f_xh[:, 4 * hf:4 * hf + 4, t * P:(t + 1) * P],
                         PS[:, (banks or X_BANKS[t])[hf], :].rearrange("p (k q) -> p k q", k=4))\
                        .then_inc(xhi_ev[t], 1)

            def unit(u, s0, par0, n, kind, more, before_last, behind_x=None):
                nt, few = kind
                two, four = shares(kind, 2), shares(kind, 4)
                if nt == 2:
                    unit_x_high(u, 1)
                else:
                    act.sem_inc(xhi_ev[1], 2)
                if behind_x:
                    behind_x()

                def hidden_T(s):
                    for t in range(nt):
                        act.wait_ge(ht_tr, s * 2 + (t + 1) * two[0])
                        copy(f_hh[:, t, :, :], PS[:, 6 + t, 0:2 * P].rearrange("p (c q) -> p c q", c=2))\
                            .then_inc(hth_done, 2 if few else two[0])

                def step(s, par, which, nxt):
                    if which:
                        hidden_T(s - 1)
                    if nxt:
                        hi_gu(s + 1, 1 - par)
                    else:
                        act.wait_ge(lo_g, 2 * FFN_TOTAL + 4)
                        qkv_high(2)
                    for t in range(nt):
                        act.wait_ge(gu_done, s * 2 + (4 + (t + 1) * two[0]))
                        act.activation(f_sg[t][:, :], PS[:, 4 + t, 0:FB], ACT.Silu)\
                            .then_inc(sg_done, 1 if few else four[0])
                    if few:
                        act.wait_ge(gu_done, s * 2 + 6)
                        copy(f_cb[0:FEW, :], PS[FEW:2 * FEW, 5, 0:FB])
                        copy(f_cb[2 * FEW:3 * FEW, :], PS[3 * FEW:P, 5, 0:FB]).then_inc(sg_done, 1)
                    act.wait_ge(raw_d[par], s * 8 + (16 - 8 * par))
                    act.wait_ge(down_done, s + 1)
                    copy(f_hd[par][:, 0, :], f_rd[par][:, 0, :])
                    if few:
                        act.wait_ge(h_ready, s * 4 + 2)
                        act.activation(f_sb, f_gb[:, 0:FB], ACT.Silu).then_inc(sg_done, 2)
                    copy(f_hd[par][:, 1, :], f_rd[par][:, 1, :]).then_inc(hi_d, 1)

                steps(act, s0, par0, n, step, more)
                hidden_T(s0 + (n - 1))
                before_last()

            hi_gu(0, 0)
            for t in range(NT):
                std(1, t)
            unit_x_high(0, 0, (6, 7))
            for u in range(2):
                unit(u, u * FFN_STEPS, u * FFN_STEPS % 2, FFN_STEPS, TWO, u == 0,
                     (lambda: x_evict(1, s_xT, 0, (4, 5, 6, 7))) if u else lambda: unit_x_high(1, 0),
                     (lambda: [std(2, t) for t in range(2)]) if u else None)

            def swa_v_evict(t):
                act.wait_ge(sv_done, t + 1)
                copy(s_v[:, t, :], PS[:, 4 + t % 2, 0:KVH * HD]).then_inc(sv_ev, 1)

            x_evict(1, s_xT, 1, (4, 5, 6, 7))
            for t in range(2, NT):
                std(2, t)
            for t in range(2):
                swa_v_evict(t)
            for t in range(2, NT):
                x_evict(1, s_xT, t, (6, 7))
            for t in range(2, NT):
                swa_v_evict(t)
            qkv_high(0)
            for i, chunk in enumerate(QK_CHUNKS):
                if i == 2:
                    qkv_high(1)
                act.wait_ge(q_done, i + 1)
                for half in range(2):
                    rows, other = HALVES[half], HALVES[1 - half]
                    if chunk < 8:
                        last = copy(s_q[chunk // GRP][rows, half, chunk % GRP, :], PS[rows, i % 4, :])
                    else:
                        for dst_rows in (rows, other):
                            last = copy(s_kh[dst_rows, 2 * (chunk - 8) + half, :], PS[rows, i % 4, :])
                last.then_inc(q_ev, 1)

            def swa_probs(i):
                t = i % NT
                w = (min(NT, t + 2) - max(0, t - 1)) * P
                act.wait_ge(sm_ready, i + 1)
                if i >= 2:
                    act.wait_ge(st_tr, i - 1)
                for r_ in range(GRP):
                    act.activation(s_p[i % 2][:, r_, 0:w], s_s[i % 2][:, r_, 0:w], ACT.Exp, scale=SWA_SCALE,
                                   bias=s_nm[:, GRP * i + r_:GRP * i + r_ + 1],
                                   accum_out=s_sm[:, GRP * i + r_:GRP * i + r_ + 1])
                c = slice(GRP * i, GRP * i + GRP)
                act.activation(s_es[:, c], s_es[:, c], ACT.Exp, scale=SWA_SCALE).then_inc(se_done, 1)

            def swa_o_evict(i):
                t, half, c = i % NT, (i // NT) % 2, i // NT // 2
                act.wait_ge(spv_done, i + 1)
                rows = slice(half * HD, half * HD + HD)
                for dst in (s_o, s_or):
                    last = copy(dst[rows, c, :, t * P:(t + 1) * P], PS[rows, 7, :].rearrange("p (r q) -> p r q", r=GRP))
                last.then_inc(so_ev, 1)

            def wo_high(c, r_):
                act.wait_ge(ld_swo[c], 16)
                copy(s_woh[c][:, r_, :], s_wo[c][:, r_, :]).then_inc(swo_hi, 1)

            swa_probs(0)
            swa_probs(1)
            for i in range(16):
                t = i % NT
                nk = min(NT, t + 2) - max(0, t - 1)
                act.wait_ge(st_tr, i + 1)
                if i >= 2:
                    act.wait_ge(spv_done, i - 1)
                for j in range(nk):
                    last = copy(s_pT[i % 2][:, j, :, :], PS[:, 4 + j, :].rearrange("p (r q) -> p r q", r=GRP))
                last.then_inc(spt_ev, 1)
                if i + 2 < 16:
                    swa_probs(i + 2)
                if i:
                    swa_o_evict(i - 1)
                if WO_FROM <= i < WO_FROM + 2 * GRP:
                    wo_high((i - WO_FROM) // GRP, (i - WO_FROM) % GRP)
            swa_o_evict(15)

            stds_and_x(3, 2, g_xT, (6, 7))
            act.wait_ge(d_ready, 1)
            act.activation(g_e[:, :], g_d[:, :], ACT.Exp).then_inc(e_ready, 1)
            hi_gu(S_MOE, 0)
            act.wait_ge(cnt_ready, 1)

            def expert(e, turn, kind):
                u = e + (U_MOE + NE * turn)
                s0 = e * MOE_STEPS + (S_MOE + turn * NE * MOE_STEPS)
                act.activation(f_one[:, :], EPSC[:, :], ACT.Silu)
                unit(u, s0, 0, MOE_STEPS, kind, True, lambda: unit_x_high(u + 1, 0))
                rows_out(act, copy, e, turn, kind, 0)

            act.sem_inc(yo_ready, 2)
            unit_x_high(U_MOE, 0)
            with act.Fori(0, NE) as e:
                n = act.value_load(CNT[0:1, bass.ds(e, 1)], min_val=0, max_val=CAP)
                by_count(act, n, lambda kind: expert(e, 0, kind))
            most = act.value_load(CNT[0:1, NE:NE + 1], min_val=0, max_val=CAP)
            with act.If(most > 2 * P):
                with act.Fori(0, NE) as e:
                    expert(e, 1, TWO)
            for t in range(NT):
                act.wait_ge(y_used, t + 1)
                act.activation(y_rows[t][:, 1, :], H[:, t, :], ACT.Square, accum_out=SS[:, t:t + 1]).then_inc(ss_ready, 1)
                act.wait_ge(ss_ready, NT * 4 + t + 1)
                act.activation(SD[:, t:t + 1], SS[:, t:t + 1], ACT.Sqrt, scale=1.0 / D, bias=EPSC[:, :])\
                    .then_inc(std_ready, 1)

        @block.vector
        def _(dve):
            dve.sem_inc(lo_g, 4)
            dve.sem_inc(lo_d, 2)
            count = [0]

            def link(ins):
                count[0] += 1
                ins.then_inc(chain, 1)
                dve.wait_ge(chain, count[0])

            tt, ts, stt = dve.tensor_tensor, dve.tensor_scalar, dve.scalar_tensor_tensor

            def mean_square(t, squares=None):
                if squares is None:
                    squares = PS[:, 4:6, :].rearrange("p b n -> p (b n)")
                dve.tensor_tensor_reduce(out=squares, in0=H[:, t, :], in1=H[:, t, :],
                                         scale=1.0 / D, scalar=0.0, op0=ALU.mult, op1=ALU.add,
                                         accum_out=SS[:, t:t + 1]).then_inc(ss_ready, 1)

            def rstd(norm, t):
                dve.wait_ge(std_ready, NT * norm + t + 1)
                link(dve.reciprocal(RS[:, t:t + 1], SD[:, t:t + 1]))

            def rows(t, gain_):
                return stt(XG[t % 2][:, :], H[:, t, :], RS[:, t:t + 1], gain_[:, :], ALU.mult, ALU.mult)

            def lo_part(dst, src, hi):
                return tt(dst, src, hi.bitcast(F32), ALU.subtract)

            dve.memset(EPSC[:, :], EPS).then_inc(eps_set, 1)
            for t in range(NT):
                dve.wait_ge(ld_h[t], 16)
                if t:
                    dve.wait_ge(ss_ready, t)
                mean_square(t, PS[:, 6:8, :].rearrange("p b n -> p (b n)"))
                if t == 0:
                    dve.wait_ge(ld_gain, 16)
                rstd(0, t)
                if t >= 2:
                    dve.wait_ge(xT_tr, 2 * (t - 1))
                rows(t, GB[0]).then_inc(xn_ready, 1)
            dve.wait_ge(ld_tab, 48)
            for t in range(NT):
                dve.wait_ge(cstd, t + 1)
                link(dve.reciprocal(m_rq[:, 2 * t:2 * t + 2], m_sd[:, 2 * t:2 * t + 2]))
                for i in range(2):
                    c = slice(i * QR, (i + 1) * QR)
                    ins = stt(m_cn[:, t, c], PS[:, 4 + t % 2, c], m_rq[:, 2 * t + i:2 * t + i + 1], m_gq[:, c],
                              ALU.mult, ALU.mult)
                ins.then_inc(cn_ready, 1)

            def rope():
                tt(m_t1[:, :], PS[0:ROPE, 6, :], m_tab[0:ROPE, :], ALU.mult)
                link(tt(m_t2[:, :], PS[ROPE:P, 6, :], m_tab[ROPE:P, :], ALU.mult))
                return tt(m_t1[:, :], m_t1[:, :], m_t2[:, :], ALU.add)

            dve.wait_ge(kr_done, 1)
            rope().then_inc(ks_ready, 1)
            dve.wait_ge(kh_ready, 2)
            lo_part(m_krl[:, :], m_t1[:, :], m_kr[0:ROPE, :]).then_inc(kr_ready, 1)

            def rope_head(h):
                dve.wait_ge(pj_done, 3 * h + 1)
                if h >= 2:
                    dve.wait_ge(sc_done, NT * (h - 1))
                if h:
                    dve.wait_ge(qr_ready, h)
                else:
                    dve.wait_ge(kr_ready, 1)
                rope().then_inc(qs_ready, 1)
                for i, (hi, lo) in enumerate(((m_qn, m_qnl), (m_kn, m_knl))):
                    dve.wait_ge(pj_ev, 2 * h + i + 1)
                    lo_part(lo[h % 2][:, :], PS[:, 4 + i, :], hi[h % 2][:, :]).then_inc(pj_lo, 1)
                dve.wait_ge(qh_ready, h + 1)
                lo_part(m_qr[h % 2][ROPE:P, :], m_t1[:, :], m_qr[h % 2][0:ROPE, :]).then_inc(qr_ready, 1)

            def normalise(h, qt):
                i = NT * h + qt
                dve.wait_ge(ex_done, i + 1)
                link(dve.reciprocal(m_rc[:, i:i + 1], m_sm[:, i:i + 1]))
                ts(m_p[h % 2][:, qt, :], m_p[h % 2][:, qt, :], m_rc[:, i:i + 1], None, ALU.mult).then_inc(pn_ready, 1)

            rope_head(0)
            for h in range(HEADS):
                for qt in range(NT):
                    i = NT * h + qt
                    dve.wait_ge(sc_done, i + 1)
                    link(dve.reduce_max(m_mx[:, i:i + 1], PS[:, qt, :], AXX))
                    ts(m_nm[:, i:i + 1], m_mx[:, i:i + 1], -MLA_SCALE, None, ALU.mult).then_inc(nm_ready, 1)
                    if qt:
                        normalise(h, qt - 1)
                normalise(h, NT - 1)
                if h + 1 < HEADS:
                    rope_head(h + 1)

            def add_projection(phase, norm, then, squares=None):
                for t in range(NT):
                    for n_ in range(2):
                        i, c = 2 * t + n_, slice(n_ * 512, (n_ + 1) * 512)
                        dve.wait_ge(wo_done, 2 * NT * phase + i + 1)
                        tt(H[:, t, c], H[:, t, c], PS[:, i % 4, :], ALU.add).then_inc(wo_add, 1)
                    dve.wait_ge(wo_add, 2 * NT * phase + 2 * t + 2)
                    if t:
                        dve.wait_ge(ss_ready, NT * norm + t)
                    mean_square(t, squares)
                    rstd(norm, t)
                    then(t)

            def qkv_low(c, order):
                for k in range(0, KD, 4):
                    dve.wait_ge(sw_hi, 2 * order + k // 4 + 1)
                    lo_part(s_wl[c][:, k:k + 4, :], s_w[c][:, k:k + 4, :], s_wh[c][:, k:k + 4, :]).then_inc(sw_lo, 1)

            def swa_x_low(t, banks):
                for hf in range(2):
                    dve.wait_ge(xT_ev, 2 * NT + 2 * t + hf + 1)
                    k, tok = slice(4 * hf, 4 * hf + 4), slice(t * P, (t + 1) * P)
                    lo_part(s_xl[:, k, tok], PS[:, banks[hf], :].rearrange("p (k q) -> p k q", k=4),
                            s_xT[:, k, tok]).then_inc(sx_lo, 1)

            def lo_gu(s, par):
                for i in range(2):
                    dve.wait_ge(hi_g, s * 2 + (i + 1))
                    for j in range(2):
                        k = slice(4 * i + 2 * j, 4 * i + 2 * j + 2)
                        last = lo_part(f_lg[par][:, k, :], f_rg[par][i][:, 2 * j:2 * j + 2, :], f_hg[par][:, k, :])
                    last.then_inc(lo_g, 1)

            def unit_x_low(u, t, banks=None):
                for hf in range(2):
                    dve.wait_ge(xhi_ev[t], u * 2 + (hf + 1))
                    k, tok = slice(4 * hf, 4 * hf + 4), slice(t * P, (t + 1) * P)
                    lo_part(f_xl[:, k, tok], PS[:, (banks or X_BANKS[t])[hf], :].rearrange("p (k q) -> p k q", k=4),
                            f_xh[:, k, tok]).then_inc(xlo_ev[t], 1)

            def unit(u, s0, par0, n, kind, more, before_last, behind_x=None):
                nt, few = kind
                two, four = shares(kind, 2), shares(kind, 4)
                if nt == 2:
                    unit_x_low(u, 1)
                elif few:
                    dve.wait_ge(xu_tr[1], u * 2 + 2)
                    for hf in range(2):
                        dve.tensor_copy(f_xb[:, 4 * hf:4 * hf + 4, :],
                                        PS[:, 6 + hf, :].rearrange("p (k q) -> p k q", k=4)[:, :, 0:FEW])\
                            .then_inc(xlo_ev[1], 1)
                else:
                    dve.sem_inc(xlo_ev[1], 2)
                if behind_x:
                    behind_x()

                def hidden_T(s):
                    for t in range(nt):
                        dve.wait_ge(hth_done, s * 2 + (t + 1) * two[0])
                        lo_part(f_hl[:, t, :, :], PS[:, 6 + t, 0:2 * P].rearrange("p (c q) -> p c q", c=2),
                                f_hh[:, t, :, :]).then_inc(htl_done, two[0])

                def few_hidden_T(s):
                    dve.wait_ge(ht_tr, s * 2 + 2)
                    dve.tensor_copy(f_hbT[:, :, :], PS[:, 7, 0:2 * P].rearrange("p (c q) -> p c q", c=2)[:, :, 0:FEW])\
                        .then_inc(htl_done, 1)

                def step(s, par, which, nxt):
                    if which:
                        hidden_T(s - 1)
                    if nxt:
                        lo_gu(s + 1, 1 - par)
                    else:
                        qkv_low(2, 0)
                    if few and which:
                        few_hidden_T(s - 1)
                    for t in range(nt):
                        dve.wait_ge(sg_done, s * 4 + (1 if few else (t + 1) * four[0]))
                        tt(f_h[t][:, :], f_sg[t][:, :], PS[:, 4 + t, FB:2 * FB], ALU.mult)\
                            .then_inc(h_ready, 1 if few else four[0])
                    if few:
                        dve.wait_ge(sg_done, s * 4 + 2)
                        tt(f_gb[:, 0:FB], PS[0:FEW, 5, 0:FB], f_cb[0:FEW, :], ALU.add)
                        tt(f_gb[:, FB:2 * FB], PS[2 * FEW:3 * FEW, 5, 0:FB], f_cb[2 * FEW:3 * FEW, :], ALU.add)\
                            .then_inc(h_ready, 1)
                    dve.wait_ge(hi_d, s + 1)
                    lo_part(f_ld[par][:, 0, :], f_rd[par][:, 0, :], f_hd[par][:, 0, :])
                    if few:
                        dve.wait_ge(sg_done, s * 4 + 4)
                        tt(f_hb, f_sb, f_gb[:, FB:2 * FB], ALU.mult).then_inc(h_ready, 2)
                    lo_part(f_ld[par][:, 1, :], f_rd[par][:, 1, :], f_hd[par][:, 1, :]).then_inc(lo_d, 1)

                steps(dve, s0, par0, n, step, more)
                hidden_T(s0 + (n - 1))
                if few:
                    few_hidden_T(s0 + (n - 1))
                before_last()

            lo_gu(0, 0)
            dve.wait_ge(gain_b, 16)

            def ffn_rows(t):
                rows(t, GB[1]).then_inc(xn_ready, 1)

            def swa_rows(t):
                rstd(2, t)
                if t >= 2:
                    dve.wait_ge(xT_tr, 2 * NT + 2 * (t - 1))
                rows(t, GB[0]).then_inc(xn_ready, 1)

            def swa_square(t):
                if t:
                    dve.wait_ge(ss_ready, NT * 2 + t)
                mean_square(t, GB[1][:, :])

            def swa_rows_early():
                dve.wait_ge(out_free, 1)
                dve.wait_ge(xu_tr[1], 4)
                dve.wait_ge(ld_gain, 32)
                for t in range(2):
                    swa_square(t)
                for t in range(2):
                    swa_rows(t)

            add_projection(0, 1, lambda t: ffn_rows(t) if t < 2 else None)

            def ffn_rows_late():
                for t in range(2):
                    dve.wait_ge(xu_tr[t], 2)
                    ffn_rows(2 + t)

            def swa_x_first():
                dve.wait_ge(lo_d, FFN_TOTAL + 2)
                swa_x_low(0, (4, 5))

            unit_x_low(0, 0, (6, 7))
            for u in range(2):
                unit(u, u * FFN_STEPS, u * FFN_STEPS % 2, FFN_STEPS, TWO, u == 0,
                     swa_x_first if u else lambda: unit_x_low(1, 0), swa_rows_early if u else ffn_rows_late)
                dve.wait_ge(down_done, 2 + (u + 1) * FFN_STEPS)
                for t in range(2 * u, 2 * u + 2):
                    for n_ in range(2):
                        c = slice(n_ * 512, (n_ + 1) * 512)
                        ins = tt(H[:, t, c], H[:, t, c], PS[:, 2 * (t - 2 * u) + n_, :], ALU.add)
                    if t % 2:
                        ins.then_inc(out_free, 1)
                    elif u:
                        link(ins)
                        swa_square(t)
                        swa_x_low(1, (6, 7))

            dve.wait_ge(out_free, 2)
            swa_square(NT - 1)
            for t in range(2, NT):
                swa_rows(t)
            for t in range(2, NT):
                swa_x_low(t, (6, 7))
            qkv_low(0, 1)
            for i, chunk in enumerate(QK_CHUNKS):
                if i == 2:
                    qkv_low(1, 2)
                dve.wait_ge(q_ev, i + 1)
                for half in range(2):
                    own, other = HALVES[half], HALVES[1 - half]
                    if chunk < 8:
                        r_ = chunk % GRP
                        last = lo_part(s_q[chunk // GRP][other, half, r_, :], PS[own, i % 4, :],
                                       s_q[chunk // GRP][own, half, r_, :])
                    else:
                        last = lo_part(s_kl[own, chunk - 8, :], PS[own, i % 4, :],
                                       s_kh[own, 2 * (chunk - 8) + half, :])
                last.then_inc(q_lo, 1)
            dve.wait_ge(ld_sc, 32)
            link(ts(s_sk8[:, :], s_snk[:, :], SCALE8, None, ALU.mult))

            def swa_logits(i):
                g, t = i // NT, i % NT
                w = (min(NT, t + 2) - max(0, t - 1)) * P
                off = P if t == 0 else 0
                b, c = i % 2, slice(GRP * i, GRP * i + GRP)
                dve.wait_ge(ss_done, i + 1)
                if i >= 2:
                    dve.wait_ge(se_done, i - 1)
                for r_ in range(GRP):
                    slope = 2.0 ** (-8.0 * (GRP * g + r_ + 1) / QH)
                    last = stt(s_s[b][:, r_, 0:w], s_dist[:, off:off + w], -SCALE8 * slope, PS[:, r_, 0:w],
                               ALU.mult, ALU.add)
                last.then_inc(st_ready, 1)
                dve.wait_ge(st_ready, i + 1)
                link(dve.reduce_max(s_rc[:, c], s_s[b][:, :, 0:w], AXX))
                link(tt(s_mx[:, c], s_rc[:, c], s_sk8[:, GRP * g:GRP * g + GRP], ALU.max))
                ts(s_nm[:, c], s_mx[:, c], -SWA_SCALE, None, ALU.mult)
                tt(s_es[:, c], s_sk8[:, GRP * g:GRP * g + GRP], s_mx[:, c], ALU.subtract).then_inc(sm_ready, 1)

            def swa_normalise(i):
                t = i % NT
                w = (min(NT, t + 2) - max(0, t - 1)) * P
                c = slice(GRP * i, GRP * i + GRP)
                dve.wait_ge(se_done, i + 1)
                link(tt(s_mx[:, c], s_sm[:, c], s_es[:, c], ALU.add))
                link(dve.reciprocal(s_rc[:, c], s_mx[:, c]))
                for r_ in range(GRP):
                    last = ts(s_p[i % 2][:, r_, 0:w], s_p[i % 2][:, r_, 0:w], s_rc[:, GRP * i + r_:GRP * i + r_ + 1],
                              None, ALU.mult)
                last.then_inc(sp_ready, 1)

            swa_logits(0)
            swa_logits(1)
            for i in range(16):
                swa_normalise(i)
                if i + 2 < 16:
                    swa_logits(i + 2)
            dve.wait_ge(gain_b, 32)

            def moe_rows(t):
                if t >= 2:
                    dve.wait_ge(xT_tr, 4 * NT + 2 * (t - 1))
                    dve.wait_ge(hn_st[t % 2], 16)
                rows(t, GB[1]).then_inc(xn_ready, 1)

            add_projection(1, 3, moe_rows, s_squares[:, :])

            dve.wait_ge(ld_route, 80)
            dve.memset(g_m[:, NT * NE:], 0.0)
            wide = lambda x: x[:, :].unsqueeze(2).to_broadcast((P, NT, NE))
            rev, at_list = (g_c[:, i, :, :] for i in range(2))
            slot_row, list_column, choice_value = g_sc[:, 0:P], g_sc[:, P:P + NE * NT], g_sc[:, P + NE * NT:]
            dve.wait_ge(lg_done, 1)
            link(dve.tensor_copy(g_lg[:, :, :], PS[:, 0, 0:NT * NE].rearrange("p (t e) -> p t e", t=NT)))

            def pick(lg, m, eq, w, first, oh):
                link(dve.reduce_max(m[:, :], lg[:, :, :], AXX))
                link(tt(eq[:, :, :], lg[:, :, :], wide(m), ALU.is_equal))
                link(tt(w[:, :, :], eq[:, :, :], rev, ALU.mult))
                link(dve.reduce_max(first[:, :], w[:, :, :], AXX))
                link(tt(oh[:, :, :], rev, wide(first), ALU.is_equal))

            pick(g_lg, g_m1, g_eq, g_w1, g_i1, g_o1)
            link(stt(g_l2[:, :, :], g_o1[:, :, :], -3e38, g_lg[:, :, :], ALU.mult, ALU.add))
            pick(g_l2, g_m2, g_eq, g_w2, g_i2, g_o2)
            tt(g_m[:, 0:NT * NE].rearrange("p (t e) -> p t e", t=NT), g_o1[:, :, :], g_o2[:, :, :], ALU.add).then_inc(m_ready, 1)
            tt(g_d[:, :], g_m2[:, :], g_m1[:, :], ALU.subtract).then_inc(d_ready, 1)
            dve.wait_ge(e_ready, 1)
            link(ts(g_s1[:, :], g_e[:, :], 1.0, None, ALU.add))
            link(dve.reciprocal(G12[:, 0:NT], g_s1[:, :]))
            link(tt(G12[:, NT:2 * NT], g_e[:, :], G12[:, 0:NT], ALU.mult))
            dve.wait_ge(rk_done, 1)
            link(dve.tensor_copy(g_cf[:, 0:NE], PS[:, 5, NT * NE:NT * NE + NE]))
            link(dve.reduce_max(g_cf[:, NE:NE + 1], g_cf[:, 0:NE], AXX))
            dve.tensor_copy(CNT[:, :], g_cf[:, :]).then_inc(cnt_ready, 1)
            link(dve.tensor_copy(g_rk[:, :, :], PS[:, 5, 0:NT * NE].rearrange("p (t e) -> p t e", t=NT)))
            link(ts(g_j[:, :, :], g_rk[:, :, :], float(P), None, ALU.is_ge))
            link(stt(g_j2[:, :, :], g_rk[:, :, :], float(2 * P), g_j[:, :, :], ALU.is_ge, ALU.add))
            link(stt(g_tile[:, :, :], g_rk[:, :, :], float(3 * P), g_j2[:, :, :], ALU.is_ge, ALU.add))
            tt(g_list[:, :, :], g_tile[:, :, :], at_list, ALU.add)
            link(stt(g_part[:, :, :], g_tile[:, :, :], float(-P), g_rk[:, :, :], ALU.mult, ALU.add))
            for i, x in enumerate((g_part, g_list)):
                for c in range(2):
                    ins = tt(g_pr[i][:, c * NT:(c + 1) * NT, :], g_oh[:, c, :, :], x[:, :, :], ALU.mult)
            link(ins)
            for i in range(2):
                ins = dve.reduce_sum(g_sel[i][:, :], g_pr[i][:, :, :], AXX)
            link(ins)
            for i in range(2 * NT):
                ts(g_at[:, i, :], slot_row, g_sel[0][:, i:i + 1], None, ALU.is_equal)
                ts(g_val[:, i, :], list_column, g_sel[1][:, i:i + 1], choice_value[:, i:i + 1], ALU.is_equal, ALU.mult)\
                    .then_inc(hot_ready, 1)
            dve.wait_ge(list_done, 1)
            link(ts(g_lf[:, :], PS[:, 4, 0:NE * NT], float(2 * S), None, ALU.add))
            link(dve.tensor_copy(LST[:, :], g_lf[:, :]))
            link(ts(LSM[:, :], LST[:, :], 2 * S - 1, None, ALU.min))
            ts(LSG[:, :], LSM[:, :], 1, None, ALU.arith_shift_right).then_inc(lsg_ready, 1)

            lo_gu(S_MOE, 0)
            unit_x_low(U_MOE, 0)

            def expert(e, turn, kind):
                u = e + (U_MOE + NE * turn)
                unit(u, e * MOE_STEPS + (S_MOE + turn * NE * MOE_STEPS), 0, MOE_STEPS, kind, True,
                     lambda: unit_x_low(u + 1, 0))
                rows_out(dve, dve.tensor_copy, e, turn, kind, 1)

            with dve.Fori(0, NE) as e:
                n = dve.value_load(CNT[0:1, bass.ds(e, 1)], min_val=0, max_val=CAP)
                by_count(dve, n, lambda kind: expert(e, 0, kind))
            most = dve.value_load(CNT[0:1, NE:NE + 1], min_val=0, max_val=CAP)
            with dve.If(most > 2 * P):
                with dve.Fori(0, NE) as e:
                    expert(e, 1, TWO)

            def final_rows(t):
                rstd(4, t)
                if t == 0:
                    dve.wait_ge(ld_gain, 48)
                stt(y_rows[t][:, 0, :], H[:, t, :], RS[:, t:t + 1], GB[0][:, :], ALU.mult, ALU.mult)\
                    .then_inc(fo_ready, 1)

            for t in range(NT):
                dve.wait_ge(y_ld[t], 16)
                for c in range(2):
                    ins = stt(H[:, t, :], y_rows[t][:, c, :], G12[:, c * NT + t:c * NT + t + 1], H[:, t, :],
                              ALU.mult, ALU.add)
                    if c == 0:
                        link(ins)
                ins.then_inc(y_used, 1)
                if t:
                    final_rows(t - 1)
            final_rows(NT - 1)

        @block.gpsimd
        def _(pool):
            def with_swapped(dst, src, s):
                h_ = ROPE // 2
                pool.tensor_copy(dst[..., 0:ROPE], src).then_inc(s, 1)
                pool.tensor_copy(dst[..., ROPE:ROPE + h_], src[..., h_:ROPE]).then_inc(s, 1)
                pool.tensor_copy(dst[..., ROPE + h_:P], src[..., 0:h_]).then_inc(s, 1)

            for loaded in ld_wd:
                pool.wait_ge(loaded, 16)
            with_swapped(m_wkr[:, :, :], m_wd[:, :, QR + KVR:DOWN], wkr_ready)
            pool.wait_ge(ld_uq, 16)
            for c in range(2):
                with_swapped(m_wqr[:, c, :, :], m_uq[:, c, :, NOPE:QK], wqr_ready)

            def pool_low(dst, src, hi, s, n):
                pool.tensor_tensor(dst, src, hi.bitcast(F32), ALU.subtract).then_inc(s, 1)
                pool.wait_ge(s, n)

            for i in range(16):
                t, half, c = i % NT, (i // NT) % 2, i // NT // 2
                pool.wait_ge(so_ev, i + 1)
                at_i = (slice(half * HD, half * HD + HD), c, slice(0, GRP), slice(t * P, (t + 1) * P))
                pool_low(s_ol[at_i], s_or[at_i], s_o[at_i], so_lo, i + 1)
                if WO_FROM <= i < WO_FROM + 2 * GRP:
                    j = i - WO_FROM
                    c, k = j // GRP, j % GRP
                    pool.wait_ge(swo_hi, j + 1)
                    pool_low(s_wol[c][:, k, :], s_wo[c][:, k, :], s_woh[c][:, k, :], swo_lo, j + 1)

            offset = lambda ap: bass.IndirectOffsetOnAxis(ap=ap, axis=0)
            pool.wait_ge(lsg_ready, 1)
            for i in range(2):
                pool.wait_ge(hn_st[i], 16 * NT // 2)

            def gather(k, t):
                e, turn = k % NE, min(k // NE, 1)
                pool.wait_ge(xu_tr[t], 2 * (U_MOE + k))
                if k:
                    pool.wait_ge(xg_ready[t], 16 * k)
                j = NT * e + 2 * turn + t
                pool.indirect_dma_start(out=XG[t][:, :], out_offset=None, in_=hn_d,
                                        in_offset=offset(LSG[:, j:j + 1])).then_inc(xg_ready[t], 16)

            def scatter(k):
                e, turn = k % NE, k // NE
                pool.wait_ge(yo_ready, 2 * k + 4)
                for t in range(2):
                    j = NT * e + 2 * turn + t
                    pool.indirect_dma_start(out=y_d, out_offset=offset(LST[:, j:j + 1]), in_=GB[1 - t][:, :],
                                            in_offset=None, bounds_check=2 * S - 1, oob_is_err=False)\
                        .then_inc(y_st[t], 16)
                for t in range(2):
                    pool.wait_ge(y_st[t], 16 * (k + 1))
                pool.sem_inc(y_free, 1)

            def experts(turn):
                if turn == 0:
                    gather(0, 0)
                gather(NE * turn, 1)
                for k in range(NE * turn, NE * turn + NE):
                    gather(k + 1, 0)
                    if (k + 1) % NE:
                        gather(k + 1, 1)
                    scatter(k)

            pool.sem_inc(y_free, 1)
            experts(0)
            most = pool.value_load(CNT[0:1, NE:NE + 1], min_val=0, max_val=CAP)
            with pool.If(most > 2 * P):
                experts(1)
            pool.sem_inc(y_all, 1)


def constants():
    inv = (1.0 / (np.float32(10000.0) ** (np.arange(0, ROPE, 2, dtype=np.float32) / np.float32(ROPE)))).astype(np.float32)
    ang = (np.arange(S, dtype=np.float32)[:, None] * inv[None, :]).astype(np.float32)
    cos, sin = np.cos(ang).T, np.sin(ang).T
    j = np.arange(SPAN) - WIN
    dist = np.abs(np.arange(P)[:, None] - j[None, :]).astype(np.float32)
    e = np.arange(NE, dtype=np.float32)
    route = np.stack([NE - e, NT * e])[None, :, None, :]
    choice = (np.arange(P)[:, None, None] + P * np.arange(NT)) * 2 + np.arange(2)[:, None] - 2 * S
    numbers = np.broadcast_to(np.concatenate([np.arange(P), np.arange(NE * NT)]), (P, P + NE * NT))
    return {
        "slot_consts": np.concatenate([numbers, choice.reshape(P, 2 * NT)], 1).astype(np.float32),
        "identity": np.eye(P, dtype=np.float32),
        "earlier": np.triu(np.ones((P, P), np.float32), 1),
        "ones": np.ones((P, P), np.float32),
        "rope_table": np.concatenate([cos, cos, -sin, sin]).astype(np.float32),
        "distance": np.where(dist <= WIN, dist, np.float32(1e30)).astype(np.float32),
        "route_consts": np.broadcast_to(route, (P, 2, NT, NE)).astype(np.float32).copy(),
    }


def laid_out(inputs):
    rest = ["x", "mla_norm", "mla_w_dqkv", "mla_q_norm", "mla_w_uq", "mla_kv_norm", "mla_w_uk", "mla_w_uv", "mla_w_o",
            "swa_norm", "swa_sink", "ffn_norm", "moe_norm", "moe_router", "final_norm"]
    got = {n: np.asarray(inputs[n]) for n in rest}

    def gate_up(gate, up, blocks):
        both = np.stack([np.asarray(gate), np.asarray(up)], -2)
        n = both.shape[0]
        x = both.reshape(n, 2, KD // 2, P, 2, blocks, FB)
        return x.transpose(0, 5, 1, 3, 2, 4, 6).reshape(n, blocks, 2, P, KD // 2, 2 * FB)

    def down(w, blocks):
        w = np.asarray(w)
        return w.reshape(w.shape[0], blocks, 2, P, D).transpose(0, 1, 3, 2, 4)

    got["ffn_gu"] = gate_up(inputs["ffn_w_gate"], inputs["ffn_w_up"], FFN_STEPS)[0]
    got["ffn_down"] = down(inputs["ffn_w_down"], FFN_STEPS)[0]
    got["moe_gu"] = gate_up(inputs["moe_w_gate"][0], inputs["moe_w_up"][0], MOE_STEPS)
    got["moe_down"] = down(inputs["moe_w_down"][0], MOE_STEPS)
    w = np.asarray(inputs["swa_w_qkv"])[0]
    q = w[:, :QH * HD].reshape(D, 2, 2, GRP, HD).transpose(0, 1, 3, 2, 4).reshape(D, QH * HD)
    got["swa_w_qkv"] = np.concatenate([q, w[:, QH * HD:]], 1)
    wo = np.asarray(inputs["swa_w_o"])[0]
    got["swa_w_o"] = wo.reshape(2, 2, GRP, HD, D).transpose(0, 2, 1, 3, 4).reshape(QH * HD, D)
    return {n: np.ascontiguousarray(x) for n, x in got.items()}


def kernel(**inputs):
    import concourse.bacc as bacc
    from concourse.bass_utils import run_bass_kernel_spmd

    nc = bacc.Bacc("TRN2", target_bir_lowering=False, num_devices=1)
    arrays, args = {}, {}
    for name, x in {**laid_out(inputs), **constants()}.items():
        arrays[f"in_{name}"] = x
        args[name] = nc.dram_tensor(f"in_{name}", x.shape, mybir.dt.from_np(x.dtype), kind="ExternalInput").ap()
    out = nc.dram_tensor("out", (1, S, D), F32, kind="ExternalOutput").ap()
    build_trunk(nc, args, out)
    r = run_bass_kernel_spmd(nc, [arrays], core_ids=[0])
    return r.results[0]["out"]
```
